# Optimizing a Trainium2 kernel written in Bass

```python
import math
import jax, jax.numpy as jnp
from jax import lax
import numpy as np

D_MODEL = 1024
BATCH = 1
SEQ = 256
DEPTH = 2
DEC_BATCH = 8
DEC_SEQ = 1
PAST_LEN = 2048
PAGE_SIZE = 128

H_RET = 4
DK_RET = 128
DV_RET = 256
H_GDN = 4
DK_GDN = 128
DV_GDN = 256
CONV_W = 4
H_X = 4
HD_X = 256
N_MEM = 256
D_FF = 2816
CHUNK = 64
ROPE_BASE = 10000.0
EPS = 1e-6

RET_QK = H_RET * DK_RET
RET_V = H_RET * DV_RET
GDN_QK = H_GDN * DK_GDN
GDN_V = H_GDN * DV_GDN
CONV_DIM = 2 * GDN_QK + GDN_V
X_W = H_X * HD_X
_W_IN_SIZES = (RET_QK, RET_QK, RET_V, RET_V, CONV_DIM, GDN_V, H_GDN, H_GDN, X_W, 3 * D_MODEL)
W_IN_DIM = sum(_W_IN_SIZES)
W_IN_SPLITS = tuple(sum(_W_IN_SIZES[:i]) for i in range(1, len(_W_IN_SIZES)))

kernel_name = 'hybrid_retention_gdn_memory_decoder_step'

def rms_norm(x, gain=None):
    xf = x.astype(jnp.float32)
    y = xf * lax.rsqrt(jnp.mean(xf * xf, axis=-1, keepdims=True) + EPS)
    if gain is not None:
        y = y * gain.astype(jnp.float32)
    return y.astype(x.dtype)

def l2_normalize(x):
    return x * lax.rsqrt(jnp.sum(x * x, axis=-1, keepdims=True) + EPS)

def swiglu(x, w_in, w_out):
    gate, up = jnp.split(x @ w_in, 2, axis=-1)
    return (jax.nn.silu(gate) * up) @ w_out

def rotary(x, pos):
    half = x.shape[-1] // 2
    inv_freq = ROPE_BASE ** (-jnp.arange(half, dtype=jnp.float32) / half)
    ang = pos.astype(jnp.float32)[:, None] * inv_freq[None, :]
    cos = jnp.cos(ang)[:, None, :]
    sin = jnp.sin(ang)[:, None, :]
    x1, x2 = x[..., :half], x[..., half:]
    return jnp.concatenate([x1 * cos - x2 * sin, x1 * sin + x2 * cos], axis=-1)

def heads_first(t):
    return jnp.swapaxes(t, 1, 2)

def chunk_decay_scan(q, k, v, g, beta, s0):
    b_, h_, L, dk = q.shape
    dv = v.shape[-1]
    c = min(CHUNK, L)
    n = -(-L // c)
    pad = n * c - L
    if pad:
        q, k, v = (jnp.pad(t, ((0, 0), (0, 0), (0, pad), (0, 0))) for t in (q, k, v))
        g = jnp.pad(g, ((0, 0), (0, 0), (0, pad)))
        if beta is not None:
            beta = jnp.pad(beta, ((0, 0), (0, 0), (0, pad)))
    q, k, v = (t.reshape(b_, h_, n, c, t.shape[-1]) for t in (q, k, v))
    b = jnp.cumsum(g.reshape(b_, h_, n, c), axis=-1)
    causal = jnp.tril(jnp.ones((c, c), dtype=bool))
    decay = jnp.exp(jnp.where(causal, b[..., :, None] - b[..., None, :], -jnp.inf))
    attn = jnp.einsum('bhncd,bhnmd->bhncm', q, k) * decay
    q_dec = q * jnp.exp(b)[..., None]
    k_dec = k * jnp.exp(b[..., -1:] - b)[..., None]
    chunk_decay = jnp.exp(b[..., -1])
    if beta is None:
        xs = (q_dec, k_dec, v, attn, chunk_decay)
    else:
        beta = beta.reshape(b_, h_, n, c)[..., None]
        k_beta = k * beta
        strict = jnp.tril(jnp.ones((c, c), dtype=bool), -1)
        a = jnp.where(strict, jnp.einsum('bhncd,bhnmd->bhncm', k_beta, k) * decay, 0.0)
        rhs = jnp.concatenate([v * beta, k_beta * jnp.exp(b)[..., None]], axis=-1)
        sol = lax.linalg.triangular_solve(a, rhs, left_side=True, lower=True, unit_diagonal=True)
        xs = (q_dec, k_dec, sol[..., :dv], attn, chunk_decay, sol[..., dv:])
    xs = tuple(jnp.moveaxis(t, 2, 0) for t in xs)

    def step(s, inp):
        q_c, k_c, u_c, a_c, d_c = inp[:5]
        v_new = u_c if beta is None else u_c - jnp.einsum('bhcd,bhde->bhce', inp[5], s)
        o_c = jnp.einsum('bhcd,bhde->bhce', q_c, s) + jnp.einsum('bhcm,bhme->bhce', a_c, v_new)
        s = s * d_c[..., None, None] + jnp.einsum('bhcd,bhce->bhde', k_c, v_new)
        return s, o_c

    s_fin, o = lax.scan(step, s0.astype(jnp.float32), xs)
    o = jnp.moveaxis(o, 0, 2).reshape(b_, h_, n * c, dv)[:, :, :L]
    return o, s_fin

def retention_branch(q_raw, k_raw, v_raw, g_raw, pos, s0):
    bsz, L, _ = q_raw.shape
    f32 = jnp.float32
    q = rotary(q_raw.astype(f32).reshape(bsz, L, H_RET, DK_RET), pos)
    k = rotary(k_raw.astype(f32).reshape(bsz, L, H_RET, DK_RET), pos) * DK_RET ** -0.5
    v = v_raw.astype(f32).reshape(bsz, L, H_RET, DV_RET)
    log_gamma = jnp.log1p(-jnp.exp2(-5.0 - jnp.arange(H_RET, dtype=f32)))
    g = jnp.broadcast_to(log_gamma[None, :, None], (bsz, H_RET, L))
    o, s = chunk_decay_scan(heads_first(q), heads_first(k), heads_first(v), g, None, s0)
    o = heads_first(rms_norm(o)).reshape(bsz, L, RET_V)
    return (jax.nn.silu(g_raw.astype(f32)) * o).astype(q_raw.dtype), s

def gated_delta_branch(qkv_raw, z_raw, a_raw, b_raw, conv_buf, conv_w, a_log, dt_bias, norm_w, s0):
    bsz, L, _ = qkv_raw.shape
    f32 = jnp.float32
    full = jnp.concatenate([conv_buf.astype(qkv_raw.dtype), qkv_raw], axis=1)
    conv = sum(full[:, j:j + L] * conv_w[j] for j in range(CONV_W))
    new_buf = full[:, L:]
    qkv = jax.nn.silu(conv.astype(f32))
    q, k, v = jnp.split(qkv, [GDN_QK, 2 * GDN_QK], axis=-1)
    q = l2_normalize(q.reshape(bsz, L, H_GDN, DK_GDN)) * DK_GDN ** -0.5
    k = l2_normalize(k.reshape(bsz, L, H_GDN, DK_GDN))
    v = v.reshape(bsz, L, H_GDN, DV_GDN)
    beta = jax.nn.sigmoid(b_raw.astype(f32))
    g = -jnp.exp(a_log.astype(f32)) * jax.nn.softplus(a_raw.astype(f32) + dt_bias.astype(f32))
    o, s = chunk_decay_scan(heads_first(q), heads_first(k), heads_first(v),
                            jnp.swapaxes(g, 1, 2), jnp.swapaxes(beta, 1, 2), s0)
    o = rms_norm(heads_first(o), norm_w)
    z = z_raw.astype(f32).reshape(bsz, L, H_GDN, DV_GDN)
    o = (o * jax.nn.silu(z)).reshape(bsz, L, GDN_V)
    return o.astype(qkv_raw.dtype), s, new_buf

def memory_attention(q_raw, mem_k, mem_v):
    bsz, L, _ = q_raw.shape
    q = q_raw.reshape(bsz, L, H_X, HD_X)
    s = jnp.einsum('blhd,bmhd->bhlm', q, mem_k.astype(q.dtype)).astype(jnp.float32) * HD_X ** -0.5
    prob = jax.nn.softmax(s, axis=-1).astype(q.dtype)
    o = jnp.einsum('bhlm,bmhd->blhd', prob, mem_v.astype(q.dtype))
    return o.reshape(bsz, L, X_W)

def token_mixing(xn, pos, mem_k, mem_v, s_ret, s_gdn, conv_buf, p):
    bsz, L, _ = xn.shape
    r_q, r_k, r_v, r_g, g_qkv, g_z, g_a, g_b, m_q, gates = jnp.split(xn @ p['w_in'], W_IN_SPLITS, axis=-1)
    o_ret, s_ret = retention_branch(r_q, r_k, r_v, r_g, pos, s_ret)
    o_gdn, s_gdn, conv_buf = gated_delta_branch(g_qkv, g_z, g_a, g_b, conv_buf, p['gdn_conv_w'],
                                                p['gdn_a_log'], p['gdn_dt_bias'], p['gdn_norm'], s_gdn)
    o_mem = memory_attention(m_q, mem_k, mem_v)
    gate = jax.nn.sigmoid(gates.astype(jnp.float32)).astype(xn.dtype).reshape(bsz, L, 3, D_MODEL)
    merged = (gate[:, :, 0] * (o_ret @ p['w_branch_ret'])
              + gate[:, :, 1] * (o_gdn @ p['w_branch_gdn'])
              + gate[:, :, 2] * (o_mem @ p['w_branch_mem']))
    return merged @ p['w_out'], s_ret, s_gdn, conv_buf

def decoder_layer(x, pos, mem_k, mem_v, s_ret, s_gdn, conv_buf, p):
    h = x + 0.5 * rms_norm(swiglu(rms_norm(x, p['n_ffn1_pre']), p['ffn1_w_in'], p['ffn1_w_out']), p['n_ffn1_post'])
    m, s_ret, s_gdn, conv_buf = token_mixing(rms_norm(h, p['n_mix_pre']), pos, mem_k, mem_v,
                                             s_ret, s_gdn, conv_buf, p)
    h = h + rms_norm(m, p['n_mix_post'])
    h = h + 0.5 * rms_norm(swiglu(rms_norm(h, p['n_ffn2_pre']), p['ffn2_w_in'], p['ffn2_w_out']), p['n_ffn2_post'])
    return h, s_ret, s_gdn, conv_buf

def setup_inputs(seed: int = 0) -> dict:
    key = jax.random.key(seed)
    keys = iter(jax.random.split(key, 40))

    def nrm(shape, scale):
        return scale * jax.random.normal(next(keys), shape, jnp.float32)

    def gain(width=D_MODEL):
        return 1.0 + nrm((DEPTH, width), 0.02)

    a_log = jnp.log(jax.random.uniform(next(keys), (DEPTH, H_GDN), jnp.float32, 1.0, 16.0))
    dt = jnp.exp(jax.random.uniform(next(keys), (DEPTH, H_GDN), jnp.float32, math.log(1e-3), math.log(1e-1)))
    dt_bias = dt + jnp.log(-jnp.expm1(-dt))
    return {
        'x_prompt': nrm((BATCH, SEQ, D_MODEL), 1.0),
        'x_sample': nrm((DEC_BATCH, DEC_SEQ, D_MODEL), 1.0),
        'mem_prompt': nrm((BATCH, N_MEM, D_MODEL), 1.0),
        'state_ret': nrm((DEPTH, DEC_BATCH, H_RET, DK_RET, DV_RET), 0.5),
        'state_gdn': nrm((DEPTH, DEC_BATCH, H_GDN, DK_GDN, DV_GDN), 0.5),
        'state_conv': nrm((DEPTH, DEC_BATCH, CONV_W - 1, CONV_DIM), 1.0),
        'cache_mem_k': nrm((DEPTH, DEC_BATCH, N_MEM, H_X, HD_X), 1.0),
        'cache_mem_v': nrm((DEPTH, DEC_BATCH, N_MEM, H_X, HD_X), 1.0),
        'norm_ffn1_pre': gain(),
        'norm_ffn1_post': gain(),
        'ffn1_w_in': nrm((DEPTH, D_MODEL, 2 * D_FF), D_MODEL ** -0.5),
        'ffn1_w_out': nrm((DEPTH, D_FF, D_MODEL), D_FF ** -0.5),
        'norm_mix_pre': gain(),
        'norm_mix_post': gain(),
        'w_in': nrm((DEPTH, D_MODEL, W_IN_DIM), D_MODEL ** -0.5),
        'gdn_conv_w': nrm((DEPTH, CONV_W, CONV_DIM), 0.5),
        'gdn_a_log': a_log,
        'gdn_dt_bias': dt_bias,
        'gdn_norm': gain(DV_GDN),
        'norm_mem': gain(),
        'w_mem_k': nrm((DEPTH, D_MODEL, X_W), D_MODEL ** -0.5),
        'w_mem_v': nrm((DEPTH, D_MODEL, X_W), D_MODEL ** -0.5),
        'w_branch_ret': nrm((DEPTH, RET_V, D_MODEL), RET_V ** -0.5),
        'w_branch_gdn': nrm((DEPTH, GDN_V, D_MODEL), GDN_V ** -0.5),
        'w_branch_mem': nrm((DEPTH, X_W, D_MODEL), X_W ** -0.5),
        'w_out': nrm((DEPTH, D_MODEL, D_MODEL), D_MODEL ** -0.5),
        'norm_ffn2_pre': gain(),
        'norm_ffn2_post': gain(),
        'ffn2_w_in': nrm((DEPTH, D_MODEL, 2 * D_FF), D_MODEL ** -0.5),
        'ffn2_w_out': nrm((DEPTH, D_FF, D_MODEL), D_FF ** -0.5),
    }

def reference(x_prompt, x_sample, mem_prompt, state_ret, state_gdn, state_conv, cache_mem_k, cache_mem_v,
              norm_ffn1_pre, norm_ffn1_post, ffn1_w_in, ffn1_w_out, norm_mix_pre, norm_mix_post, w_in,
              gdn_conv_w, gdn_a_log, gdn_dt_bias, gdn_norm, norm_mem, w_mem_k, w_mem_v,
              w_branch_ret, w_branch_gdn, w_branch_mem, w_out, norm_ffn2_pre, norm_ffn2_post,
              ffn2_w_in, ffn2_w_out):
    f32 = jnp.float32
    dt = x_prompt.dtype
    bp, sp = x_prompt.shape[0], x_prompt.shape[1]
    ss = x_sample.shape[1]
    pos_prompt = jnp.arange(sp)
    pos_sample = PAST_LEN + jnp.arange(ss)
    hp, hs = x_prompt, x_sample
    ret_p, gdn_p, conv_p, mk_p, mv_p, ret_s, gdn_s, conv_s = ([] for _ in range(8))
    for l in range(DEPTH):
        p = dict(n_ffn1_pre=norm_ffn1_pre[l], n_ffn1_post=norm_ffn1_post[l],
                 ffn1_w_in=ffn1_w_in[l], ffn1_w_out=ffn1_w_out[l],
                 n_mix_pre=norm_mix_pre[l], n_mix_post=norm_mix_post[l], w_in=w_in[l],
                 gdn_conv_w=gdn_conv_w[l], gdn_a_log=gdn_a_log[l], gdn_dt_bias=gdn_dt_bias[l],
                 gdn_norm=gdn_norm[l], w_branch_ret=w_branch_ret[l], w_branch_gdn=w_branch_gdn[l],
                 w_branch_mem=w_branch_mem[l], w_out=w_out[l],
                 n_ffn2_pre=norm_ffn2_pre[l], n_ffn2_post=norm_ffn2_post[l],
                 ffn2_w_in=ffn2_w_in[l], ffn2_w_out=ffn2_w_out[l])
        mem_n = rms_norm(mem_prompt, norm_mem[l])
        mk = (mem_n @ w_mem_k[l]).reshape(bp, N_MEM, H_X, HD_X)
        mv = (mem_n @ w_mem_v[l]).reshape(bp, N_MEM, H_X, HD_X)
        hp, sr, sg, cb = decoder_layer(hp, pos_prompt, mk, mv,
                                       jnp.zeros((bp, H_RET, DK_RET, DV_RET), f32),
                                       jnp.zeros((bp, H_GDN, DK_GDN, DV_GDN), f32),
                                       jnp.zeros((bp, CONV_W - 1, CONV_DIM), dt), p)
        ret_p.append(sr)
        gdn_p.append(sg)
        conv_p.append(cb)
        mk_p.append(mk)
        mv_p.append(mv)
        hs, sr, sg, cb = decoder_layer(hs, pos_sample, cache_mem_k[l], cache_mem_v[l],
                                       state_ret[l], state_gdn[l], state_conv[l], p)
        ret_s.append(sr)
        gdn_s.append(sg)
        conv_s.append(cb)
    return (hp, hs,
            jnp.stack(ret_p).astype(dt), jnp.stack(gdn_p).astype(dt), jnp.stack(conv_p).astype(dt),
            jnp.stack(mk_p).astype(dt), jnp.stack(mv_p).astype(dt),
            jnp.stack(ret_s).astype(dt), jnp.stack(gdn_s).astype(dt), jnp.stack(conv_s).astype(dt))


_drawn_inputs = setup_inputs


def setup_inputs(seed=0):
    import zlib

    import numpy as np

    out = dict(_drawn_inputs(seed))
    spreads = {}
    factors = {'norm_ffn1_post': 2.808,
     'gdn_norm': 14.214,
     'norm_mem': 8.496,
     'norm_ffn2_pre': 3.942,
     'norm_ffn2_post': 5.615,
     'norm_mix_post': 2.921,
     'cache_mem_k': 4.51,
     'cache_mem_v': 3.493}
    for name, (base, spread) in spreads.items():
        noise = np.random.default_rng([zlib.crc32(name.encode()), seed]).standard_normal(out[name].shape)
        drawn = base * np.exp(spread * noise) if base else spread * noise
        out[name] = __import__('jax').numpy.asarray(drawn.astype(out[name].dtype))
    for name, factor in factors.items():
        out[name] = (out[name] * factor).astype(out[name].dtype)
    return out
```

```python
from contextlib import ExitStack

import numpy as np

import concourse.bass as bass
from concourse import mybir

F32 = mybir.dt.float32
F32R = mybir.dt.float32r
ALU = mybir.AluOpType
ACT = mybir.ActivationFunctionType
AX = mybir.AxisListType

P = 128
L = 2
D = 1024
KT = D // P
SEQ, NS = 256, 8
T = SEQ + NS
FF = 2816
FT = FF // P
H = 4
DK, DV = 128, 256
NM = 256
CW = 4
PAST = 2048
EPS = 1e-6
GW = 2048
HKT = FT // 2

C_RQK, C_RV, C_RG, C_GQ, C_GZ, C_AB, C_MQ, C_GATE = 0, 1024, 2048, 3072, 5120, 6144, 6152, 7176

PHASES = [("mv", 4, 2), ("f1i", 22, 2), ("f1o", 16, 0), ("mk", 4, 2), ("mq", 4, 2), ("x2", 8, 2),
          ("rqk", 4, 2), ("rv", 4, 2), ("rg", 4, 2), ("x0", 8, 2), ("gq", 8, 2), ("gz", 4, 2),
          ("x1", 8, 2), ("out", 4, 2), ("f2i", 22, 2), ("f2o", 16, 0)]
GROUPS = sum(p[1] for p in PHASES)
FIRSTS = sum(p[1] for p in PHASES if p[2])


class Phase:
    def __init__(self, name, groups, tiles, c0, m0, base, last):
        self.name, self.groups, self.tiles, self.c0, self.m0, self.base = name, groups, tiles, c0, m0, base
        self.peel = last


def plan():
    found, c, m, uses = {}, 0, 0, [0] * 4
    for k, (name, groups, tiles) in enumerate(PHASES):
        after = PHASES[k + 1][2] if k + 1 < len(PHASES) else None
        found[name] = Phase(name, groups, tiles, c, m, list(uses), 0 if after == tiles else 2)
        c += groups
        if tiles:
            m += groups
            for b in range(4):
                uses[b] += groups // 2 + (1 if groups % 2 and b < 2 else 0)
        else:
            for b in range(2):
                uses[b] += groups // 4
    return found, uses


PLAN, BANK_USES = plan()
STEPS = (["n1", "p1", "mkt0", "mkt1", "n2", "gab"]
         + ["ms0", "ms1", "mpt0", "mpt1", "mo0", "mo1", "mqs"] + [f"qb{b}" for b in range(NS)] + ["smt", "spt", "smo"]
         + [f"rw{j}" for j in range(4)] + ["rkn", "rvn0", "rvn1", "rvs", "rks", "rs0", "rs1", "ro0", "ro1", "rst"]
         + [x for b in range(NS) for x in (f"rS{b}", f"rq{b}")] + ["rn0", "rn1"]
         + ["gcs"] + [f"gn{j}" for j in range(4)] + ["gct0", "gct1", "gvn0", "gvn1", "gkn", "gcol", "gev"]
         + [x for s in range(2) for x in (f"gbr{s}", f"gG{s}", f"gQ{s}", f"gT{s}")]
         + [f"{x}{lv}{s}" for lv in range(6) for x in ("gy", "gt") for s in range(2)]
         + ["gv0", "gS0", "go0", "gks", "gv1", "go1", "gS1", "gkS", "gvS"]
         + [x for b in range(NS) for x in (f"gr{b}", f"gx{b}", f"gq{b}")] + ["gm0", "gm1"]
         + ["p2", "n3", "p3"])
if len(STEPS) % 2:
    STEPS.append("pad")
NSTEP = len(STEPS)

NUNIT = 6 * NS
SRING = 3
MILESTONES = ("mem_split mem_split2 x1 sq1 ssq1 rt1 xn1 sqp1 rtp1 x2 sq2 ssq2 rt2 xn2 sqp2 rtp2 x3 sq3 ssq3 rt3 xn3 sqp3 rtp3 "
              "mvn mkt_all mkn1 ab_in ab_neg ab_exp gb_done mqt mmx0 mmx1 mpe0 mpe1 mpr0 mpr1 mpT0 mpT1 mqs sall smx "
              "spe spr sptd o_mem merged rraw rot rvt rkd rvn rvsd rp0 rp1 rS_out rof rsq rlr o_ret "
              "conv_s gsq gqr gqk tail cso bcd gexp geb dm0 dm1 dme0 dme1 g_at0 g_at1 "
              "gvb gvn0d gsg gvb1 gvn1d gqd gS_out gof g2sq glr o_gdn ").split()


def build(nc, x_prompt, x_sample, mem_prompt, state_ret, state_gdn, state_conv, cache_mem_k, cache_mem_v,
          norms, w_mem_k, w_mem_v, w_in, gdn_conv_w, gdn_a_log, gdn_dt_bias, gdn_norm, branches, w_out,
          ffn_in, ffn_out, tables, outs):
    (y_prompt, y_sample, ret_p, gdn_p, conv_p, mk_p, mv_p, ret_s, gdn_s, conv_s) = outs
    (t_ident, t_swap, t_tri, t_masks, t_rot, t_dec, t_kdec) = tables
    ctx = ExitStack()
    with ctx:
        def sb(name, shape, dt=F32):
            return ctx.enter_context(nc.sbuf_tensor(name, shape, dt))

        def sem(name):
            return ctx.enter_context(nc.semaphore(name))

        x = sb("x", [P, KT, T])
        xh, xl = sb("xh", [P, KT, T], F32R), sb("xl", [P, KT, T], F32R)
        y = sb("y", [P, KT, T])
        raw = sb("raw", [P, 2, GW])
        wh, wl = sb("wh", [P, 2, GW], F32R), sb("wl", [P, 2, GW], F32R)
        mkt, mvn = sb("mkt", [P, KT, NM]), sb("mvn", [P, 2, D])
        memr = sb("memr", [P, KT, NM])
        sring = sb("sring", [P, SRING, D])
        stg = sb("stg", [P, D])
        rot_tab = sb("rot_tab", [P, 4, T])
        dec_tab = sb("dec_tab", [P, H, SEQ])
        kdec_tab = sb("kdec_tab", [P, 2 * H])
        ident, swap, tri, ones = (sb(n, [P, P]) for n in ("ident", "swap", "tri", "ones"))
        masks = sb("masks", [P, 7, P])
        sc = sb("sc", [P, 16, NS, CW])
        tail = sb("tail", [P, 16, 3 + 3 * NS])
        erow = sb("erow", [P, H, P])
        gate = sb("gate", [P, 2, T])
        sqt = sb("sqt", [P, 2, T])
        tmpf = sb("tmpf", [P, T])
        acc, rt = sb("acc", [P, T]), sb("rt", [P, T])
        full = sb("full", [P, 2, SEQ + 3])
        csum = sb("csum", [P, 16, NS])
        gains, gl = sb("gains", [P, KT, 14]), sb("gl", [P, KT, 7])
        convw, cwl = sb("convw", [P, 16, 2 * CW]), sb("cwl", [P, 16, CW])
        gng, gnl = sb("gng", [P, 2, L]), sb("gnl", [P, 2])
        alog, dtb, epst = sb("alog", [P, L, H]), sb("dtb", [P, L, H]), sb("epst", [P, 1])
        wab = sb("wab", [P, KT, 8])
        gb, abt = sb("gb", [P, 3, 8]), sb("abt", [P, 4, 3, H])
        mx, msum = sb("mx", [P, 8]), sb("msum", [P, 8])
        sall, pts = sb("sall", [P, 2, 4 * NS]), sb("pts", [P, 2, 4 * NS])
        ps = sb("ps", [32, NM])
        smx = sb("smx", [32, 2])
        bc, ex = sb("bc", [P, 16]), sb("ex", [P, 24])
        egb, egs = sb("egb", [P, H * NS]), sb("egs", [NS, H])
        srs = sb("srs", [P, 2])

        ZONE = 54528

        def at(name, offset, shape, dt=F32):
            with ExitStack() as own:
                if offset:
                    own.enter_context(nc.sbuf_tensor(name + "_below", [P, offset // 4], F32))
                return own.enter_context(nc.sbuf_tensor(name, shape, dt))

        hh = at("hh", 0, [P, FT, T], F32R)
        hl = at("hl", FT * T * 4, [P, FT, T], F32R)
        memh = at("memh", 0, [P, KT, NM], F32R)
        meml = at("meml", 8192, [P, KT, NM], F32R)
        sqw = at("sqw", 29184, [P, KT, T])
        xnat = at("xnat", 0, [P, 3, D])
        yout = at("yout", 0, [P, 3, D])
        mnat = at("mnat", 12288, [P, 2, D])
        grow = at("grow", 20480, [16, D])
        crow = at("crow", 24576, [8, 16 * P])
        nrow = at("nrow", 32768, [L, DV])
        qkvt = at("qkvt", 0, [P, 16, T])
        mqt = at("mqt", 0, [P, KT, T])
        pt = at("pt", 8448, [P, H, 2, SEQ])
        prob = at("prob", 16896, [P, 8, NM])
        mkn = at("mkn", 16896, [P, 2, D])
        qs = at("qs", 46080, [NS, D])
        junk = at("junk", 50176, [P, 256])
        pr = at("pr", 0, [P, H, 384])
        rsq = at("rsq", 0, [P, KT, T])
        rot = at("rot", 8448, [P, KT, T])
        vn = at("vn", 16896, [P, 2, D])
        kn = at("kn", 25088, [P, 8, P])
        r4 = at("r4", 16896, [P, H, T])
        oh = at("oh", 29184, [P, KT, T], F32R)
        ol = at("ol", 37632, [P, KT, T], F32R)
        rvt = at("rvt", 46080, [P, KT, T])
        vs = at("vs", 29184, [NS, D])
        ks = at("ks", 33280, [NS, 512])
        kdb = at("kdb", 35328, [NS, 2, 512])
        vns = at("vns", 39424, [NS, D])
        scr = at("scr", 16896, [3 * NS, 16 * P])
        cso = at("cso", 16896, [3 + 3 * NS, 16 * P])
        MS = 2048
        a_t = [at(f"a_t{s}", 29184 + s * MS, [P, 4, P]) for s in range(2)]
        t_m = [at(f"t_m{s}", 29184 + (2 + s) * MS, [P, 4, P]) for s in range(2)]
        c_t = [at(f"c_t{s}", 29184 + (4 + s) * MS, [P, 4, P]) for s in range(2)]
        y_m = [at(f"y_m{s}", 29184 + (6 + s) * MS, [P, 4, P]) for s in range(2)]
        t_t = [at(f"t_t{s}", 29184 + (8 + s) * MS, [P, 4, P]) for s in range(2)]
        a_q = [at(f"a_q{s}", 29184 + (10 + s) * MS, [P, 4, P]) for s in range(2)]
        vb = at("vb", 29184, [P, D])
        vnew = at("vnew", 29184 + 2 * MS, [P, D])
        kd = at("kd", 29184 + 4 * MS, [P, 2, H, P])
        sb("zone", [P, ZONE // 4])

        proj = [ctx.enter_context(nc.psum_tensor(f"proj{b}", [P, 512], F32)) for b in range(4)]
        aux = [ctx.enter_context(nc.psum_tensor(f"aux{b}", [P, 2, 512], F32)) for b in range(2)]

        raw_loaded = [sem(f"raw_loaded{s}") for s in range(2)]
        up_loaded = [sem(f"up_loaded{s}") for s in range(2)]
        hi_done = [sem(f"hi_done{s}") for s in range(2)]
        split_done = [sem(f"split_done{s}") for s in range(2)]
        group_done = [sem(f"group_done{s}") for s in range(2)]
        first_done = sem("first_done")
        bank_free = [sem(f"bank_free{b}") for b in range(4)]
        gate_ready, gate_used = sem("gate_ready"), [sem(f"gate_used{s}") for s in range(2)]
        sq_ready, sq_used = sem("sq_ready"), [sem(f"sq_used{s}") for s in range(2)]
        conv_ready, conv_used = sem("conv_ready"), [sem(f"conv_used{s}") for s in range(2)]
        aux_full = [sem(f"aux_full{b}") for b in range(2)]
        aux_free = [sem(f"aux_free{b}") for b in range(2)]
        unit_loaded = [sem(f"unit_loaded{s}") for s in range(SRING)]
        unit_used = [sem(f"unit_used{s}") for s in range(SRING)]
        state_new = sem("state_new")
        state_kd = sem("state_kd")
        state_stored, out_stored = sem("state_stored"), sem("out_stored")
        mk_stored, mv_stored, ret_stored, conv_stored = sem("mk_stored"), sem("mv_stored"), sem("ret_stored"), sem("conv_stored")
        gdn_stored = sem("gdn_stored")
        inv_t, inv_y = sem("inv_t"), sem("inv_y")
        wab_loaded, scr_loaded = sem("wab_loaded"), sem("scr_loaded")
        const_loaded = sem("const_loaded")
        pro_mem, pro_pe, pro_dve, pro_act = sem("pro_mem"), sem("pro_pe"), sem("pro_dve"), sem("pro_act")
        hidden = sem("hidden")
        order_act, order_dve, waits_passed = sem("order_act"), sem("order_dve"), sem("waits_passed")
        M = {n: sem(n) for n in MILESTONES}
        block = ctx.enter_context(nc.Block())
        NBANK = BANK_USES
        HALF = GROUPS // 2

        class Order:

            def __init__(self, e, own):
                self.e, self.own, self.n = e, own, 0

            def fresh(self):
                self.e.sem_clear(self.own)
                self.n = 0

            def __call__(self, ins):
                self.n += 1
                ins.then_inc(self.own, 1)
                self.e.wait_ge(self.own, self.n)

        def each_group(e, l, name, body):
            ph = PLAN[name]
            whole = (ph.groups - ph.peel) // 4
            if whole > 1:
                with e.Fori(0, whole) as i:
                    for u in range(4):
                        body(ph, i, u)
            else:
                whole = 0
            for g in range(4 * whole, ph.groups):
                body(ph, g // 4, g % 4)

        def passed(e):
            e.sem_inc(waits_passed, 1)

        def start_at_one(e, sems):
            for s in sems:
                e.sem_inc(s, 1)

        def use(l, ph, i, u):
            return l * HALF + ph.c0 // 2 + 2 * i + u // 2

        def bank_use(l, ph, i, u, b):
            k = 2 * i + u // 2 if ph.tiles else i
            return l * NBANK[b] + ph.base[b] + k

        def step_of(name):
            s = STEPS.index(name)
            return s % 2, s // 2

        def take(e, l, name):
            b, k = step_of(name)
            e.wait_ge(aux_full[b], l * (NSTEP // 2) + k + 1)
            return aux[b]

        def release(e, name):
            e.sem_inc(aux_free[step_of(name)[0]], 1)

        def unit_wait(e, l, n):
            e.wait_ge(unit_loaded[n % SRING], 16 * (l * (NUNIT // SRING) + n // SRING + 1))
            return n % SRING

        @block.sync
        def _(sp):
            start_at_one(sp, split_done)
            for dst, src in [
                    (xnat[:, 0:2, :], x_prompt[0].rearrange("(t p) d -> p t d", p=P)),
                    (xnat[0:NS, 2, :], x_sample.rearrange("b s d -> (b s) d")),
                    (mnat[:], mem_prompt[0].rearrange("(t p) d -> p t d", p=P)),
                    (crow[:], gdn_conv_w.rearrange("l j c -> (l j) c")), (nrow[:], gdn_norm),
                    (ident[:], t_ident), (swap[:], t_swap), (tri[:], t_tri), (masks[:], t_masks),
                    (rot_tab[:], t_rot), (dec_tab[:], t_dec), (kdec_tab[:], t_kdec),
                    (alog[:], gdn_a_log.rearrange("l h -> (l h)").partition_broadcast(P).rearrange("p (l h) -> p l h", l=L)),
                    (dtb[:], gdn_dt_bias.rearrange("l h -> (l h)").partition_broadcast(P).rearrange("p (l h) -> p l h", l=L)),
            ] + [(grow[2 * k:2 * k + 2, :], n) for k, n in enumerate(norms)]:
                sp.dma_start(dst, src).then_inc(const_loaded, 16)

            def weight(l, name, i, u):
                def cols(w, off, width=256):
                    return w[l].rearrange("(k p) n -> p k n", p=P)[:, :, bass.ds(off, width)]
                g = 4 * i + u
                if name == "mv":
                    return [cols(w_mem_v, g * 256)]
                if name == "mk":
                    return [cols(w_mem_k, g * 256)]
                if name in ("f1i", "f2i"):
                    w = ffn_in[int(name[1]) - 1]
                    return [cols(w, g * P, P), cols(w, g * P + FF, P)]
                if name in ("f1o", "f2o"):
                    w = ffn_out[int(name[1]) - 1]
                    half = u % 2
                    return [w[l, half * HKT * P:(half + 1) * HKT * P].rearrange("(k p) n -> p k n", p=P)[
                        :, :, bass.ds((2 * i + u // 2) * P, P)]]
                if name in ("x0", "x1", "x2"):
                    b, off = int(name[1]), (2 * i + u // 2) * 256
                    return [cols(branches[b], off) if u % 2 else cols(w_in, off + C_GATE + b * D)]
                if name == "out":
                    return [cols(w_out, g * 256)]
                start = {"mq": C_MQ, "rqk": C_RQK, "rv": C_RV, "rg": C_RG, "gq": C_GQ, "gz": C_GZ}[name]
                return [cols(w_in, g * 256 + start)]

            with sp.Fori(0, L) as l:
                for name, _, _ in PHASES:
                    def load(ph, i, u, name=name):
                        s = u % 2
                        parts = weight(l, name, i, u)
                        sp.wait_ge(split_done[s], use(l, ph, i, u) + 1)
                        passed(sp)
                        k, n = parts[0].shape[1], parts[0].shape[2]
                        if len(parts) == 2:
                            dst = raw[:, s, :].rearrange("p (k two n) -> p k two n", k=k, two=2)
                            sp.dma_start(dst[:, :, 0, :], parts[0]).then_inc(raw_loaded[s], 16)
                            sp.dma_start(dst[:, :, 1, :], parts[1]).then_inc(up_loaded[s], 16)
                        else:
                            dst = raw[:, s, 0:k * n].rearrange("p (k n) -> p k n", k=k)
                            sp.dma_start(dst, parts[0]).then_inc(raw_loaded[s], 16)
                    each_group(sp, l, name, load)

            for t in range(2):
                sp.wait_ge(pro_dve, 20 + t)
                sp.dma_start(y_prompt[0, t * P:(t + 1) * P], yout[:, t, :]).then_inc(out_stored, 16)
            sp.wait_ge(pro_dve, 22)
            sp.dma_start(y_sample.rearrange("b s d -> (b s) d"), yout[0:NS, 2, :]).then_inc(out_stored, 16)
            sp.wait_ge(out_stored, 16 * 3)

        @block.gpsimd
        def _(pool):
            start_at_one(pool, unit_used)
            def unit(l, n):
                s, k = n % SRING, n // SRING
                pool.wait_ge(unit_used[s], l * (NUNIT // SRING) + k + 1)
                if n - SRING >= 4 * NS:
                    pool.wait_ge(state_stored, (l * 2 * NS + (n - SRING - 4 * NS + 1)) * 16)
                if n < 4 * NS:
                    cache = cache_mem_k if n < 2 * NS else cache_mem_v
                    b, half = n % (2 * NS) // 2, n % 2
                    src = cache[l, b, half * P:(half + 1) * P].rearrange("m h d -> m (h d)")
                    dst = sring[:, s, :]
                else:
                    st = state_ret if n < 5 * NS else state_gdn
                    src = st[l, n % NS].rearrange("h k v -> k h v")
                    dst = sring[:, s, :].rearrange("p (h v) -> p h v", h=H)
                passed(pool)
                pool.dma_start(dst, src).then_inc(unit_loaded[s], 16)

            def store_state(l, n, to):
                pool.wait_ge(state_new, l * 2 * NS + (n - 4 * NS + 1))
                passed(pool)
                pool.dma_start(to[l, n % NS].rearrange("h k v -> k h v"),
                               sring[:, n % SRING, :].rearrange("p (h v) -> p h v", h=H)).then_inc(state_stored, 16)

            with pool.Fori(0, L) as l:
                passed(pool)
                pool.dma_start(wab[:], w_in[l].rearrange("(k p) n -> p k n", p=P)[:, :, C_AB:C_AB + 8]).then_inc(wab_loaded, 16)
                for n in range(SRING):
                    unit(l, n)
                pool.wait_ge(M["mvn"], l + 1)
                passed(pool)
                pool.dma_start(mv_p[l, 0].rearrange("(t p) h d -> p t (h d)", p=P), mvn[:]).then_inc(mv_stored, 16)
                pool.wait_ge(M["mkn1"], l + 1)
                passed(pool)
                pool.dma_start(mk_p[l, 0].rearrange("(t p) h d -> p t (h d)", p=P), mkn[:]).then_inc(mk_stored, 16)
                for n in range(SRING, 4 * NS + SRING):
                    unit(l, n)
                pool.wait_ge(M["rS_out"], l + 1)
                passed(pool)
                pool.dma_start(ret_p[l, 0].rearrange("h k v -> k h v"), stg[:].rearrange("p (h v) -> p h v", h=H)).then_inc(ret_stored, 16)
                for b in range(NS):
                    store_state(l, 4 * NS + b, ret_s)
                    unit(l, 4 * NS + b + SRING)
                pool.wait_ge(M["o_ret"], l + 1)
                passed(pool)
                pool.dma_start(scr[:], state_conv[l].rearrange("b j c -> (b j) c")).then_inc(scr_loaded, 16)
                pool.wait_ge(M["cso"], l + 1)
                passed(pool)
                pool.dma_start(conv_p[l, 0], cso[0:3, :]).then_inc(conv_stored, 16)
                passed(pool)
                pool.dma_start(conv_s[l].rearrange("b j c -> (b j) c"), cso[3:3 + 3 * NS, :]).then_inc(conv_stored, 16)
                pool.wait_ge(M["gS_out"], l + 1)
                passed(pool)
                pool.dma_start(gdn_p[l, 0].rearrange("h k v -> k h v"), stg[:].rearrange("p (h v) -> p h v", h=H)).then_inc(gdn_stored, 16)
                for b in range(NS):
                    store_state(l, 5 * NS + b, gdn_s)
                    if 5 * NS + b + SRING < NUNIT:
                        unit(l, 5 * NS + b + SRING)
                for s, n in ((mk_stored, 1), (mv_stored, 1), (ret_stored, 1), (gdn_stored, 1), (conv_stored, 2), (state_stored, 2 * NS)):
                    pool.wait_ge(s, (l + 1) * (16 * n))
                pool.wait_ge(M["ab_in"], l + 1)

        @block.tensor
        def _(pe):
            start_at_one(pe, aux_free + bank_free + group_done)
            pe.wait_ge(const_loaded, 16 * 21)
            for k in range(KT):
                if k >= 4:
                    pe.wait_ge(pro_dve, k - 3)
                for t in range(2):
                    pe.transpose(proj[k % 4][:, t * P:(t + 1) * P], xnat[:, t, k * P:(k + 1) * P], ident[:])
                pe.transpose(proj[k % 4][:, SEQ:T], xnat[0:NS, 2, k * P:(k + 1) * P], ident[0:NS, 0:NS]).then_inc(pro_pe, 1)
            pe.wait_ge(pro_mem, 1)
            for k in range(KT):
                pe.wait_ge(pro_dve, k + 5)
                for t in range(2):
                    mm = pe.transpose(proj[k % 4][:, t * P:(t + 1) * P], mnat[:, t, k * P:(k + 1) * P], ident[:])
                mm.then_inc(pro_pe, 1)
            pe.wait_ge(pro_dve, 13)
            for k in range(KT):
                mm = pe.transpose(proj[0][:, k * 16:k * 16 + 14], grow[0:14, k * P:(k + 1) * P], ident[0:14, 0:14])
            mm.then_inc(pro_pe, 1)
            pe.wait_ge(pro_dve, 14)
            for j in range(16):
                mm = pe.transpose(proj[1][:, j * 8:(j + 1) * 8], crow[:, j * P:(j + 1) * P], ident[0:8, 0:8])
            mm.then_inc(pro_pe, 1)
            pe.wait_ge(pro_dve, 15)
            for j in range(2):
                mm = pe.transpose(proj[2][:, j * 2:(j + 1) * 2], nrow[:, j * P:(j + 1) * P], ident[0:L, 0:L])
            mm.then_inc(pro_pe, 1)
            pe.wait_ge(pro_dve, 19)

            def begin(l, name):
                b, k = step_of(name)
                pe.wait_ge(aux_free[b], l * (NSTEP // 2) + k + 1)
                return aux[b]

            def end(mm, name):
                mm.then_inc(aux_full[step_of(name)[0]], 1)

            def products(l, name, high, low, kind=""):
                def group(ph, i, u):
                    s = u % 2
                    n = use(l, ph, i, u)
                    pe.wait_ge(split_done[s], n + 2)
                    if ph.tiles:
                        for t in range(2):
                            bank = 2 * s + t
                            pe.wait_ge(bank_free[bank], bank_use(l, ph, i, u, bank) + 1)
                            for k in range(KT):
                                if kind == "natural":
                                    o = proj[bank][:, 0:256]
                                    a, b_ = (m[:, k, t * P:(t + 1) * P] for m in (high, low))
                                    c, d = (m[:, s, k * 256:(k + 1) * 256] for m in (wh, wl))
                                else:
                                    hi_, lo_ = (low if isinstance(low, tuple) and u % 2 else high) if kind == "mix" else (high, low)
                                    a, b_ = (m[:, s, k * 256 + t * P:k * 256 + (t + 1) * P] for m in (wh, wl))
                                    c, d = hi_[:, k, :], lo_[:, k, :]
                                    o = proj[bank][:, 0:hi_.shape[2]]
                                pe.matmul(o, a, c, start=(k == 0), stop=False)
                                pe.matmul(o, a, d, start=False, stop=False)
                                mm = pe.matmul(o, b_, c, start=False, stop=(k == KT - 1))
                            mm.then_inc(group_done[s] if t else first_done, 1)
                    else:
                        bank = u // 2
                        o = proj[bank][:, 0:T]
                        if u % 2 == 0:
                            pe.wait_ge(bank_free[bank], bank_use(l, ph, i, u, bank) + 1)
                        for k in range(HKT):
                            kk = k + HKT * (u % 2)
                            a, b_ = (m[:, s, k * P:(k + 1) * P] for m in (wh, wl))
                            pe.matmul(o, a, high[:, kk, :], start=(kk == 0), stop=False)
                            pe.matmul(o, a, low[:, kk, :], start=False, stop=False)
                            mm = pe.matmul(o, b_, high[:, kk, :], start=False, stop=(kk == FT - 1))
                        mm.then_inc(group_done[s], 1)
                passed(pe)
                each_group(pe, l, name, group)

            def total(l, name, ready):
                pe.wait_ge(M[ready], l + 1)
                o = begin(l, name)
                end(pe.matmul(o[:, 0, 0:T], ones[:], acc[:], start=True, stop=True), name)

            def turn(l, name, tiles):
                o = begin(l, name)
                if tiles[0][1].shape[0] <= 32:
                    passed(pe)
                for col, src in tiles:
                    n = src.shape[0]
                    mm = pe.transpose(o[0:src.shape[1], col // 512, col % 512:col % 512 + n], src, ident[0:n, 0:n])
                end(mm, name)

            with pe.Fori(0, L) as l:
                def ready(name):
                    pe.wait_ge(M[name], l + 1)

                ready("mem_split")
                products(l, "mv", memh, meml, "natural")
                total(l, "n1", "ssq1")
                ready("xn1")
                products(l, "f1i", xh, xl)
                pe.wait_ge(hidden, l * 2 * FT + FT)
                products(l, "f1o", hh, hl)
                total(l, "p1", "sqp1")
                ready("mem_split2")
                products(l, "mk", memh, meml)
                ready("mkt_all")
                for t in range(2):
                    turn(l, f"mkt{t}", [(j * P, mkt[:, j, t * P:(t + 1) * P]) for j in range(KT)])
                total(l, "n2", "ssq2")
                ready("xn2")
                pe.wait_ge(wab_loaded, 16 * (l + 1))
                o = begin(l, "gab")
                for t in range(3):
                    n = P if t < 2 else NS
                    for k in range(KT):
                        mm = pe.matmul(o[0:n, 0, t * 8:t * 8 + 8], y[:, k, t * P:t * P + n], wab[:, k, :],
                                       start=(k == 0), stop=(k == KT - 1))
                end(mm, "gab")

                products(l, "mq", xh, xl)
                ready("mqt")
                for s in range(2):
                    o = begin(l, f"ms{s}")
                    for hd in range(2):
                        for t in range(2):
                            for d in range(2):
                                j = 2 * (2 * s + hd) + d
                                mm = pe.matmul(o[:, hd, t * 256:(t + 1) * 256], mqt[:, j, t * P:(t + 1) * P], mkt[:, j, :],
                                               start=(d == 0), stop=(d == 1))
                    end(mm, f"ms{s}")
                for s in range(2):
                    ready(f"mpr{s}")
                    turn(l, f"mpt{s}", [(hd * 512 + m * 256 + t * P, prob[:, 4 * s + 2 * hd + t, m * P:(m + 1) * P])
                                        for hd in range(2) for m in range(2) for t in range(2)])
                for s in range(2):
                    ready(f"mpT{s}")
                    o = begin(l, f"mo{s}")
                    for hd in range(2):
                        h = 2 * s + hd
                        for dt in range(2):
                            for m in range(2):
                                mm = pe.matmul(o[:, hd, dt * 256:(dt + 1) * 256], mvn[:, m, h * 256 + dt * P:h * 256 + (dt + 1) * P],
                                               pt[:, h, m, :], start=(m == 0), stop=(m == 1))
                    end(mm, f"mo{s}")
                turn(l, "mqs", [(j * P, mqt[:, j, SEQ:T]) for j in range(KT)])
                ready("mqs")
                for b in range(NS):
                    o = begin(l, f"qb{b}")
                    for z in range(2):
                        mm = pe.matmul(o[:, z, :], ident[0:NS, b:b + 1].broadcast_to([NS, P]), qs[:, z * 512:(z + 1) * 512],
                                       start=True, stop=True)
                    end(mm, f"qb{b}")
                ready("sall")
                turn(l, "smt", [(m * P, sall[:, m, :]) for m in range(2)])
                ready("spr")
                turn(l, "spt", [(m * 32, ps[:, m * P:(m + 1) * P]) for m in range(2)])
                ready("sptd")
                o = begin(l, "smo")
                for b in range(NS):
                    slots = [unit_wait(pe, l, 2 * NS + 2 * b + m) for m in range(2)]
                    for j in range(KT):
                        for m in range(2):
                            mm = pe.matmul(o[:, 0, j * NS + b:j * NS + b + 1], sring[:, slots[m], j * P:(j + 1) * P],
                                           pts[:, m, 4 * b + j // 2:4 * b + j // 2 + 1], start=(m == 0), stop=(m == 1))
                            if j == KT - 1 and (b, m) != (NS - 1, 1):
                                mm.then_inc(unit_used[slots[m]], 1)
                end(mm, "smo")
                ready("o_mem")
                products(l, "x2", (xh, xl), (oh, ol), "mix")

                products(l, "rqk", xh, xl)
                products(l, "rv", xh, xl)
                ready("rraw")
                for j in range(4):
                    o = begin(l, f"rw{j}")
                    for t in range(2):
                        mm = pe.matmul(o[:, t, 0:T], swap[:], rot[:, 2 * j + t, :], start=True, stop=True)
                    end(mm, f"rw{j}")
                ready("rot")
                turn(l, "rkn", [((2 * h + t) * P, rot[:, 4 + h, t * P:(t + 1) * P]) for h in range(H) for t in range(2)])
                ready("rvt")
                for t in range(2):
                    turn(l, f"rvn{t}", [(j * P, rvt[:, j, t * P:(t + 1) * P]) for j in range(KT)])
                turn(l, "rvs", [(j * P, rvt[:, j, SEQ:T]) for j in range(KT)])
                turn(l, "rks", [(h * P, rot[:, 4 + h, SEQ:T]) for h in range(H)])
                for s in range(2):
                    o = begin(l, f"rs{s}")
                    for hd in range(2):
                        h = 2 * s + hd
                        pe.matmul(o[:, hd, 0:256], rot[:, 4 + h, 0:P], rot[:, h, 0:SEQ], start=True, stop=True)
                        mm = pe.matmul(o[:, hd, 256:384], rot[:, 4 + h, P:SEQ], rot[:, h, P:SEQ], start=True, stop=True)
                    end(mm, f"rs{s}")
                ready("rvn")
                for s in range(2):
                    ready(f"rp{s}")
                    o = begin(l, f"ro{s}")
                    for hd in range(2):
                        h = 2 * s + hd
                        for dt in range(2):
                            c = h * DV + dt * P
                            pe.matmul(o[:, hd, dt * 256:(dt + 1) * 256], vn[:, 0, c:c + P], pr[:, h, 0:256], start=True, stop=False)
                            mm = pe.matmul(o[:, hd, dt * 256 + P:(dt + 1) * 256], vn[:, 1, c:c + P], pr[:, h, 256:384],
                                           start=False, stop=True)
                    end(mm, f"ro{s}")
                ready("rkd")
                o = begin(l, "rst")
                for h in range(H):
                    for t in range(2):
                        mm = pe.matmul(o[:, h // 2, (h % 2) * DV:(h % 2 + 1) * DV], kn[:, 2 * h + t, :],
                                       vn[:, t, h * DV:(h + 1) * DV], start=(t == 0), stop=(t == 1))
                end(mm, "rst")

                def outer(name, b, n, values):
                    pe.wait_ge(state_kd, l * 2 * NS + n)
                    o = begin(l, name)
                    for h in range(H):
                        mm = pe.matmul(o[:, h // 2, (h % 2) * DV:(h % 2 + 1) * DV], kdb[:, b % 2, h * P:(h + 1) * P],
                                       values[:, h * DV:(h + 1) * DV], start=True, stop=True)
                    end(mm, name)

                def read_state(name, b, n, q, slot):
                    pe.wait_ge(state_new, l * 2 * NS + n)
                    o = begin(l, name)
                    for j in range(2 * H):
                        mm = pe.matmul(o[:, 0, j:j + 1], sring[:, slot, j * P:(j + 1) * P], q[:, j // 2, SEQ + b:SEQ + b + 1],
                                       start=True, stop=True)
                    end(mm, name)

                ready("rvsd")
                for b in range(NS):
                    outer(f"rS{b}", b, b + 1, vs)
                    read_state(f"rq{b}", b, b + 1, rot, (4 * NS + b) % SRING)
                ready("rsq")
                for s in range(2):
                    o = begin(l, f"rn{s}")
                    for hd in range(2):
                        for dt in range(2):
                            mm = pe.matmul(o[:, hd, 0:T], ones[:], rsq[:, 4 * s + 2 * hd + dt, :], start=(dt == 0), stop=(dt == 1))
                    end(mm, f"rn{s}")
                products(l, "rg", xh, xl)
                ready("o_ret")
                products(l, "x0", (xh, xl), (oh, ol), "mix")

                pe.wait_ge(scr_loaded, 16 * (l + 1))
                turn(l, "gcs", [(j * 24, scr[:, j * P:(j + 1) * P]) for j in range(16)])
                products(l, "gq", xh, xl)
                ready("gsq")
                for j in range(4):
                    o = begin(l, f"gn{j}")
                    for t in range(2):
                        mm = pe.matmul(o[:, t, 0:T], ones[:], sqw[:, 2 * j + t, :], start=True, stop=True)
                    end(mm, f"gn{j}")
                ready("tail")
                for z in range(2):
                    turn(l, f"gct{z}", [(j * P, tail[:, 8 * z + j, :]) for j in range(8)])
                for t in range(2):
                    turn(l, f"gvn{t}", [(j * P, qkvt[:, 8 + j, t * P:(t + 1) * P]) for j in range(KT)])
                ready("gqk")
                turn(l, "gkn", [((2 * h + t) * P, qkvt[:, 4 + h, t * P:(t + 1) * P]) for h in range(H) for t in range(2)])
                ready("gb_done")
                o = begin(l, "gcol")
                for c in range(2):
                    pe.matmul(o[:, 0, c * 4:c * 4 + 4], tri[:], gb[:, c, 0:4], start=True, stop=True)
                    mm = pe.matmul(o[:, 0, 8 + c * 4:12 + c * 4], ones[:], gb[:, c, 0:4], start=True, stop=True)
                end(mm, "gcol")
                o = begin(l, "gev")
                for h in range(H):
                    mm = pe.matmul(o[:, 0, h * NS:(h + 1) * NS], gb[0:NS, 2, h:h + 1].broadcast_to([NS, P]), ident[0:NS, 0:NS],
                                   start=True, stop=True)
                end(mm, "gev")
                for s in range(2):
                    mats = [(q, 2 * s + q // 2, q % 2) for q in range(4)]
                    o = begin(l, f"gbr{s}")
                    for q, h, c in mats:
                        pe.matmul(o[:, 0, q * P:(q + 1) * P], gb[:, c, h:h + 1].broadcast_to([P, P]), tri[:], start=True, stop=True)
                    for q, h, c in mats:
                        mm = pe.matmul(o[:, 1, q * P:(q + 1) * P], gb[:, c, 4 + h:5 + h].broadcast_to([P, P]), ident[:],
                                       start=True, stop=True)
                    end(mm, f"gbr{s}")
                    for step, other in (("gG", 4), ("gQ", 0)):
                        o = begin(l, f"{step}{s}")
                        for q, h, c in mats:
                            mm = pe.matmul(o[:, 0, q * P:(q + 1) * P], qkvt[:, 4 + h, c * P:(c + 1) * P],
                                           qkvt[:, other + h, c * P:(c + 1) * P], start=True, stop=True)
                        end(mm, f"{step}{s}")
                    ready(f"g_at{s}")
                    turn(l, f"gT{s}", [(q * P, t_t[s][:, q, :]) for q in range(4)])
                for lv in range(6):
                    for s in range(2):
                        pe.wait_ge(inv_t, l * 12 + 2 * lv + s + 1)
                        o = begin(l, f"gy{lv}{s}")
                        for q in range(4):
                            mm = pe.matmul(o[:, 0, q * P:(q + 1) * P], c_t[s][:, q, :], t_m[s][:, q, :], start=True, stop=True)
                        end(mm, f"gy{lv}{s}")
                    for s in range(2):
                        pe.wait_ge(inv_y, l * 12 + 2 * lv + s + 1)
                        o = begin(l, f"gt{lv}{s}")
                        for q in range(4):
                            pe.matmul(o[:, 0, q * P:(q + 1) * P], t_t[s][:, q, :], y_m[s][:, q, :], start=True, stop=True)
                        for q in range(4):
                            mm = pe.matmul(o[:, 1, q * P:(q + 1) * P], y_m[s][:, q, :], t_t[s][:, q, :], start=True, stop=True)
                        end(mm, f"gt{lv}{s}")

                def per_head(name, lhs, rhs):
                    o = begin(l, name)
                    for h in range(H):
                        mm = pe.matmul(o[:, h // 2, (h % 2) * DV:(h % 2 + 1) * DV], lhs(h), rhs(h), start=True, stop=True)
                    end(mm, name)

                ready("gvb")
                per_head("gv0", lambda h: t_t[h // 2][:, 2 * (h % 2), :], lambda h: vb[:, h * DV:(h + 1) * DV])
                ready("gvn0d")
                per_head("gS0", lambda h: kd[:, 0, h, :], lambda h: vnew[:, h * DV:(h + 1) * DV])
                o = begin(l, "go0")
                for j in range(KT):
                    h = j // 2
                    mm = pe.matmul(o[:, j // 4, (j % 4) * P:(j % 4 + 1) * P], vnew[:, j * P:(j + 1) * P],
                                   a_q[h // 2][:, 2 * (h % 2), :], start=True, stop=True)
                end(mm, "go0")
                ready("gsg")
                per_head("gks", lambda h: qkvt[:, 4 + h, P:SEQ], lambda h: stg[:, h * DV:(h + 1) * DV])
                ready("gvb1")
                per_head("gv1", lambda h: t_t[h // 2][:, 2 * (h % 2) + 1, :], lambda h: vb[:, h * DV:(h + 1) * DV])
                ready("gvn1d")
                ready("gqd")
                o = begin(l, "go1")
                for j in range(KT):
                    h = j // 2
                    r = o[:, j // 4, (j % 4) * P:(j % 4 + 1) * P]
                    pe.matmul(r, vnew[:, j * P:(j + 1) * P], a_q[h // 2][:, 2 * (h % 2) + 1, :], start=True, stop=False)
                    mm = pe.matmul(r, stg[:, j * P:(j + 1) * P], qkvt[:, h, P:SEQ], start=False, stop=True)
                end(mm, "go1")
                per_head("gS1", lambda h: kd[:, 1, h, :], lambda h: vnew[:, h * DV:(h + 1) * DV])
                turn(l, "gkS", [(h * P, qkvt[:, 4 + h, SEQ:T]) for h in range(H)])
                turn(l, "gvS", [(j * P, qkvt[:, 8 + j, SEQ:T]) for j in range(KT)])
                for b in range(NS):
                    n = 5 * NS + b
                    slot = unit_wait(pe, l, n)
                    o = begin(l, f"gr{b}")
                    for h in range(H):
                        mm = pe.matmul(o[0:NS, h // 2, (h % 2) * DV:(h % 2 + 1) * DV], qkvt[:, 4 + h, SEQ:T],
                                       sring[:, slot, h * DV:(h + 1) * DV], start=True, stop=True)
                    end(mm, f"gr{b}")
                    outer(f"gx{b}", b, NS + b + 1, vns)
                    read_state(f"gq{b}", b, NS + b + 1, qkvt, slot)
                ready("g2sq")
                for s in range(2):
                    o = begin(l, f"gm{s}")
                    for hd in range(2):
                        for dt in range(2):
                            mm = pe.matmul(o[:, hd, 0:T], ones[:], sqw[:, 4 * s + 2 * hd + dt, :], start=(dt == 0), stop=(dt == 1))
                    end(mm, f"gm{s}")
                products(l, "gz", xh, xl)
                ready("o_gdn")
                products(l, "x1", (xh, xl), (oh, ol), "mix")

                ready("merged")
                products(l, "out", xh, xl)
                total(l, "p2", "sqp2")
                total(l, "n3", "ssq3")
                ready("xn3")
                products(l, "f2i", xh, xl)
                pe.wait_ge(hidden, l * 2 * FT + 2 * FT)
                products(l, "f2o", hh, hl)
                total(l, "p3", "sqp3")
                if "pad" in STEPS:
                    b, k = step_of("pad")
                    pe.wait_ge(aux_free[b], l * (NSTEP // 2) + k + 1)
                    pe.sem_inc(aux_full[b], 1)

            for t in range(3):
                n = P if t < 2 else NS
                pe.wait_ge(M["x1"], L + 1)
                if t == 2:
                    pe.wait_ge(pro_dve, 20)
                for k in range(KT):
                    mm = pe.transpose(aux[t % 2][0:n, k // 4, (k % 4) * P:(k % 4 + 1) * P], x[:, k, t * P:t * P + n], ident[:])
                mm.then_inc(pro_pe, 1)

        ACT_TILES = 22 * 2 + 24 + 16
        GATE0 = {"f1i": 0, "x2": 22, "rg": 30, "x0": 38, "gz": 46, "x1": 54, "f2i": 62}
        SQ0 = {"f1o": 0, "out": 8, "f2o": 16}

        def tile_wait(e, l, ph, i, u, t):
            if ph.tiles and t == 0:
                e.wait_ge(first_done, l * FIRSTS + ph.m0 + 4 * i + u + 1)
            else:
                e.wait_ge(group_done[u % 2], use(l, ph, i, u) + 2)
            return 2 * (u % 2) + t if ph.tiles else u // 2

        def two_on(name, ph, i, u):
            k = [p[0] for p in PHASES].index(name)
            n = 2 * i + u // 2 + 1
            if isinstance(i, int) and 4 * i + u >= ph.groups - 2:
                if k + 1 == len(PHASES):
                    return None, None
                k, n = k + 1, 0
            name = PHASES[k][0]
            up = {"f1i": n, "f2i": 11 + n}.get(name)
            return GW if PHASES[k][2] else HKT * P, up

        @block.scalar
        def _(act):
            order = Order(act, order_act)
            start_at_one(act, gate_used + sq_used + conv_used)
            act.wait_ge(const_loaded, 16 * 21)
            act.wait_ge(pro_act, 1)
            order.fresh()
            for t in range(2):
                order(act.activation(stg[:], mnat[:, t, :], ACT.Square, accum_out=srs[:, t:t + 1]))
            order(act.activation(srs[:], srs[:], ACT.Sqrt, bias=epst[:], scale=1.0 / D))
            act.sem_inc(pro_act, 1)

            def split(l, slot, n, size, up=None):
                act.wait_ge(raw_loaded[slot], 16 * (n + 1))
                if up is not None:
                    act.wait_ge(up_loaded[slot], 16 * (l * 22 + up + 1))
                act.wait_ge(group_done[slot], n + 1)
                act.copy(wh[:, slot, 0:size], raw[:, slot, 0:size]).then_inc(hi_done[slot], 1)

            def stream(l, name, tile=None):
                def body(ph, i, u):
                    if tile:
                        order.fresh()
                        tile(ph, i, u)
                    size, up = two_on(name, ph, i, u)
                    if size:
                        split(l, u % 2, use(l, ph, i, u) + 1, size, up)
                each_group(act, l, name, body)

            def through(l, func, every=None):
                def tile(ph, i, u):
                    if every == "gate" and u % 2:
                        return
                    for t in range(1 if every == "first" else 2):
                        if every == "first":
                            n, slot = 2 * i + u // 2, u % 2
                            a = GATE0[ph.name] + 4 * i + u
                        else:
                            g = 4 * i + u if every is None else 2 * i + u // 2
                            n, slot = g, t
                            a = GATE0[ph.name] + 2 * g + t
                        bank = tile_wait(act, l, ph, i, u, t)
                        act.wait_ge(gate_used[slot], l * (ACT_TILES // 2) + GATE0[ph.name] // 2 + n + 1)
                        order(act.activation(gate[:, slot, :], proj[bank][:, 0:T], func))
                        act.sem_inc(bank_free[bank], 1)
                        act.sem_inc(gate_ready, 1)
                return tile

            def squares(l):
                def tile(ph, i, u):
                    if not ph.tiles and u % 2 == 0:
                        return
                    for t in range(2 if ph.tiles else 1):
                        slot = t if ph.tiles else u // 2
                        n = 4 * i + u if ph.tiles else i
                        bank = tile_wait(act, l, ph, i, u, t)
                        act.wait_ge(sq_used[slot], l * 12 + SQ0[ph.name] // 2 + n + 1)
                        order(act.activation(sqt[:, slot, :], proj[bank][:, 0:T], ACT.Square))
                        act.sem_inc(sq_ready, 1)
                return tile

            with act.Fori(0, L) as l:
                def ready(name):
                    act.wait_ge(M[name], l + 1)

                def tell(name):
                    act.sem_inc(M[name], 1)

                def root(name, out):
                    o = take(act, l, name)
                    order(act.activation(rt[:], o[:, 0, 0:T], ACT.Sqrt, bias=epst[:], scale=1.0 / D))
                    release(act, name)
                    tell(out)

                def square_x(n):
                    ready(f"x{n}")
                    order(act.activation(sqw[:], x[:], ACT.Square))
                    tell(f"sq{n}")

                order.fresh()
                for s in range(2):
                    split(l, s, l * HALF, GW)
                square_x(1)
                stream(l, "mv")
                root("n1", "rt1")
                stream(l, "f1i", through(l, ACT.Silu, "first"))
                stream(l, "f1o", squares(l))
                order.fresh()
                root("p1", "rtp1")
                square_x(2)
                stream(l, "mk")
                root("n2", "rt2")
                ready("ab_neg")
                order(act.activation(abt[:, 2], abt[:, 1], ACT.Exp))
                order(act.activation(abt[:, 3, 0], alog[:, l], ACT.Exp))
                order(act.activation(abt[:, 2], abt[:, 2], ACT.Ln, bias=ones[:, 0:1]))
                order(act.activation(gb[:, :, 4:8], gb[:, :, 4:8], ACT.Sigmoid))
                tell("ab_exp")

                stream(l, "mq")
                for s in range(2):
                    ready(f"mmx{s}")
                    o = take(act, l, f"ms{s}")
                    for q in range(4):
                        order(act.activation(prob[:, 4 * s + q, :], o[:, q // 2, (q % 2) * 256:(q % 2 + 1) * 256], ACT.Exp,
                                             bias=mx[:, 4 * s + q:4 * s + q + 1], scale=DV ** -0.5,
                                             accum_out=msum[:, 4 * s + q:4 * s + q + 1]))
                    release(act, f"ms{s}")
                    tell(f"mpe{s}")
                ready("smx")
                o = take(act, l, "smt")
                order(act.activation(ps[:], o[0:32, 0, 0:NM], ACT.Exp, bias=smx[:, 0:1], scale=DV ** -0.5, accum_out=smx[:, 1:2]))
                release(act, "smt")
                tell("spe")
                stream(l, "x2", through(l, ACT.Sigmoid, "gate"))

                stream(l, "rqk")
                stream(l, "rv")
                order.fresh()

                def inverse_root(src, steps, out, name):
                    for s, st in enumerate(steps):
                        o = take(act, l, st)
                        order(act.activation(out[:, 2 * s:2 * s + 2, :], o[:, :, 0:T], ACT.Ln, bias=epst[:], scale=src))
                        release(act, st)
                    order(act.activation(out[:, 0:2 * len(steps), :], out[:, 0:2 * len(steps), :], ACT.Exp, scale=-0.5))
                    tell(name)

                ready("rof")
                order(act.activation(rsq[:], rvt[:], ACT.Square))
                tell("rsq")
                inverse_root(1.0 / DV, ["rn0", "rn1"], r4, "rlr")
                stream(l, "rg", through(l, ACT.Silu))
                stream(l, "x0", through(l, ACT.Sigmoid, "gate"))

                def conv_input(ph, i, u):
                    for t in range(2):
                        bank = tile_wait(act, l, ph, i, u, t)
                        act.wait_ge(conv_used[t], l * 8 + 4 * i + u + 1)
                        order(act.copy(full[:, t, 3:SEQ + 3], proj[bank][:, 0:SEQ]))
                        order(act.copy(sc[:, 2 * (4 * i + u) + t, :, 3], proj[bank][:, SEQ:T]))
                        act.sem_inc(bank_free[bank], 1)
                        act.sem_inc(conv_ready, 1)
                stream(l, "gq", conv_input)
                order.fresh()
                ready("conv_s")
                order(act.activation(qkvt[:], qkvt[:], ACT.Silu))
                order(act.activation(sqw[:], qkvt[:, 0:8, :], ACT.Square))
                tell("gsq")
                inverse_root(1.0, [f"gn{j}" for j in range(4)], sqw, "gqr")
                ready("bcd")
                order(act.activation(ex[:], ex[:], ACT.Exp))
                tell("gexp")
                o = take(act, l, "gev")
                order(act.activation(egb[:], o[:, 0, 0:H * NS], ACT.Exp))
                order(act.activation(egs[:], gb[0:NS, 2, 0:4], ACT.Exp))
                release(act, "gev")
                tell("geb")
                for s in range(2):
                    o = take(act, l, f"gbr{s}")
                    ready(f"dm{s}")
                    for hd in range(2):
                        q = 2 * hd + 1
                        order(act.activation(erow[:, 2 * s + hd, :], o[:, 0, q * P:(q + 1) * P], ACT.Exp))
                    order(act.activation(y_m[s][:], y_m[s][:], ACT.Exp))
                    release(act, f"gbr{s}")
                    tell(f"dme{s}")
                ready("gof")
                order(act.activation(sqw[:], qkvt[:, 8:16, :], ACT.Square))
                tell("g2sq")
                inverse_root(1.0 / DV, ["gm0", "gm1"], r4, "glr")
                stream(l, "gz", through(l, ACT.Silu))
                stream(l, "x1", through(l, ACT.Sigmoid, "gate"))
                stream(l, "out", squares(l))
                order.fresh()
                root("p2", "rtp2")
                square_x(3)
                root("n3", "rt3")
                stream(l, "f2i", through(l, ACT.Silu, "first"))
                stream(l, "f2o", squares(l))
                order.fresh()
                root("p3", "rtp3")

        @block.vector
        def _(dve):
            order = Order(dve, order_dve)
            tt, ts_, stt = dve.tensor_tensor, dve.tensor_scalar, dve.scalar_tensor_tensor
            cp = dve.tensor_copy
            order.fresh()
            order(dve.memset(epst[:], EPS))
            order(dve.memset(ones[:], 1.0))
            order(dve.memset(full[:], 0.0))
            order(dve.memset(gb[:], 0.0))
            dve.sem_inc(pro_act, 1)
            dve.wait_ge(const_loaded, 16 * 21)
            for k in range(KT):
                dve.wait_ge(pro_pe, k + 1)
                order(cp(x[:, k, :], proj[k % 4][:, 0:T]))
                dve.sem_inc(pro_dve, 1)
            dve.wait_ge(pro_act, 2)
            order(dve.reciprocal(srs[:], srs[:]))
            for t in range(2):
                order(ts_(mnat[:, t, :], mnat[:, t, :], srs[:, t:t + 1], None, ALU.mult))
            dve.sem_inc(pro_mem, 1)
            for k in range(KT):
                dve.wait_ge(pro_pe, k + 9)
                order(cp(memr[:, k, :], proj[k % 4][:, 0:NM]))
                dve.sem_inc(pro_dve, 1)
            dve.wait_ge(pro_pe, 17)
            order(cp(gains[:], proj[0][:, 0:KT * 16].rearrange("p (k n) -> p k n", n=16)[:, :, 0:14]))
            dve.sem_inc(pro_dve, 1)
            dve.wait_ge(pro_pe, 18)
            order(cp(convw[:], proj[1][:, 0:P].rearrange("p (j n) -> p j n", n=8)))
            dve.sem_inc(pro_dve, 1)
            dve.wait_ge(pro_pe, 19)
            order(cp(gng[:], proj[2][:, 0:4].rearrange("p (j n) -> p j n", n=2)))
            dve.sem_inc(pro_dve, 1)
            dve.sem_inc(M["x1"], 1)

            def split(l, slot, n, size):
                dve.wait_ge(hi_done[slot], n + 1)
                dve.tensor_sub(wl[:, slot, 0:size], raw[:, slot, 0:size], wh[:, slot, 0:size].bitcast(F32)).then_inc(split_done[slot], 1)

            def stream(l, name, tile=None):
                def body(ph, i, u):
                    if tile:
                        order.fresh()
                        tile(ph, i, u)
                    size, _ = two_on(name, ph, i, u)
                    if size:
                        split(l, u % 2, use(l, ph, i, u) + 1, size)
                each_group(dve, l, name, body)
                order.fresh()

            def parts(high, low, src):
                order(cp(high, src))
                order(tt(low, src, high.bitcast(F32), ALU.subtract))

            def hidden_tile(l, first):
                def tile(ph, i, u):
                    j = 4 * i + u
                    bank = tile_wait(dve, l, ph, i, u, 1)
                    dve.wait_ge(gate_ready, l * ACT_TILES + GATE0[ph.name] + j + 1)
                    order(tt(tmpf[:], proj[bank][:, 0:T], gate[:, u % 2, :], ALU.mult))
                    dve.sem_inc(bank_free[bank], 1)
                    dve.sem_inc(gate_used[u % 2], 1)
                    parts(hh[:, j, :], hl[:, j, :], tmpf[:])
                    dve.sem_inc(hidden, 1)
                return tile

            def result_tile(l, gain):
                def tile(ph, i, u):
                    if not ph.tiles and u % 2 == 0:
                        return
                    for t in range(2 if ph.tiles else 1):
                        j = 2 * (4 * i + u) + t if ph.tiles else 2 * i + u // 2
                        slot = t if ph.tiles else u // 2
                        bank = tile_wait(dve, l, ph, i, u, t)
                        dve.wait_ge(sq_ready, l * 24 + SQ0[ph.name] + j + 1)
                        order(ts_(y[:, j, :], proj[bank][:, 0:T], gl[:, j, gain:gain + 1], None, ALU.mult))
                        order(tt(acc[:], acc[:], sqt[:, slot, :], ALU.add))
                        dve.sem_inc(bank_free[bank], 1)
                        dve.sem_inc(sq_used[slot], 1)
                return tile

            def copy_tile(l, out):
                def tile(ph, i, u):
                    for t in range(2):
                        bank = tile_wait(dve, l, ph, i, u, t)
                        dst = out(4 * i + u, t)
                        order(cp(dst, proj[bank][:, 0:dst.shape[-1]]))
                        dve.sem_inc(bank_free[bank], 1)
                return tile

            def gated_tile(l, out, gain=None):
                def tile(ph, i, u):
                    for t in range(2):
                        j = 2 * (4 * i + u) + t
                        dve.wait_ge(gate_ready, l * ACT_TILES + GATE0[ph.name] + j + 1)
                        if gain is None:
                            order(tt(tmpf[:], gate[:, t, :], out[:, j, :], ALU.mult))
                        else:
                            order(stt(tmpf[:], gate[:, t, :], gain[:, t:t + 1], out[:, 8 + j, :], ALU.mult, ALU.mult))
                        dve.sem_inc(gate_used[t], 1)
                        parts(oh[:, j, :], ol[:, j, :], tmpf[:])
                return tile

            def merge_tile(l, first):
                def tile(ph, i, u):
                    if u % 2 == 0:
                        return
                    for t in range(2):
                        j = 2 * (2 * i + u // 2) + t
                        bank = tile_wait(dve, l, ph, i, u, t)
                        dve.wait_ge(gate_ready, l * ACT_TILES + GATE0[ph.name] + j + 1)
                        order(tt(y[:, j, :] if first else tmpf[:], proj[bank][:, 0:T], gate[:, t, :], ALU.mult))
                        dve.sem_inc(bank_free[bank], 1)
                        dve.sem_inc(gate_used[t], 1)
                        if not first:
                            order(tt(y[:, j, :], y[:, j, :], tmpf[:], ALU.add))
                return tile

            with dve.Fori(0, L) as l:
                def ready(name):
                    dve.wait_ge(M[name], l + 1)

                def tell(name):
                    dve.sem_inc(M[name], 1)

                def flat(name):
                    return take(dve, l, name)[:].rearrange("p a b -> p (a b)")

                order.fresh()
                g2 = gains[:].rearrange("p k (a l) -> p k a l", l=L)
                order(cp(gl[:], g2[:, :, :, l]))
                for a in (1, 5):
                    order(ts_(gl[:, :, a:a + 1], gl[:, :, a:a + 1], 0.5, None, ALU.mult))
                order(cp(cwl[:], convw[:].rearrange("p j (l k) -> p j l k", l=L)[:, :, l, :]))
                order(cp(gnl[:], gng[:, :, l]))

                def split_memory(name):
                    for k in range(KT):
                        order(ts_(mkt[:, k, :], memr[:, k, :], gl[:, k, 6:7], None, ALU.mult))
                    parts(memh[:], meml[:], mkt[:])
                    tell(name)

                def sum_x(n):
                    ready(f"sq{n}")
                    order(dve.tensor_reduce(acc[:], sqw[:].rearrange("p k t -> p t k"), AX.X, ALU.add))
                    tell(f"ssq{n}")

                def norm_x(n, gain):
                    ready(f"rt{n}")
                    order(dve.reciprocal(rt[:], rt[:]))
                    for k in range(KT):
                        order(stt(y[:, k, :], x[:, k, :], gl[:, k, gain:gain + 1], rt[:], ALU.mult, ALU.mult))
                    parts(xh[:], xl[:], y[:])
                    tell(f"xn{n}")

                def add_result(n, nxt):
                    ready(f"rtp{n}")
                    order(dve.reciprocal(rt[:], rt[:]))
                    order(tt(y[:], y[:], rt[:].unsqueeze(1).broadcast_to([P, KT, T]), ALU.mult))
                    order(tt(x[:], x[:], y[:], ALU.add))
                    tell(nxt)

                for s in range(2):
                    split(l, s, l * HALF, GW)
                split_memory("mem_split")
                sum_x(1)
                stream(l, "mv", copy_tile(l, lambda g, t: mvn[:, t, bass.ds(g * 256, 256)]))
                tell("mvn")
                norm_x(1, 0)
                stream(l, "f1i", hidden_tile(l, True))
                order(dve.memset(acc[:], 0.0))
                stream(l, "f1o", result_tile(l, 1))
                tell("sqp1")
                split_memory("mem_split2")
                add_result(1, "x2")
                sum_x(2)
                stream(l, "mk", copy_tile(l, lambda g, t: mkt[:, 2 * g + t, :]))
                tell("mkt_all")
                for t in range(2):
                    order(cp(mkn[:, t, :], flat(f"mkt{t}")))
                    release(dve, f"mkt{t}")
                tell("mkn1")
                norm_x(2, 2)
                o = take(dve, l, "gab")
                order(cp(gb[:, 0:2, :], o[:, 0, 0:16].rearrange("p (t n) -> p t n", t=2)))
                order(cp(gb[0:NS, 2, :], o[0:NS, 0, 16:24]))
                release(dve, "gab")
                tell("ab_in")
                order(tt(abt[:, 0], gb[:, :, 0:4], dtb[:, l, :].unsqueeze(1).broadcast_to([P, 3, H]), ALU.add))
                order(ts_(abt[:, 1], abt[:, 0], -1.0, None, ALU.mult))
                order(tt(abt[:, 1], abt[:, 0], abt[:, 1], ALU.min))
                tell("ab_neg")
                ready("ab_exp")
                order(stt(abt[:, 0], abt[:, 0], 0.0, abt[:, 2], ALU.max, ALU.add))
                order(stt(gb[:, :, 0:4], abt[:, 0], -1.0, abt[:, 3, 0:1].broadcast_to([P, 3, H]), ALU.mult, ALU.mult))
                tell("gb_done")

                stream(l, "mq", copy_tile(l, lambda g, t: mqt[:, 2 * g + t, :]))
                tell("mqt")
                dve.wait_ge(mk_stored, 16 * (l + 1))
                for s in range(2):
                    o = flat(f"ms{s}").rearrange("p (q m) -> p q m", m=NM)
                    order(dve.tensor_reduce(mx[:, 4 * s:4 * s + 4], o, AX.X, ALU.max))
                    order(ts_(mx[:, 4 * s:4 * s + 4], mx[:, 4 * s:4 * s + 4], -DV ** -0.5, None, ALU.mult))
                    tell(f"mmx{s}")
                for s in range(2):
                    ready(f"mpe{s}")
                    order(dve.reciprocal(msum[:, 4 * s:4 * s + 4], msum[:, 4 * s:4 * s + 4]))
                    order(tt(prob[:, 4 * s:4 * s + 4, :], prob[:, 4 * s:4 * s + 4, :],
                             msum[:, 4 * s:4 * s + 4].unsqueeze(2).broadcast_to([P, 4, NM]), ALU.mult))
                    tell(f"mpr{s}")
                for s in range(2):
                    order(cp(pt[:, 2 * s:2 * s + 2].rearrange("p h m t -> p (h m t)"), flat(f"mpt{s}")))
                    release(dve, f"mpt{s}")
                    tell(f"mpT{s}")
                for s in range(2):
                    o = flat(f"mo{s}").rearrange("p (j t) -> p j t", j=4)
                    parts(oh[:, 4 * s:4 * s + 4, 0:SEQ], ol[:, 4 * s:4 * s + 4, 0:SEQ], o)
                    release(dve, f"mo{s}")
                order(cp(qs[:], flat("mqs")[0:NS, :]))
                release(dve, "mqs")
                tell("mqs")
                for b in range(NS):
                    o = flat(f"qb{b}")
                    for m in range(2):
                        slot = unit_wait(dve, l, 2 * b + m)
                        for h in range(H):
                            order(dve.tensor_tensor_reduce(junk[:], sring[:, slot, h * DV:(h + 1) * DV], o[:, h * DV:(h + 1) * DV],
                                                           1.0, 0.0, ALU.mult, ALU.add, sall[:, m, 4 * b + h:4 * b + h + 1]))
                        dve.sem_inc(unit_used[slot], 1)
                    release(dve, f"qb{b}")
                tell("sall")
                o = take(dve, l, "smt")[0:32, 0, 0:NM]
                order(dve.tensor_reduce(smx[:, 0:1], o, AX.X, ALU.max))
                order(ts_(smx[:, 0:1], smx[:, 0:1], -DV ** -0.5, None, ALU.mult))
                tell("smx")
                ready("spe")
                order(dve.reciprocal(smx[:, 1:2], smx[:, 1:2]))
                order(ts_(ps[:], ps[:], smx[:, 1:2], None, ALU.mult))
                tell("spr")
                order(cp(pts[:].rearrange("p m n -> p (m n)"), flat("spt")[:, 0:64]))
                release(dve, "spt")
                tell("sptd")
                o = flat("smo")[:, 0:KT * NS].rearrange("p (j b) -> p j b", b=NS)
                parts(oh[:, :, SEQ:T], ol[:, :, SEQ:T], o)
                release(dve, "smo")
                dve.sem_inc(unit_used[(4 * NS - 1) % SRING], 1)
                tell("o_mem")
                stream(l, "x2", merge_tile(l, True))

                stream(l, "rqk", copy_tile(l, lambda g, t: rot[:, 2 * g + t, :]))
                tell("rraw")
                stream(l, "rv", copy_tile(l, lambda g, t: rvt[:, 2 * g + t, :]))
                tell("rvt")
                for j in range(4):
                    o = take(dve, l, f"rw{j}")[:, :, 0:T]
                    c = 0 if j < 2 else 2
                    r = rot[:, 2 * j:2 * j + 2, :]
                    order(tt(r, r, rot_tab[:, c:c + 1, :].broadcast_to([P, 2, T]), ALU.mult))
                    sw = rsq[:, 0:2, :]
                    order(tt(sw, o, rot_tab[:, c + 1:c + 2, :].broadcast_to([P, 2, T]), ALU.mult))
                    release(dve, f"rw{j}")
                    order(tt(r, r, sw, ALU.add))
                tell("rot")
                order(tt(kn[:], flat("rkn").rearrange("p (n d) -> p n d", d=P), kdec_tab[:].unsqueeze(2).broadcast_to([P, 8, P]), ALU.mult))
                release(dve, "rkn")
                tell("rkd")
                for t in range(2):
                    order(cp(vn[:, t, :], flat(f"rvn{t}")))
                    release(dve, f"rvn{t}")
                tell("rvn")
                order(cp(vs[:], flat("rvs")[0:NS, :]))
                release(dve, "rvs")
                order(cp(ks[:], flat("rks")[0:NS, 0:512]))
                release(dve, "rks")
                tell("rvsd")
                for s in range(2):
                    o = take(dve, l, f"rs{s}")
                    order(tt(pr[:, 2 * s:2 * s + 2, 0:256], o[:, :, 0:256], dec_tab[:, 2 * s:2 * s + 2, :], ALU.mult))
                    order(tt(pr[:, 2 * s:2 * s + 2, 256:384], o[:, :, 256:384], dec_tab[:, 2 * s:2 * s + 2, 0:P], ALU.mult))
                    release(dve, f"rs{s}")
                    tell(f"rp{s}")
                for s in range(2):
                    order(cp(rvt[:, 4 * s:4 * s + 4, 0:SEQ], flat(f"ro{s}").rearrange("p (j t) -> p j t", j=4)))
                    release(dve, f"ro{s}")
                order(cp(stg[:], flat("rst")))
                release(dve, "rst")
                tell("rS_out")

                def one_row(b):
                    order(ts_(kdb[:, b % 2, :], ks[:], ident[0:NS, b:b + 1], None, ALU.mult))
                    dve.sem_inc(state_kd, 1)

                def update(name, slot, decay):
                    o = flat(name)
                    for h in range(H):
                        r = sring[:, slot, h * DV:(h + 1) * DV]
                        order(stt(r, r, decay(h), o[:, h * DV:(h + 1) * DV], ALU.mult, ALU.add))
                    release(dve, name)
                    dve.sem_inc(state_new, 1)

                for b in range(NS):
                    one_row(b)
                    slot = unit_wait(dve, l, 4 * NS + b)
                    update(f"rS{b}", slot, lambda h: float(np.exp(np.log1p(-2.0 ** (-5 - h)))))
                    order(cp(rvt[:, :, SEQ + b], flat(f"rq{b}")[:, 0:KT]))
                    release(dve, f"rq{b}")
                    dve.sem_inc(unit_used[slot], 1)
                tell("rof")
                ready("rlr")
                v4 = "p (h d) t -> p h d t"
                order(tt(rvt[:].rearrange(v4, d=2), rvt[:].rearrange(v4, d=2), r4[:].unsqueeze(2).broadcast_to([P, H, 2, T]), ALU.mult))
                stream(l, "rg", gated_tile(l, rvt))
                tell("o_ret")
                stream(l, "x0", merge_tile(l, False))

                order(cp(sc[:, :, :, 0:3], flat("gcs")[:, 0:384].rearrange("p (j b k) -> p j b k", b=NS, k=3)))
                release(dve, "gcs")

                def conv_tile(ph, i, u):
                    for t in range(2):
                        j = 2 * (4 * i + u) + t
                        dve.wait_ge(conv_ready, l * 16 + j + 1)
                        r = qkvt[:, j, 0:SEQ]
                        order(ts_(r, full[:, t, 0:SEQ], cwl[:, j, 0:1], None, ALU.mult))
                        for k in range(1, CW):
                            order(stt(r, full[:, t, k:k + SEQ], cwl[:, j, k:k + 1], r, ALU.mult, ALU.add))
                        order(cp(tail[:, j, 0:3], full[:, t, SEQ:SEQ + 3]))
                        dve.sem_inc(conv_used[t], 1)
                stream(l, "gq", conv_tile)
                for k in range(CW):
                    w = cwl[:, :, k:k + 1].broadcast_to([P, 16, NS])
                    if k == 0:
                        order(tt(qkvt[:, :, SEQ:T], sc[:, :, :, 0], w, ALU.mult))
                    else:
                        order(tt(csum[:], sc[:, :, :, k], w, ALU.mult))
                        order(tt(qkvt[:, :, SEQ:T], qkvt[:, :, SEQ:T], csum[:], ALU.add))
                tell("conv_s")
                order(cp(tail[:, :, 3:].rearrange("p j (b k) -> p j b k", k=3), sc[:, :, :, 1:4]))
                tell("tail")
                for z in range(2):
                    order(cp(cso[:, z * 1024:(z + 1) * 1024], flat(f"gct{z}")[0:27, :]))
                    release(dve, f"gct{z}")
                tell("cso")
                ready("gqr")
                order(stt(qkvt[:, 0:4, :], qkvt[:, 0:4, :], DK ** -0.5, sqw[:, 0:4, :], ALU.mult, ALU.mult))
                order(tt(qkvt[:, 4:8, :], qkvt[:, 4:8, :], sqw[:, 4:8, :], ALU.mult))
                tell("gqk")
                dve.wait_ge(conv_stored, 32 * (l + 1))
                for t in range(2):
                    order(cp(vn[:, t, :], flat(f"gvn{t}")))
                    release(dve, f"gvn{t}")
                order(cp(kn[:].rearrange("p n d -> p (n d)"), flat("gkn")))
                release(dve, "gkn")
                order(cp(bc[:], flat("gcol")[:, 0:16]))
                release(dve, "gcol")
                order(tt(ex[:, 0:8], bc[:, 8:16], bc[:, 0:8], ALU.subtract))
                order(cp(ex[:, 8:24], bc[:]))
                tell("bcd")
                ready("gexp")
                order(ts_(ex[:, 8:16], ex[:, 8:16], -1.0, None, ALU.mult))
                ready("geb")
                order(ts_(egs[:], egs[:], -1.0, None, ALU.mult))

                def masked(s, k):
                    order(tt(c_t[s][:], a_t[s][:], masks[:, k:k + 1, :].broadcast_to([P, 4, P]), ALU.mult))

                for s in range(2):
                    o = take(dve, l, f"gbr{s}")
                    for q in range(4):
                        col = (q % 2) * 4 + 2 * s + q // 2
                        order(ts_(y_m[s][:, q, :], o[:, 0, q * P:(q + 1) * P], bc[:, col:col + 1], 0.0, ALU.subtract, ALU.min))
                    order(cp(a_t[s][:].rearrange("p q m -> p (q m)"), o[:, 1, :]))
                    tell(f"dm{s}")
                    ready(f"dme{s}")
                    order(tt(y_m[s][:], y_m[s][:], tri[:].unsqueeze(1).broadcast_to([P, 4, P]), ALU.mult))
                    o = take(dve, l, f"gG{s}")[:, 0, :].rearrange("p (q m) -> p q m", q=4)
                    order(tt(a_t[s][:], a_t[s][:], o, ALU.mult))
                    release(dve, f"gG{s}")
                    order(tt(a_t[s][:], a_t[s][:], y_m[s][:], ALU.mult))
                    o = take(dve, l, f"gQ{s}")[:, 0, :].rearrange("p (q m) -> p q m", q=4)
                    order(tt(a_q[s][:], y_m[s][:], o, ALU.mult))
                    release(dve, f"gQ{s}")
                    masked(s, 0)
                    order(stt(t_t[s][:], c_t[s][:], -1.0, ident[:].unsqueeze(1).broadcast_to([P, 4, P]), ALU.mult, ALU.add))
                    tell(f"g_at{s}")
                    order(cp(t_m[s][:].rearrange("p q m -> p (q m)"), take(dve, l, f"gT{s}")[:, 0, :]))
                    release(dve, f"gT{s}")
                    masked(s, 1)
                    dve.sem_inc(inv_t, 1)
                for lv in range(6):
                    for s in range(2):
                        order(cp(y_m[s][:].rearrange("p q m -> p (q m)"), take(dve, l, f"gy{lv}{s}")[:, 0, :]))
                        release(dve, f"gy{lv}{s}")
                        dve.sem_inc(inv_y, 1)
                    for s in range(2):
                        o = take(dve, l, f"gt{lv}{s}")
                        if lv < 5:
                            order(tt(t_m[s][:].rearrange("p q m -> p (q m)"), t_m[s][:].rearrange("p q m -> p (q m)"), o[:, 0, :], ALU.subtract))
                        order(tt(t_t[s][:].rearrange("p q m -> p (q m)"), t_t[s][:].rearrange("p q m -> p (q m)"), o[:, 1, :], ALU.subtract))
                        release(dve, f"gt{lv}{s}")
                        if lv < 5:
                            masked(s, lv + 2)
                            dve.sem_inc(inv_t, 1)
                for h in range(H):
                    order(ts_(vb[:, h * DV:(h + 1) * DV], vn[:, 0, h * DV:(h + 1) * DV], gb[:, 0, 4 + h:5 + h], None, ALU.mult))
                tell("gvb")
                for c in range(2):
                    order(tt(kd[:, c], kn[:].rearrange("p (h c) d -> p h c d", c=2)[:, :, c, :],
                             ex[:, c * 4:c * 4 + 4].unsqueeze(2).broadcast_to([P, H, P]), ALU.mult))
                order(cp(vnew[:], flat("gv0")))
                release(dve, "gv0")
                tell("gvn0d")
                dve.wait_ge(ret_stored, 16 * (l + 1))
                order(cp(stg[:], flat("gS0")))
                release(dve, "gS0")
                tell("gsg")
                order(cp(qkvt[:, 8:16, 0:P], flat("go0").rearrange("p (j t) -> p j t", j=KT)))
                release(dve, "go0")
                order(tt(qkvt[:, 0:4, P:SEQ], qkvt[:, 0:4, P:SEQ], erow[:], ALU.mult))
                tell("gqd")
                o = flat("gks")
                for h in range(H):
                    r = vb[:, h * DV:(h + 1) * DV]
                    order(stt(r, o[:, h * DV:(h + 1) * DV], ex[:, 12 + h:13 + h], vn[:, 1, h * DV:(h + 1) * DV], ALU.mult, ALU.add))
                    order(ts_(r, r, gb[:, 1, 4 + h:5 + h], None, ALU.mult))
                release(dve, "gks")
                tell("gvb1")
                order(cp(vnew[:], flat("gv1")))
                release(dve, "gv1")
                tell("gvn1d")
                order(cp(qkvt[:, 8:16, P:SEQ], flat("go1").rearrange("p (j t) -> p j t", j=KT)))
                release(dve, "go1")
                o = flat("gS1")
                for h in range(H):
                    r = stg[:, h * DV:(h + 1) * DV]
                    order(stt(r, r, ex[:, 20 + h:21 + h], o[:, h * DV:(h + 1) * DV], ALU.mult, ALU.add))
                release(dve, "gS1")
                tell("gS_out")
                o = flat("gkS")
                for h in range(H):
                    order(ts_(ks[:, h * P:(h + 1) * P], o[0:NS, h * P:(h + 1) * P], gb[0:NS, 2, 4 + h:5 + h], None, ALU.mult))
                release(dve, "gkS")
                order(cp(vs[:], flat("gvS")[0:NS, :]))
                release(dve, "gvS")
                for b in range(NS):
                    o = flat(f"gr{b}")
                    for h in range(H):
                        c = slice(h * DV, (h + 1) * DV)
                        order(stt(vns[:, c], o[0:NS, c], egs[:, h:h + 1], vs[:, c], ALU.mult, ALU.add))
                    release(dve, f"gr{b}")
                    one_row(b)
                    slot = unit_wait(dve, l, 5 * NS + b)
                    update(f"gx{b}", slot, lambda h: egb[:, h * NS + b:h * NS + b + 1])
                    order(cp(qkvt[:, 8:16, SEQ + b], flat(f"gq{b}")[:, 0:KT]))
                    release(dve, f"gq{b}")
                    dve.sem_inc(unit_used[slot], 1)
                tell("gof")
                ready("glr")
                ov = qkvt[:, 8:16, :].rearrange(v4, d=2)
                order(tt(ov, ov, r4[:].unsqueeze(2).broadcast_to([P, H, 2, T]), ALU.mult))
                stream(l, "gz", gated_tile(l, qkvt, gnl))
                tell("o_gdn")
                stream(l, "x1", merge_tile(l, False))
                parts(xh[:], xl[:], y[:])
                tell("merged")
                order(dve.memset(acc[:], 0.0))
                stream(l, "out", result_tile(l, 3))
                tell("sqp2")
                add_result(2, "x3")
                sum_x(3)
                norm_x(3, 4)
                stream(l, "f2i", hidden_tile(l, False))
                order(dve.memset(acc[:], 0.0))
                stream(l, "f2o", result_tile(l, 5))
                tell("sqp3")
                add_result(3, "x1")
                dve.wait_ge(mv_stored, 16 * (l + 1))
                dve.wait_ge(gdn_stored, 16 * (l + 1))
                passed(dve)
                if "pad" in STEPS:
                    take(dve, l, "pad")
                    release(dve, "pad")

            for t in range(3):
                n = P if t < 2 else NS
                dve.wait_ge(pro_pe, 20 + t)
                order(cp(yout[0:n, t, :], aux[t % 2][0:n].rearrange("p a b -> p (a b)")))
                dve.sem_inc(pro_dve, 1)


def launch_arrays(inputs):
    i = np.arange(P)
    ident = np.eye(P, dtype=np.float32)
    swap = ident[(i + 64) % P]
    tri = (i[:, None] <= i[None, :]).astype(np.float32)
    masks = np.zeros((P, 7, P), np.float32)
    for k in range(7):
        size = 2 << k
        same = i[:, None] // size == i[None, :] // size
        masks[:, k] = same & (i[:, None] % size < size // 2) & (i[None, :] % size >= size // 2)
    f32 = np.float32
    inv = (f32(10000.0) ** (-np.arange(64, dtype=f32) / f32(64))).astype(f32)
    pos = np.concatenate([np.arange(SEQ), np.full(NS, PAST)]).astype(f32)
    ang = (inv[:, None] * pos[None, :]).astype(f32).astype(np.float64)
    cos, sin = np.cos(ang), np.sin(ang)
    cc, ss = np.concatenate([cos, cos]), np.concatenate([-sin, sin])
    scale = DK ** -0.5
    rot = np.stack([cc, ss, cc * scale, ss * scale], 1).astype(f32)
    lg = np.log1p(-np.exp2(-5.0 - np.arange(H)))
    d = np.arange(SEQ)[None, :] - i[:, None]
    dec = np.where(d[:, None, :] >= 0, np.exp(np.maximum(d, 0)[:, None, :] * lg[None, :, None]), 0.0).astype(f32)
    tok = i[:, None, None] + P * np.arange(2)[None, None, :]
    kdec = np.exp((SEQ - 1 - tok) * lg[None, :, None]).reshape(P, 8).astype(f32)
    return {"t_ident": ident, "t_swap": swap, "t_tri": tri, "t_masks": masks, "t_rot": rot, "t_dec": dec, "t_kdec": kdec}


NORMS = ["norm_ffn1_pre", "norm_ffn1_post", "norm_mix_pre", "norm_mix_post", "norm_ffn2_pre", "norm_ffn2_post", "norm_mem"]
OUTS = [(1, SEQ, D), (NS, 1, D), (L, 1, H, DK, DV), (L, 1, H, DK, DV), (L, 1, 3, 16 * P),
        (L, 1, NM, H, DV), (L, 1, NM, H, DV), (L, NS, H, DK, DV), (L, NS, H, DK, DV), (L, NS, 3, 16 * P)]


def program(nc, aps):
    a = aps
    outs = [nc.dram_tensor(f"out_{k}", s, F32, kind="ExternalOutput").ap() for k, s in enumerate(OUTS)]
    build(nc, a["x_prompt"], a["x_sample"], a["mem_prompt"], a["state_ret"], a["state_gdn"], a["state_conv"],
          a["cache_mem_k"], a["cache_mem_v"], [a[n] for n in NORMS], a["w_mem_k"], a["w_mem_v"], a["w_in"],
          a["gdn_conv_w"], a["gdn_a_log"], a["gdn_dt_bias"], a["gdn_norm"],
          [a["w_branch_ret"], a["w_branch_gdn"], a["w_branch_mem"]], a["w_out"],
          [a["ffn1_w_in"], a["ffn2_w_in"]], [a["ffn1_w_out"], a["ffn2_w_out"]],
          [a[n] for n in ("t_ident", "t_swap", "t_tri", "t_masks", "t_rot", "t_dec", "t_kdec")], outs)


def kernel(**inputs):
    import concourse.bacc as bacc
    from concourse.bass_utils import run_bass_kernel_spmd

    nc = bacc.Bacc("TRN2", target_bir_lowering=False, num_devices=1)
    arrays, aps = {}, {}
    for name, a in list(inputs.items()) + list(launch_arrays(inputs).items()):
        arrays[name] = np.ascontiguousarray(a)
        aps[name] = nc.dram_tensor(name, arrays[name].shape, F32, kind="ExternalInput").ap()
    program(nc, aps)
    r = run_bass_kernel_spmd(nc, [arrays], core_ids=[0])
    return tuple(r.results[0][f"out_{k}"] for k in range(len(OUTS)))
```

```python
from contextlib import ExitStack

import numpy as np

import concourse.bass as bass
from concourse import mybir

F32 = mybir.dt.float32
F32R = mybir.dt.float32r
ALU = mybir.AluOpType
ACT = mybir.ActivationFunctionType
AX = mybir.AxisListType

P = 128
L = 2
D = 1024
KT = D // P
SEQ, NS = 256, 8
T = SEQ + NS
FF = 2816
FT = FF // P
H = 4
DK, DV = 128, 256
NM = 256
CW = 4
PAST = 2048
EPS = 1e-6
GW = 2048
HKT = FT // 2

C_RQK, C_RV, C_RG, C_GQ, C_GZ, C_AB, C_MQ, C_GATE = 0, 1024, 2048, 3072, 5120, 6144, 6152, 7176

PHASES = [("mv", 4, 2), ("f1i", 22, 2), ("f1o", 16, 0), ("mk", 4, 2), ("mq", 4, 2),
          ("rqk", 4, 2), ("rv", 4, 2), ("x2", 8, 2), ("gq", 8, 2), ("rg", 4, 2), ("x0", 8, 2), ("gz", 4, 2),
          ("x1", 8, 2), ("out", 4, 2), ("f2i", 22, 2), ("f2o", 16, 0)]
GROUPS = sum(p[1] for p in PHASES)
FIRSTS = sum(p[1] for p in PHASES if p[2])


class Phase:
    def __init__(self, name, groups, tiles, c0, m0, base, last):
        self.name, self.groups, self.tiles, self.c0, self.m0, self.base = name, groups, tiles, c0, m0, base
        self.peel = last


def plan():
    found, c, m, uses = {}, 0, 0, [0] * 4
    for k, (name, groups, tiles) in enumerate(PHASES):
        after = PHASES[k + 1][2] if k + 1 < len(PHASES) else None
        found[name] = Phase(name, groups, tiles, c, m, list(uses), 0 if after == tiles else 2)
        c += groups
        if tiles:
            m += groups
            for b in range(4):
                uses[b] += groups // 2 + (1 if groups % 2 and b < 2 else 0)
        else:
            for b in range(2):
                uses[b] += groups // 4
    return found, uses


PLAN, BANK_USES = plan()
STEPS = (["n1", "p1", "mkt0", "mkt1", "n2", "gab"]
         + ["ms0", "ms1", "mpt0", "mpt1", "mo0", "mo1", "mqs"] + [f"qb{b}" for b in range(NS)] + ["smt", "spt", "smo", "smw"]
         + [f"rw{j}" for j in range(4)] + ["rkn", "rvn0", "rvn1", "rvs", "rks", "rs0", "rs1", "ro0", "ro1", "rst"]
         + ["rqs"] + [f"rS{b}" for b in range(NS)] + ["rqt", "rn0", "rn1"]
         + ["gcs"] + [f"gn{j}" for j in range(4)] + ["gct0", "gct1", "gvn0", "gvn1", "gkn", "gcol", "gev"]
         + [x for s in range(2) for x in (f"gbr{s}", f"gG{s}", f"gQ{s}")] + ["gT0", "gT1"]
         + [f"{x}{lv}{s}" for lv in range(6) for x in ("gy", "gt") for s in range(2)]
         + ["gv0", "gS0", "go0", "gks", "gv1", "go1", "gS1", "gkS", "gvS"]
         + [x for b in range(NS) for x in (f"gr{b}", f"gx{b}")] + ["gqt", "gm0", "gm1"]
         + ["p2", "n3", "p3"])
PAIR, AUX_USES = {}, [0, 0]
pair = 1
for step in STEPS:
    pair = 0 if step == "rqs" else 1 if step.startswith("rS") else 1 - pair
    PAIR[step] = pair, AUX_USES[pair]
    AUX_USES[pair] += 1

NUNIT = 6 * NS
SRING = 3
MILESTONES = ("mem_split mem_split2 x1 sq1 ssq1 rt1 xn1 sqp1 rtp1 x2 sq2 ssq2 rt2 xn2 sqp2 rtp2 x3 sq3 ssq3 rt3 xn3 sqp3 rtp3 "
              "mvn mkt_all mkn1 ab_in ab_neg ab_exp gb_done mqt mmx0 mmx1 mpe0 mpe1 mpr0 mpr1 mpT0 mpT1 mqs sall smx "
              "spe spr sptd sov rqv gqsum gqv gsmp conv_p "
              "x_half sq_half y_half y_all xh_half xh_all memhi memhi2 o_mem merged rraw rot rvt rkd rvn rvsd rp0 rp1 rS_out rof rsq rlr o_ret "
              "conv_s gsq gqr gqk tail cso bcd gexp geb dm0 dm1 dme0 dme1 g_at0 g_at1 "
              "gvb gvn0d gsg gvb1 gvn1d gqd gS_out gof g2sq glr o_gdn ").split()


def build(nc, x_prompt, x_sample, mem_prompt, state_ret, state_gdn, state_conv, cache_mem_k, cache_mem_v,
          norms, w_mem_k, w_mem_v, w_in, gdn_conv_w, gdn_a_log, gdn_dt_bias, gdn_norm, branches, w_out,
          ffn_in, ffn_out, tables, outs):
    (y_prompt, y_sample, ret_p, gdn_p, conv_p, mk_p, mv_p, ret_s, gdn_s, conv_s) = outs
    (t_ident, t_swap, t_tri, t_masks, t_rot, t_dec, t_kdec) = tables
    ctx = ExitStack()
    with ctx:
        def sb(name, shape, dt=F32):
            return ctx.enter_context(nc.sbuf_tensor(name, shape, dt))

        def sem(name):
            return ctx.enter_context(nc.semaphore(name))

        x = sb("x", [P, KT, T])
        xh, xl = sb("xh", [P, KT, T], F32R), sb("xl", [P, KT, T], F32R)
        y = sb("y", [P, KT, T])
        raw = sb("raw", [P, 2, GW])
        wh, wl = sb("wh", [P, 2, GW], F32R), sb("wl", [P, 2, GW], F32R)
        mkt, mvn = sb("mkt", [P, KT, NM]), sb("mvn", [P, 2, D])
        memr = sb("memr", [P, KT, NM])
        sring = sb("sring", [P, SRING, D])
        stg = sb("stg", [P, D])
        rot_tab = sb("rot_tab", [P, 4, T])
        dec_tab = sb("dec_tab", [P, H, SEQ])
        kdec_tab = sb("kdec_tab", [P, 2 * H])
        ident, swap, tri, ones = (sb(n, [P, P]) for n in ("ident", "swap", "tri", "ones"))
        masks = sb("masks", [P, 7, P])
        sc = sb("sc", [P, 16, NS, CW])
        tail = sb("tail", [P, 16, 3 + 3 * NS])
        erow = sb("erow", [P, H, P])
        gate = sb("gate", [P, 2, T])
        sqt = sb("sqt", [P, 2, T])
        tmpf = sb("tmpf", [P, T])
        acc, rt = sb("acc", [P, T]), sb("rt", [P, T])
        full = sb("full", [P, 2, SEQ + 3])
        csum = sb("csum", [P, 16, NS])
        gains, gl = sb("gains", [P, KT, 14]), sb("gl", [P, KT, 7])
        convw, cwl = sb("convw", [P, 16, 2 * CW]), sb("cwl", [P, 16, CW])
        gng, gnl = sb("gng", [P, 2, L]), sb("gnl", [P, 2])
        alog, dtb, epst = sb("alog", [P, L, H]), sb("dtb", [P, L, H]), sb("epst", [P, 1])
        wab = sb("wab", [P, KT, 8])
        gb, abt = sb("gb", [P, 3, 8]), sb("abt", [P, 4, 3, H])
        mx, msum = sb("mx", [P, 8]), sb("msum", [P, 8])
        sall, pts = sb("sall", [P, 2, 4 * NS]), sb("pts", [P, KT, NS])
        ps = sb("ps", [32, NM])
        smx = sb("smx", [32, 2])
        bc, ex = sb("bc", [P, 16]), sb("ex", [P, 24])
        egb = sb("egb", [P, H * NS])
        kneg = sb("kneg", [P, H, NS])
        srs = sb("srs", [P, 2])

        ZONE = 54528

        def at(name, offset, shape, dt=F32):
            with ExitStack() as own:
                if offset:
                    own.enter_context(nc.sbuf_tensor(name + "_below", [P, offset // 4], F32))
                return own.enter_context(nc.sbuf_tensor(name, shape, dt))

        hh = at("hh", 0, [P, FT, T], F32R)
        hl = at("hl", FT * T * 4, [P, FT, T], F32R)
        memh = at("memh", 0, [P, KT, NM], F32R)
        meml = at("meml", 8192, [P, KT, NM], F32R)
        sqw = at("sqw", 29184, [P, KT, T])
        xnat = at("xnat", 0, [P, 3, D])
        yout = at("yout", 0, [P, 3, D])
        mnat = at("mnat", 12288, [P, 2, D])
        grow = at("grow", 20480, [16, D])
        crow = at("crow", 24576, [8, 16 * P])
        nrow = at("nrow", 32768, [L, DV])
        qkvt = at("qkvt", 0, [P, 16, T])
        mqt = at("mqt", 0, [P, KT, T])
        pt = at("pt", 8448, [P, H, 2, SEQ])
        prob = at("prob", 16896, [P, 8, NM])
        mkn = at("mkn", 16896, [P, 2, D])
        qs = at("qs", 16896, [NS, D])
        junk = at("junk", 20992, [P, 256])
        pmask = at("pmask", 16896, [P, 2 * NS * 4 * NS + 4 * NS])
        sov = at("sov", 20480, [4 * NS, D])
        qmask = at("qmask", 25088, [P, NS * (4 * NS + 1)])
        qout = at("qout", 43520, [NS, D])
        qout_ret = at("qout_ret", 16896, [NS, D])
        pr = at("pr", 0, [P, H, 384])
        rsq = at("rsq", 29184, [P, KT, T])
        rot = at("rot", 8448, [P, KT, T])
        vn = at("vn", 16896, [P, 2, D])
        kn = at("kn", 25088, [P, 8, P])
        sqg = at("sqg", 46080, [P, KT, T])
        oh = at("oh", 29184, [P, KT, T], F32R)
        ol = at("ol", 37632, [P, KT, T], F32R)
        rvt = at("rvt", 46080, [P, KT, T])
        mh = at("mh", 0, [P, KT, T], F32R)
        ml = at("ml", KT * T * 4, [P, KT, T], F32R)
        vs = at("vs", 29184, [NS, D])
        ks = at("ks", 33280, [NS, 512])
        kdb = at("kdb", 35328, [NS, 2, 512])
        vns = at("vns", 39424, [NS, D])
        scr = at("scr", 16896, [3 * NS, 16 * P])
        cso = at("cso", 16896, [3 + 3 * NS, 16 * P])
        MS = 2048
        a_t = [at(f"a_t{s}", 29184 + s * MS, [P, 4, P]) for s in range(2)]
        t_m = [at(f"t_m{s}", 29184 + (2 + s) * MS, [P, 4, P]) for s in range(2)]
        c_t = [at(f"c_t{s}", 29184 + (4 + s) * MS, [P, 4, P]) for s in range(2)]
        y_m = [at(f"y_m{s}", 29184 + (6 + s) * MS, [P, 4, P]) for s in range(2)]
        t_t = [at(f"t_t{s}", 29184 + (8 + s) * MS, [P, 4, P]) for s in range(2)]
        a_q = [at(f"a_q{s}", 29184 + (10 + s) * MS, [P, 4, P]) for s in range(2)]
        vb = at("vb", 29184, [P, D])
        vnew = at("vnew", 29184 + 2 * MS, [P, D])
        kd = at("kd", 29184 + 4 * MS, [P, 2, H, P])
        sb("zone", [P, ZONE // 4])

        r4 = mkt[:].rearrange("p k m -> p (k m)")[:, 0:H * T].rearrange("p (h t) -> p h t", h=H)

        proj = [ctx.enter_context(nc.psum_tensor(f"proj{b}", [P, 512], F32)) for b in range(4)]
        aux = [ctx.enter_context(nc.psum_tensor(f"aux{b}", [P, 2, 512], F32)) for b in range(2)]

        raw_loaded = [sem(f"raw_loaded{s}") for s in range(2)]
        up_loaded = [sem(f"up_loaded{s}") for s in range(2)]
        hi_done = [sem(f"hi_done{s}") for s in range(2)]
        split_done = [sem(f"split_done{s}") for s in range(2)]
        group_done = [sem(f"group_done{s}") for s in range(2)]
        first_done = sem("first_done")
        bank_free = [sem(f"bank_free{b}") for b in range(4)]
        gate_ready, gate_used = sem("gate_ready"), [sem(f"gate_used{s}") for s in range(2)]
        sq_ready, sq_used = sem("sq_ready"), [sem(f"sq_used{s}") for s in range(2)]
        conv_ready, conv_used = sem("conv_ready"), [sem(f"conv_used{s}") for s in range(2)]
        aux_full = [sem(f"aux_full{b}") for b in range(2)]
        aux_free = [sem(f"aux_free{b}") for b in range(2)]
        unit_loaded = [sem(f"unit_loaded{s}") for s in range(SRING)]
        unit_used = [sem(f"unit_used{s}") for s in range(SRING)]
        state_new = sem("state_new")
        state_kd = sem("state_kd")
        state_stored, out_stored = sem("state_stored"), sem("out_stored")
        mk_stored, mv_stored, ret_stored, conv_stored = sem("mk_stored"), sem("mv_stored"), sem("ret_stored"), sem("conv_stored")
        gdn_stored = sem("gdn_stored")
        inv_t, inv_y = sem("inv_t"), sem("inv_y")
        wab_loaded, scr_loaded = sem("wab_loaded"), sem("scr_loaded")
        const_loaded = sem("const_loaded")
        pro_mem, pro_pe, pro_dve, pro_act = sem("pro_mem"), sem("pro_pe"), sem("pro_dve"), sem("pro_act")
        hidden = sem("hidden")
        order_act, order_dve, waits_passed = sem("order_act"), sem("order_dve"), sem("waits_passed")
        M = {n: sem(n) for n in MILESTONES}
        block = ctx.enter_context(nc.Block())
        NBANK = BANK_USES
        HALF = GROUPS // 2

        class Order:

            def __init__(self, e, own):
                self.e, self.own, self.n = e, own, 0

            def fresh(self):
                self.e.sem_clear(self.own)
                self.n = 0

            def __call__(self, ins):
                self.n += 1
                ins.then_inc(self.own, 1)
                self.e.wait_ge(self.own, self.n)

        def each_group(e, l, name, body, after=None):
            ph = PLAN[name]
            if after:
                for g in range(ph.groups):
                    body(ph, g // 4, g % 4)
                    after(g)
                return
            whole = (ph.groups - ph.peel) // 4
            if whole > 1:
                with e.Fori(0, whole) as i:
                    for u in range(4):
                        body(ph, i, u)
            else:
                whole = 0
            for g in range(4 * whole, ph.groups):
                body(ph, g // 4, g % 4)

        def passed(e):
            e.sem_inc(waits_passed, 1)

        def norm_wait(e, l, name, n):
            e.wait_ge(M[name], l * 3 + n)

        def start_at_one(e, sems):
            for s in sems:
                e.sem_inc(s, 1)

        def use(l, ph, i, u):
            return l * HALF + ph.c0 // 2 + 2 * i + u // 2

        def bank_use(l, ph, i, u, b):
            k = 2 * i + u // 2 if ph.tiles else i
            return l * NBANK[b] + ph.base[b] + k

        def step_of(name):
            return PAIR[name]

        def take(e, l, name):
            b, k = step_of(name)
            e.wait_ge(aux_full[b], l * AUX_USES[b] + k + 1)
            return aux[b]

        def release(e, name):
            e.sem_inc(aux_free[step_of(name)[0]], 1)

        def unit_wait(e, l, n):
            e.wait_ge(unit_loaded[n % SRING], 16 * (l * (NUNIT // SRING) + n // SRING + 1))
            return n % SRING

        @block.sync
        def _(sp):
            start_at_one(sp, split_done)
            for dst, src in [
                    (xnat[:, 0:2, :], x_prompt[0].rearrange("(t p) d -> p t d", p=P)),
                    (xnat[0:NS, 2, :], x_sample.rearrange("b s d -> (b s) d")),
                    (mnat[:], mem_prompt[0].rearrange("(t p) d -> p t d", p=P)),
                    (crow[:], gdn_conv_w.rearrange("l j c -> (l j) c")), (nrow[:], gdn_norm),
                    (ident[:], t_ident), (swap[:], t_swap), (tri[:], t_tri), (masks[:], t_masks),
                    (rot_tab[:], t_rot), (dec_tab[:], t_dec), (kdec_tab[:], t_kdec),
                    (alog[:], gdn_a_log.rearrange("l h -> (l h)").partition_broadcast(P).rearrange("p (l h) -> p l h", l=L)),
                    (dtb[:], gdn_dt_bias.rearrange("l h -> (l h)").partition_broadcast(P).rearrange("p (l h) -> p l h", l=L)),
            ] + [(grow[2 * k:2 * k + 2, :], n) for k, n in enumerate(norms)]:
                sp.dma_start(dst, src).then_inc(const_loaded, 16)

            def weight(l, name, i, u):
                def cols(w, off, width=256):
                    return w[l].rearrange("(k p) n -> p k n", p=P)[:, :, bass.ds(off, width)]
                g = 4 * i + u
                if name == "mv":
                    return [cols(w_mem_v, g * 256)]
                if name == "mk":
                    return [cols(w_mem_k, g * 256)]
                if name in ("f1i", "f2i"):
                    w = ffn_in[int(name[1]) - 1]
                    return [cols(w, g * P, P), cols(w, g * P + FF, P)]
                if name in ("f1o", "f2o"):
                    w = ffn_out[int(name[1]) - 1]
                    half = u % 2
                    return [w[l, half * HKT * P:(half + 1) * HKT * P].rearrange("(k p) n -> p k n", p=P)[
                        :, :, bass.ds((2 * i + u // 2) * P, P)]]
                if name in ("x0", "x1", "x2"):
                    b, off = int(name[1]), (2 * i + u // 2) * 256
                    return [cols(branches[b], off) if u % 2 else cols(w_in, off + C_GATE + b * D)]
                if name == "out":
                    return [cols(w_out, g * 256)]
                start = {"mq": C_MQ, "rqk": C_RQK, "rv": C_RV, "rg": C_RG, "gq": C_GQ, "gz": C_GZ}[name]
                return [cols(w_in, g * 256 + start)]

            with sp.Fori(0, L) as l:
                for name, _, _ in PHASES:
                    def load(ph, i, u, name=name):
                        s = u % 2
                        parts = weight(l, name, i, u)
                        sp.wait_ge(split_done[s], use(l, ph, i, u) + 1)
                        passed(sp)
                        k, n = parts[0].shape[1], parts[0].shape[2]
                        if len(parts) == 2:
                            dst = raw[:, s, :].rearrange("p (k two n) -> p k two n", k=k, two=2)
                            sp.dma_start(dst[:, :, 0, :], parts[0]).then_inc(raw_loaded[s], 16)
                            sp.dma_start(dst[:, :, 1, :], parts[1]).then_inc(up_loaded[s], 16)
                        else:
                            dst = raw[:, s, 0:k * n].rearrange("p (k n) -> p k n", k=k)
                            sp.dma_start(dst, parts[0]).then_inc(raw_loaded[s], 16)
                    each_group(sp, l, name, load)

            for t in range(2):
                sp.wait_ge(pro_dve, 20 + t)
                sp.dma_start(y_prompt[0, t * P:(t + 1) * P], yout[:, t, :]).then_inc(out_stored, 16)
            sp.wait_ge(pro_dve, 22)
            sp.dma_start(y_sample.rearrange("b s d -> (b s) d"), yout[0:NS, 2, :]).then_inc(out_stored, 16)
            sp.wait_ge(out_stored, 16 * 3)

        @block.gpsimd
        def _(pool):
            start_at_one(pool, unit_used)
            def unit(l, n):
                s, k = n % SRING, n // SRING
                pool.wait_ge(unit_used[s], l * (NUNIT // SRING) + k + 1)
                if n - SRING >= 4 * NS:
                    pool.wait_ge(state_stored, (l * 2 * NS + (n - SRING - 4 * NS + 1)) * 16)
                if n < 4 * NS:
                    cache = cache_mem_k if n < 2 * NS else cache_mem_v
                    b, half = n % (2 * NS) // 2, n % 2
                    src = cache[l, b, half * P:(half + 1) * P].rearrange("m h d -> m (h d)")
                    dst = sring[:, s, :]
                else:
                    st = state_ret if n < 5 * NS else state_gdn
                    src = st[l, n % NS].rearrange("h k v -> k h v")
                    dst = sring[:, s, :].rearrange("p (h v) -> p h v", h=H)
                passed(pool)
                pool.dma_start(dst, src).then_inc(unit_loaded[s], 16)

            def store_state(l, n, to):
                pool.wait_ge(state_new, l * 2 * NS + (n - 4 * NS + 1))
                passed(pool)
                pool.dma_start(to[l, n % NS].rearrange("h k v -> k h v"),
                               sring[:, n % SRING, :].rearrange("p (h v) -> p h v", h=H)).then_inc(state_stored, 16)

            with pool.Fori(0, L) as l:
                passed(pool)
                pool.dma_start(wab[:], w_in[l].rearrange("(k p) n -> p k n", p=P)[:, :, C_AB:C_AB + 8]).then_inc(wab_loaded, 16)
                for n in range(SRING):
                    unit(l, n)
                pool.wait_ge(M["mvn"], l + 1)
                passed(pool)
                pool.dma_start(mv_p[l, 0].rearrange("(t p) h d -> p t (h d)", p=P), mvn[:]).then_inc(mv_stored, 16)
                pool.wait_ge(M["mkn1"], l + 1)
                passed(pool)
                pool.dma_start(mk_p[l, 0].rearrange("(t p) h d -> p t (h d)", p=P), mkn[:]).then_inc(mk_stored, 16)
                for n in range(SRING, 4 * NS + SRING):
                    unit(l, n)
                pool.wait_ge(M["rS_out"], l + 1)
                passed(pool)
                pool.dma_start(ret_p[l, 0].rearrange("h k v -> k h v"), stg[:].rearrange("p (h v) -> p h v", h=H)).then_inc(ret_stored, 16)
                for b in range(NS):
                    store_state(l, 4 * NS + b, ret_s)
                    unit(l, 4 * NS + b + SRING)
                pool.wait_ge(M["rof"], l + 1)
                passed(pool)
                pool.dma_start(scr[:], state_conv[l].rearrange("b j c -> (b j) c")).then_inc(scr_loaded, 16)
                pool.wait_ge(M["cso"], l + 1)
                passed(pool)
                pool.dma_start(conv_p[l, 0], cso[0:3, :]).then_inc(conv_stored, 16)
                passed(pool)
                pool.dma_start(conv_s[l].rearrange("b j c -> (b j) c"), cso[3:3 + 3 * NS, :]).then_inc(conv_stored, 16)
                pool.wait_ge(M["gS_out"], l + 1)
                passed(pool)
                pool.dma_start(gdn_p[l, 0].rearrange("h k v -> k h v"), stg[:].rearrange("p (h v) -> p h v", h=H)).then_inc(gdn_stored, 16)
                for b in range(NS):
                    store_state(l, 5 * NS + b, gdn_s)
                    if 5 * NS + b + SRING < NUNIT:
                        unit(l, 5 * NS + b + SRING)
                for s, n in ((mk_stored, 1), (mv_stored, 1), (ret_stored, 1), (gdn_stored, 1), (conv_stored, 2), (state_stored, 2 * NS)):
                    pool.wait_ge(s, (l + 1) * (16 * n))
                pool.wait_ge(M["ab_in"], l + 1)

        @block.tensor
        def _(pe):
            start_at_one(pe, aux_free + bank_free + group_done)
            pe.wait_ge(const_loaded, 16 * 21)
            for k in range(KT):
                if k >= 4:
                    pe.wait_ge(pro_dve, k - 3)
                for t in range(2):
                    pe.transpose(proj[k % 4][:, t * P:(t + 1) * P], xnat[:, t, k * P:(k + 1) * P], ident[:])
                pe.transpose(proj[k % 4][:, SEQ:T], xnat[0:NS, 2, k * P:(k + 1) * P], ident[0:NS, 0:NS]).then_inc(pro_pe, 1)
            pe.wait_ge(pro_mem, 1)
            for k in range(KT):
                pe.wait_ge(pro_dve, k + 5)
                for t in range(2):
                    mm = pe.transpose(proj[k % 4][:, t * P:(t + 1) * P], mnat[:, t, k * P:(k + 1) * P], ident[:])
                mm.then_inc(pro_pe, 1)
            pe.wait_ge(pro_dve, 13)
            for k in range(KT):
                mm = pe.transpose(proj[0][:, k * 16:k * 16 + 14], grow[0:14, k * P:(k + 1) * P], ident[0:14, 0:14])
            mm.then_inc(pro_pe, 1)
            pe.wait_ge(pro_dve, 14)
            for j in range(16):
                mm = pe.transpose(proj[1][:, j * 8:(j + 1) * 8], crow[:, j * P:(j + 1) * P], ident[0:8, 0:8])
            mm.then_inc(pro_pe, 1)
            pe.wait_ge(pro_dve, 15)
            for j in range(2):
                mm = pe.transpose(proj[2][:, j * 2:(j + 1) * 2], nrow[:, j * P:(j + 1) * P], ident[0:L, 0:L])
            mm.then_inc(pro_pe, 1)
            pe.wait_ge(pro_dve, 19)

            def begin(l, name):
                b, k = step_of(name)
                pe.wait_ge(aux_free[b], l * AUX_USES[b] + k + 1)
                return aux[b]

            def end(mm, name):
                mm.then_inc(aux_full[step_of(name)[0]], 1)

            def products(l, name, high, low, kind="", after=None, branch=None):
                def group(ph, i, u):
                    s = u % 2
                    n = use(l, ph, i, u)
                    if branch and u % 2:
                        pe.wait_ge(M[branch], l + 1)
                    pe.wait_ge(split_done[s], n + 2)
                    if ph.tiles:
                        for t in range(2):
                            bank = 2 * s + t
                            pe.wait_ge(bank_free[bank], bank_use(l, ph, i, u, bank) + 1)
                            for k in range(KT):
                                if kind == "natural":
                                    o = proj[bank][:, 0:256]
                                    a, b_ = (m[:, k, t * P:(t + 1) * P] for m in (high, low))
                                    c, d = (m[:, s, k * 256:(k + 1) * 256] for m in (wh, wl))
                                else:
                                    hi_, lo_ = (low if isinstance(low, tuple) and u % 2 else high) if kind == "mix" else (high, low)
                                    a, b_ = (m[:, s, k * 256 + t * P:k * 256 + (t + 1) * P] for m in (wh, wl))
                                    c, d = hi_[:, k, :], lo_[:, k, :]
                                    o = proj[bank][:, 0:hi_.shape[2]]
                                pe.matmul(o, a, c, start=(k == 0), stop=False)
                                pe.matmul(o, a, d, start=False, stop=False)
                                mm = pe.matmul(o, b_, c, start=False, stop=(k == KT - 1))
                            mm.then_inc(group_done[s] if t else first_done, 1)
                    else:
                        bank = u // 2
                        o = proj[bank][:, 0:T]
                        if u % 2 == 0:
                            pe.wait_ge(bank_free[bank], bank_use(l, ph, i, u, bank) + 1)
                        for k in range(HKT):
                            kk = k + HKT * (u % 2)
                            a, b_ = (m[:, s, k * P:(k + 1) * P] for m in (wh, wl))
                            pe.matmul(o, a, high[:, kk, :], start=(kk == 0), stop=False)
                            pe.matmul(o, a, low[:, kk, :], start=False, stop=False)
                            mm = pe.matmul(o, b_, high[:, kk, :], start=False, stop=(kk == FT - 1))
                        mm.then_inc(group_done[s], 1)
                passed(pe)
                each_group(pe, l, name, group, after)

            def total(l, name, ready):
                pe.wait_ge(M[ready], l + 1)
                o = begin(l, name)
                end(pe.matmul(o[:, 0, 0:T], ones[:], acc[:], start=True, stop=True), name)

            def turn(l, name, tiles):
                o = begin(l, name)
                if tiles[0][1].shape[0] <= 32:
                    passed(pe)
                for col, src in tiles:
                    n = src.shape[0]
                    mm = pe.transpose(o[0:src.shape[1], col // 512, col % 512:col % 512 + n], src, ident[0:n, 0:n])
                end(mm, name)

            with pe.Fori(0, L) as l:
                def ready(name):
                    pe.wait_ge(M[name], l + 1)

                ready("mem_split")
                products(l, "mv", memh, meml, "natural")
                total(l, "n1", "ssq1")
                ready("xn1")
                products(l, "f1i", xh, xl)
                pe.wait_ge(hidden, l * 2 * FT + FT)
                products(l, "f1o", hh, hl)
                total(l, "p1", "sqp1")
                ready("mem_split2")
                products(l, "mk", memh, meml)
                ready("mkt_all")
                for t in range(2):
                    turn(l, f"mkt{t}", [(j * P, mkt[:, j, t * P:(t + 1) * P]) for j in range(KT)])
                total(l, "n2", "ssq2")
                ready("xn2")
                pe.wait_ge(wab_loaded, 16 * (l + 1))
                o = begin(l, "gab")
                for t in range(3):
                    n = P if t < 2 else NS
                    for k in range(KT):
                        mm = pe.matmul(o[0:n, 0, t * 8:t * 8 + 8], y[:, k, t * P:t * P + n], wab[:, k, :],
                                       start=(k == 0), stop=(k == KT - 1))
                end(mm, "gab")

                products(l, "mq", xh, xl)
                ready("mqt")
                for s in range(2):
                    o = begin(l, f"ms{s}")
                    for hd in range(2):
                        for t in range(2):
                            for d in range(2):
                                j = 2 * (2 * s + hd) + d
                                mm = pe.matmul(o[:, hd, t * 256:(t + 1) * 256], mqt[:, j, t * P:(t + 1) * P], mkt[:, j, :],
                                               start=(d == 0), stop=(d == 1))
                    end(mm, f"ms{s}")
                for s in range(2):
                    ready(f"mpr{s}")
                    turn(l, f"mpt{s}", [(hd * 512 + m * 256 + t * P, prob[:, 4 * s + 2 * hd + t, m * P:(m + 1) * P])
                                        for hd in range(2) for m in range(2) for t in range(2)])
                for s in range(2):
                    ready(f"mpT{s}")
                    o = begin(l, f"mo{s}")
                    for hd in range(2):
                        h = 2 * s + hd
                        for dt in range(2):
                            for m in range(2):
                                mm = pe.matmul(o[:, hd, dt * 256:(dt + 1) * 256], mvn[:, m, h * 256 + dt * P:h * 256 + (dt + 1) * P],
                                               pt[:, h, m, :], start=(m == 0), stop=(m == 1))
                    end(mm, f"mo{s}")
                turn(l, "mqs", [(j * P, mqt[:, j, SEQ:T]) for j in range(KT)])
                ready("mqs")
                def spread(b):
                    o = begin(l, f"qb{b}")
                    for z in range(2):
                        mm = pe.matmul(o[:, z, :], ident[0:NS, b:b + 1].broadcast_to([NS, P]), qs[:, z * 512:(z + 1) * 512],
                                       start=True, stop=True)
                    end(mm, f"qb{b}")
                products(l, "rqk", xh, xl, after=spread)
                products(l, "rv", xh, xl, after=lambda g: spread(4 + g))
                ready("sall")
                turn(l, "smt", [(m * P, sall[:, m, :]) for m in range(2)])
                ready("spr")
                turn(l, "spt", [(m * 32, ps[:, m * P:(m + 1) * P]) for m in range(2)])
                ready("sptd")
                o = begin(l, "smo")
                for b in range(NS):
                    for m in range(2):
                        slot = unit_wait(pe, l, 2 * NS + 2 * b + m)
                        lhs = pmask[:, (m * NS + b) * 4 * NS:(m * NS + b + 1) * 4 * NS]
                        for z in range(2):
                            mm = pe.matmul(o[0:4 * NS, z, :], lhs, sring[:, slot, z * 512:(z + 1) * 512],
                                           start=((b, m) == (0, 0)), stop=((b, m) == (NS - 1, 1)))
                        if (b, m) != (NS - 1, 1):
                            mm.then_inc(unit_used[slot], 1)
                end(mm, "smo")
                ready("sov")
                turn(l, "smw", [(j * 4 * NS, sov[:, j * P:(j + 1) * P]) for j in range(KT)])
                products(l, "x2", (xh, xl), (oh, ol), "mix", branch="o_mem")

                ready("rraw")
                for j in range(4):
                    o = begin(l, f"rw{j}")
                    for t in range(2):
                        mm = pe.matmul(o[:, t, 0:T], swap[:], rot[:, 2 * j + t, :], start=True, stop=True)
                    end(mm, f"rw{j}")
                ready("rot")
                turn(l, "rkn", [((2 * h + t) * P, rot[:, 4 + h, t * P:(t + 1) * P]) for h in range(H) for t in range(2)])
                ready("rvt")
                for t in range(2):
                    turn(l, f"rvn{t}", [(j * P, rvt[:, j, t * P:(t + 1) * P]) for j in range(KT)])
                turn(l, "rvs", [(j * P, rvt[:, j, SEQ:T]) for j in range(KT)])
                turn(l, "rks", [(h * P, rot[:, 4 + h, SEQ:T]) for h in range(H)])
                for s in range(2):
                    o = begin(l, f"rs{s}")
                    for hd in range(2):
                        h = 2 * s + hd
                        pe.matmul(o[:, hd, 0:256], rot[:, 4 + h, 0:P], rot[:, h, 0:SEQ], start=True, stop=True)
                        mm = pe.matmul(o[:, hd, 256:384], rot[:, 4 + h, P:SEQ], rot[:, h, P:SEQ], start=True, stop=True)
                    end(mm, f"rs{s}")
                ready("rvn")
                for s in range(2):
                    ready(f"rp{s}")
                    o = begin(l, f"ro{s}")
                    for hd in range(2):
                        h = 2 * s + hd
                        for dt in range(2):
                            c = h * DV + dt * P
                            pe.matmul(o[:, hd, dt * 256:(dt + 1) * 256], vn[:, 0, c:c + P], pr[:, h, 0:256], start=True, stop=False)
                            mm = pe.matmul(o[:, hd, dt * 256 + P:(dt + 1) * 256], vn[:, 1, c:c + P], pr[:, h, 256:384],
                                           start=False, stop=True)
                    end(mm, f"ro{s}")
                ready("rkd")
                o = begin(l, "rst")
                for h in range(H):
                    for t in range(2):
                        mm = pe.matmul(o[:, h // 2, (h % 2) * DV:(h % 2 + 1) * DV], kn[:, 2 * h + t, :],
                                       vn[:, t, h * DV:(h + 1) * DV], start=(t == 0), stop=(t == 1))
                end(mm, "rst")

                def outer(name, b, n, values):
                    pe.wait_ge(state_kd, l * 2 * NS + n)
                    o = begin(l, name)
                    for h in range(H):
                        mm = pe.matmul(o[:, h // 2, (h % 2) * DV:(h % 2 + 1) * DV], kdb[:, b % 2, h * P:(h + 1) * P],
                                       values[:, h * DV:(h + 1) * DV], start=True, stop=True)
                    end(mm, name)

                def read_state(b, n, slot, banks, done):
                    pe.wait_ge(state_new, l * 2 * NS + n)
                    for h in range(H):
                        mm = pe.matmul(banks[h // 2][0:NS, (h % 2) * DV:(h % 2 + 1) * DV], qmask[:, (b * H + h) * NS:(b * H + h + 1) * NS],
                                       sring[:, slot, h * DV:(h + 1) * DV], start=(b == 0 and h % 2 == 0), stop=(b == NS - 1 and h % 2 == 1))
                    mm.then_inc(unit_used[slot] if b + 1 < NS else done, 1)

                ready("rvsd")
                sums = begin(l, "rqs")

                def retain(b):
                    read_state(b, b + 1, (4 * NS + b) % SRING, [sums[:, 0], sums[:, 1]], aux_full[PAIR["rqs"][0]])

                def update_states(g):
                    if g:
                        retain(g - 1)
                    outer(f"rS{g}", g, g + 1, vs)
                products(l, "gq", xh, xl, after=update_states)
                retain(NS - 1)
                def finish_retention(g):
                    if g == 0:
                        ready("rqv")
                        turn(l, "rqt", [(j * NS, qout_ret[:, j * P:(j + 1) * P]) for j in range(KT)])
                    elif g == 1:
                        ready("rsq")
                        for s in range(2):
                            o = begin(l, f"rn{s}")
                            for hd in range(2):
                                for dt in range(2):
                                    mm = pe.matmul(o[:, hd, 0:T], ones[:], rsq[:, 4 * s + 2 * hd + dt, :], start=(dt == 0), stop=(dt == 1))
                            end(mm, f"rn{s}")
                products(l, "rg", xh, xl, after=finish_retention)
                pe.wait_ge(scr_loaded, 16 * (l + 1))
                turn(l, "gcs", [(j * 24, scr[:, j * P:(j + 1) * P]) for j in range(16)])
                products(l, "x0", (xh, xl), (oh, ol), "mix", branch="o_ret")

                ready("gsq")
                for j in range(4):
                    o = begin(l, f"gn{j}")
                    for t in range(2):
                        mm = pe.matmul(o[:, t, 0:T], ones[:], sqg[:, 2 * j + t, :], start=True, stop=True)
                    end(mm, f"gn{j}")
                ready("tail")
                for z in range(2):
                    turn(l, f"gct{z}", [(j * P, tail[:, 8 * z + j, :]) for j in range(8)])
                for t in range(2):
                    turn(l, f"gvn{t}", [(j * P, qkvt[:, 8 + j, t * P:(t + 1) * P]) for j in range(KT)])
                ready("gqk")
                turn(l, "gkn", [((2 * h + t) * P, qkvt[:, 4 + h, t * P:(t + 1) * P]) for h in range(H) for t in range(2)])
                ready("gb_done")
                o = begin(l, "gcol")
                for c in range(2):
                    pe.matmul(o[:, 0, c * 4:c * 4 + 4], tri[:], gb[:, c, 0:4], start=True, stop=True)
                    mm = pe.matmul(o[:, 0, 8 + c * 4:12 + c * 4], ones[:], gb[:, c, 0:4], start=True, stop=True)
                end(mm, "gcol")
                o = begin(l, "gev")
                for h in range(H):
                    mm = pe.matmul(o[:, 0, h * NS:(h + 1) * NS], gb[0:NS, 2, h:h + 1].broadcast_to([NS, P]), ident[0:NS, 0:NS],
                                   start=True, stop=True)
                end(mm, "gev")
                for s in range(2):
                    mats = [(q, 2 * s + q // 2, q % 2) for q in range(4)]
                    o = begin(l, f"gbr{s}")
                    for q, h, c in mats:
                        pe.matmul(o[:, 0, q * P:(q + 1) * P], gb[:, c, h:h + 1].broadcast_to([P, P]), tri[:], start=True, stop=True)
                    for q, h, c in mats:
                        mm = pe.matmul(o[:, 1, q * P:(q + 1) * P], gb[:, c, 4 + h:5 + h].broadcast_to([P, P]), ident[:],
                                       start=True, stop=True)
                    end(mm, f"gbr{s}")
                    for step, other in (("gG", 4), ("gQ", 0)):
                        o = begin(l, f"{step}{s}")
                        for q, h, c in mats:
                            mm = pe.matmul(o[:, 0, q * P:(q + 1) * P], qkvt[:, 4 + h, c * P:(c + 1) * P],
                                           qkvt[:, other + h, c * P:(c + 1) * P], start=True, stop=True)
                        end(mm, f"{step}{s}")
                for s in range(2):
                    ready(f"g_at{s}")
                    turn(l, f"gT{s}", [(q * P, t_t[s][:, q, :]) for q in range(4)])
                for lv in range(6):
                    for s in range(2):
                        pe.wait_ge(inv_t, l * 12 + 2 * lv + s + 1)
                        o = begin(l, f"gy{lv}{s}")
                        for q in range(4):
                            mm = pe.matmul(o[:, 0, q * P:(q + 1) * P], c_t[s][:, q, :], t_m[s][:, q, :], start=True, stop=True)
                        end(mm, f"gy{lv}{s}")
                    for s in range(2):
                        pe.wait_ge(inv_y, l * 12 + 2 * lv + s + 1)
                        o = begin(l, f"gt{lv}{s}")
                        for q in range(4):
                            pe.matmul(o[:, 0, q * P:(q + 1) * P], t_t[s][:, q, :], y_m[s][:, q, :], start=True, stop=True)
                        for q in range(4):
                            mm = pe.matmul(o[:, 1, q * P:(q + 1) * P], y_m[s][:, q, :], t_t[s][:, q, :], start=True, stop=True)
                        end(mm, f"gt{lv}{s}")

                def per_head(name, lhs, rhs):
                    o = begin(l, name)
                    for h in range(H):
                        mm = pe.matmul(o[:, h // 2, (h % 2) * DV:(h % 2 + 1) * DV], lhs(h), rhs(h), start=True, stop=True)
                    end(mm, name)

                ready("gvb")
                per_head("gv0", lambda h: t_t[h // 2][:, 2 * (h % 2), :], lambda h: vb[:, h * DV:(h + 1) * DV])
                ready("gvn0d")
                per_head("gS0", lambda h: kd[:, 0, h, :], lambda h: vnew[:, h * DV:(h + 1) * DV])
                o = begin(l, "go0")
                for j in range(KT):
                    h = j // 2
                    mm = pe.matmul(o[:, j // 4, (j % 4) * P:(j % 4 + 1) * P], vnew[:, j * P:(j + 1) * P],
                                   a_q[h // 2][:, 2 * (h % 2), :], start=True, stop=True)
                end(mm, "go0")
                ready("gsg")
                per_head("gks", lambda h: qkvt[:, 4 + h, P:SEQ], lambda h: stg[:, h * DV:(h + 1) * DV])
                ready("gvb1")
                per_head("gv1", lambda h: t_t[h // 2][:, 2 * (h % 2) + 1, :], lambda h: vb[:, h * DV:(h + 1) * DV])
                ready("gvn1d")
                ready("gqd")
                o = begin(l, "go1")
                for j in range(KT):
                    h = j // 2
                    r = o[:, j // 4, (j % 4) * P:(j % 4 + 1) * P]
                    pe.matmul(r, vnew[:, j * P:(j + 1) * P], a_q[h // 2][:, 2 * (h % 2) + 1, :], start=True, stop=False)
                    mm = pe.matmul(r, stg[:, j * P:(j + 1) * P], qkvt[:, h, P:SEQ], start=False, stop=True)
                end(mm, "go1")
                per_head("gS1", lambda h: kd[:, 1, h, :], lambda h: vnew[:, h * DV:(h + 1) * DV])
                turn(l, "gkS", [(h * P, qkvt[:, 4 + h, SEQ:T]) for h in range(H)])
                turn(l, "gvS", [(j * P, qkvt[:, 8 + j, SEQ:T]) for j in range(KT)])
                def read_key(b):
                    slot = unit_wait(pe, l, 5 * NS + b)
                    o = begin(l, f"gr{b}")
                    for h in range(H):
                        mm = pe.matmul(o[0:NS, h // 2, (h % 2) * DV:(h % 2 + 1) * DV], kneg[:, h, :],
                                       sring[:, slot, h * DV:(h + 1) * DV], start=True, stop=True)
                    end(mm, f"gr{b}")

                ready("gsmp")
                read_key(0)
                outer("gx0", 0, NS + 1, vns)
                for b in range(NS):
                    if b + 1 < NS:
                        read_key(b + 1)
                    read_state(b, NS + b + 1, (5 * NS + b) % SRING, proj[2:4], M["gqsum"])
                    if b + 1 < NS:
                        outer(f"gx{b + 1}", b + 1, NS + b + 2, vns)
                def finish_delta(g):
                    if g == 0:
                        ready("gqv")
                        turn(l, "gqt", [(j * NS, qout[:, j * P:(j + 1) * P]) for j in range(KT)])
                    elif g == 1:
                        ready("g2sq")
                        for s in range(2):
                            o = begin(l, f"gm{s}")
                            for hd in range(2):
                                for dt in range(2):
                                    mm = pe.matmul(o[:, hd, 0:T], ones[:], sqw[:, 4 * s + 2 * hd + dt, :], start=(dt == 0), stop=(dt == 1))
                            end(mm, f"gm{s}")
                products(l, "gz", xh, xl, after=finish_delta)
                products(l, "x1", (xh, xl), (oh, ol), "mix", branch="o_gdn")

                ready("merged")
                products(l, "out", mh, ml)
                total(l, "p2", "sqp2")
                total(l, "n3", "ssq3")
                ready("xn3")
                products(l, "f2i", xh, xl)
                pe.wait_ge(hidden, l * 2 * FT + 2 * FT)
                products(l, "f2o", hh, hl)
                total(l, "p3", "sqp3")

            for t in range(3):
                n = P if t < 2 else NS
                pe.wait_ge(M["x1"], L + 1)
                if t == 2:
                    pe.wait_ge(pro_dve, 20)
                for k in range(KT):
                    mm = pe.transpose(aux[t % 2][0:n, k // 4, (k % 4) * P:(k % 4 + 1) * P], x[:, k, t * P:t * P + n], ident[:])
                mm.then_inc(pro_pe, 1)

        ACT_TILES = 22 * 2 + 24 + 16
        GATE0 = {"f1i": 0, "x2": 22, "rg": 30, "x0": 38, "gz": 46, "x1": 54, "f2i": 62}
        SQ0 = {"f1o": 0, "out": 8, "f2o": 16}

        def tile_wait(e, l, ph, i, u, t):
            if ph.tiles and t == 0:
                e.wait_ge(first_done, l * FIRSTS + ph.m0 + 4 * i + u + 1)
            else:
                e.wait_ge(group_done[u % 2], use(l, ph, i, u) + 2)
            return 2 * (u % 2) + t if ph.tiles else u // 2

        def two_on(name, ph, i, u):
            k = [p[0] for p in PHASES].index(name)
            n = 2 * i + u // 2 + 1
            if isinstance(i, int) and 4 * i + u >= ph.groups - 2:
                if k + 1 == len(PHASES):
                    return None, None
                k, n = k + 1, 0
            name = PHASES[k][0]
            up = {"f1i": n, "f2i": 11 + n}.get(name)
            return GW if PHASES[k][2] else HKT * P, up

        @block.scalar
        def _(act):
            order = Order(act, order_act)
            start_at_one(act, gate_used + sq_used + conv_used)
            act.wait_ge(const_loaded, 16 * 21)
            act.wait_ge(pro_act, 1)
            order.fresh()
            for t in range(2):
                order(act.activation(stg[:], mnat[:, t, :], ACT.Square, accum_out=srs[:, t:t + 1]))
            order(act.activation(srs[:], srs[:], ACT.Sqrt, bias=epst[:], scale=1.0 / D))
            act.sem_inc(pro_act, 1)

            def split(l, slot, n, size, up=None):
                act.wait_ge(raw_loaded[slot], 16 * (n + 1))
                if up is not None:
                    act.wait_ge(up_loaded[slot], 16 * (l * 22 + up + 1))
                act.wait_ge(group_done[slot], n + 1)
                act.copy(wh[:, slot, 0:size], raw[:, slot, 0:size]).then_inc(hi_done[slot], 1)

            def stream(l, name, tile=None):
                def body(ph, i, u):
                    if tile:
                        order.fresh()
                        tile(ph, i, u)
                    size, up = two_on(name, ph, i, u)
                    if size:
                        split(l, u % 2, use(l, ph, i, u) + 1, size, up)
                each_group(act, l, name, body)

            def through(l, func, every=None):
                def tile(ph, i, u):
                    if every == "gate" and u % 2:
                        return
                    for t in range(1 if every == "first" else 2):
                        if every == "first":
                            n, slot = 2 * i + u // 2, u % 2
                            a = GATE0[ph.name] + 4 * i + u
                        else:
                            g = 4 * i + u if every is None else 2 * i + u // 2
                            n, slot = g, t
                            a = GATE0[ph.name] + 2 * g + t
                        bank = tile_wait(act, l, ph, i, u, t)
                        act.wait_ge(gate_used[slot], l * (ACT_TILES // 2) + GATE0[ph.name] // 2 + n + 1)
                        order(act.activation(gate[:, slot, :], proj[bank][:, 0:T], func))
                        act.sem_inc(bank_free[bank], 1)
                        act.sem_inc(gate_ready, 1)
                return tile

            def squares(l):
                def tile(ph, i, u):
                    if not ph.tiles and u % 2 == 0:
                        return
                    for t in range(2 if ph.tiles else 1):
                        slot = t if ph.tiles else u // 2
                        n = 4 * i + u if ph.tiles else i
                        bank = tile_wait(act, l, ph, i, u, t)
                        act.wait_ge(sq_used[slot], l * 12 + SQ0[ph.name] // 2 + n + 1)
                        order(act.activation(sqt[:, slot, :], proj[bank][:, 0:T], ACT.Square))
                        act.sem_inc(sq_ready, 1)
                return tile

            act.wait_ge(pro_dve, 19)
            with act.Fori(0, L) as l:
                def ready(name):
                    act.wait_ge(M[name], l + 1)

                def tell(name):
                    act.sem_inc(M[name], 1)

                def root(name, out):
                    o = take(act, l, name)
                    order(act.activation(rt[:], o[:, 0, 0:T], ACT.Sqrt, bias=epst[:], scale=1.0 / D))
                    release(act, name)
                    tell(out)

                def square_x(n):
                    norm_wait(act, l, "x_half", n)
                    order(act.activation(sqw[:, 0:4, :], x[:, 0:4, :], ACT.Square))
                    tell("sq_half")
                    ready(f"x{n}")
                    order(act.activation(sqw[:, 4:8, :], x[:, 4:8, :], ACT.Square))
                    tell(f"sq{n}")

                def high_parts(n):
                    for c, y_in, out in ((slice(0, 4), "y_half", "xh_half"), (slice(4, 8), "y_all", "xh_all")):
                        norm_wait(act, l, y_in, n)
                        order(act.copy(xh[:, c, :], y[:, c, :]))
                        tell(out)

                def scale_memory(name):
                    for k in range(KT):
                        order(act.activation(mkt[:, k, :], memr[:, k, :], ACT.Copy, scale=gains[:, k, bass.ds(l + 12, 1)]))
                    order(act.copy(memh[:], mkt[:]))
                    tell(name)

                order.fresh()
                for s in range(2):
                    split(l, s, l * HALF, GW)
                scale_memory("memhi")
                square_x(1)
                stream(l, "mv")
                root("n1", "rt1")
                high_parts(1)
                stream(l, "f1i", through(l, ACT.Silu, "first"))
                stream(l, "f1o", squares(l))
                order.fresh()
                root("p1", "rtp1")
                scale_memory("memhi2")
                square_x(2)
                stream(l, "mk")
                root("n2", "rt2")
                high_parts(2)
                ready("ab_neg")
                order(act.activation(abt[:, 2], abt[:, 1], ACT.Exp))
                order(act.activation(abt[:, 3, 0], alog[:, l], ACT.Exp))
                order(act.activation(abt[:, 2], abt[:, 2], ACT.Ln, bias=ones[:, 0:1]))
                order(act.activation(gb[:, :, 4:8], gb[:, :, 4:8], ACT.Sigmoid))
                tell("ab_exp")

                stream(l, "mq")
                for s in range(2):
                    ready(f"mmx{s}")
                    o = take(act, l, f"ms{s}")
                    for q in range(4):
                        order(act.activation(prob[:, 4 * s + q, :], o[:, q // 2, (q % 2) * 256:(q % 2 + 1) * 256], ACT.Exp,
                                             bias=mx[:, 4 * s + q:4 * s + q + 1], scale=DV ** -0.5,
                                             accum_out=msum[:, 4 * s + q:4 * s + q + 1]))
                    release(act, f"ms{s}")
                    tell(f"mpe{s}")
                stream(l, "rqk")
                stream(l, "rv")
                order.fresh()
                ready("smx")
                o = take(act, l, "smt")
                order(act.activation(ps[:], o[0:32, 0, 0:NM], ACT.Exp, bias=smx[:, 0:1], scale=DV ** -0.5, accum_out=smx[:, 1:2]))
                release(act, "smt")
                tell("spe")
                stream(l, "x2", through(l, ACT.Sigmoid, "gate"))

                def conv_input(ph, i, u):
                    for t in range(2):
                        bank = tile_wait(act, l, ph, i, u, t)
                        act.wait_ge(conv_used[t], l * 8 + 4 * i + u + 1)
                        order(act.copy(full[:, t, 3:SEQ + 3], proj[bank][:, 0:SEQ]))
                        order(act.copy(sc[:, 2 * (4 * i + u) + t, :, 3], proj[bank][:, SEQ:T]))
                        act.sem_inc(bank_free[bank], 1)
                        act.sem_inc(conv_ready, 1)
                stream(l, "gq", conv_input)
                order.fresh()

                def inverse_root(src, steps, out, name):
                    for s, st in enumerate(steps):
                        o = take(act, l, st)
                        order(act.activation(out[:, 2 * s:2 * s + 2, :], o[:, :, 0:T], ACT.Ln, bias=epst[:], scale=src))
                        release(act, st)
                    order(act.activation(out[:, 0:2 * len(steps), :], out[:, 0:2 * len(steps), :], ACT.Exp, scale=-0.5))
                    tell(name)

                ready("rof")
                order(act.activation(rsq[:], rvt[:], ACT.Square))
                tell("rsq")
                inverse_root(1.0 / DV, ["rn0", "rn1"], r4, "rlr")
                stream(l, "rg", through(l, ACT.Silu))
                ready("conv_p")
                order(act.activation(qkvt[:, :, 0:SEQ], qkvt[:, :, 0:SEQ], ACT.Silu))
                ready("conv_s")
                order(act.activation(qkvt[:, :, SEQ:T], qkvt[:, :, SEQ:T], ACT.Silu))
                ready("o_ret")
                order(act.activation(sqg[:], qkvt[:, 0:8, :], ACT.Square))
                tell("gsq")
                stream(l, "x0", through(l, ACT.Sigmoid, "gate"))
                order.fresh()
                inverse_root(1.0, [f"gn{j}" for j in range(4)], sqg, "gqr")
                ready("bcd")
                order(act.activation(ex[:], ex[:], ACT.Exp))
                tell("gexp")
                o = take(act, l, "gev")
                order(act.activation(egb[:], o[:, 0, 0:H * NS], ACT.Exp))
                release(act, "gev")
                tell("geb")
                for s in range(2):
                    o = take(act, l, f"gbr{s}")
                    ready(f"dm{s}")
                    for hd in range(2):
                        q = 2 * hd + 1
                        order(act.activation(erow[:, 2 * s + hd, :], o[:, 0, q * P:(q + 1) * P], ACT.Exp))
                    order(act.activation(y_m[s][:], y_m[s][:], ACT.Exp))
                    release(act, f"gbr{s}")
                    tell(f"dme{s}")
                for lv in range(6):
                    for s in range(2):
                        order(act.copy(y_m[s][:].rearrange("p q m -> p (q m)"), take(act, l, f"gy{lv}{s}")[:, 0, :]))
                        release(act, f"gy{lv}{s}")
                        act.sem_inc(inv_y, 1)
                ready("gof")
                order(act.activation(sqw[:], qkvt[:, 8:16, :], ACT.Square))
                tell("g2sq")
                inverse_root(1.0 / DV, ["gm0", "gm1"], r4, "glr")
                stream(l, "gz", through(l, ACT.Silu))
                stream(l, "x1", through(l, ACT.Sigmoid, "gate"))
                stream(l, "out", squares(l))
                order.fresh()
                root("p2", "rtp2")
                square_x(3)
                root("n3", "rt3")
                high_parts(3)
                stream(l, "f2i", through(l, ACT.Silu, "first"))
                stream(l, "f2o", squares(l))
                order.fresh()
                root("p3", "rtp3")

        @block.vector
        def _(dve):
            order = Order(dve, order_dve)
            tt, ts_, stt = dve.tensor_tensor, dve.tensor_scalar, dve.scalar_tensor_tensor
            cp = dve.tensor_copy
            order.fresh()
            order(dve.memset(epst[:], EPS))
            order(dve.memset(ones[:], 1.0))
            order(dve.memset(full[:], 0.0))
            order(dve.memset(gb[:], 0.0))
            dve.sem_inc(pro_act, 1)
            dve.wait_ge(const_loaded, 16 * 21)
            for k in range(KT):
                dve.wait_ge(pro_pe, k + 1)
                order(cp(x[:, k, :], proj[k % 4][:, 0:T]))
                dve.sem_inc(pro_dve, 1)
            dve.wait_ge(pro_act, 2)
            order(dve.reciprocal(srs[:], srs[:]))
            for t in range(2):
                order(ts_(mnat[:, t, :], mnat[:, t, :], srs[:, t:t + 1], None, ALU.mult))
            dve.sem_inc(pro_mem, 1)
            for k in range(KT):
                dve.wait_ge(pro_pe, k + 9)
                order(cp(memr[:, k, :], proj[k % 4][:, 0:NM]))
                dve.sem_inc(pro_dve, 1)
            dve.wait_ge(pro_pe, 17)
            order(cp(gains[:], proj[0][:, 0:KT * 16].rearrange("p (k n) -> p k n", n=16)[:, :, 0:14]))
            dve.sem_inc(pro_dve, 1)
            dve.wait_ge(pro_pe, 18)
            order(cp(convw[:], proj[1][:, 0:P].rearrange("p (j n) -> p j n", n=8)))
            dve.sem_inc(pro_dve, 1)
            dve.wait_ge(pro_pe, 19)
            order(cp(gng[:], proj[2][:, 0:4].rearrange("p (j n) -> p j n", n=2)))
            dve.sem_inc(pro_dve, 1)
            dve.sem_inc(M["x_half"], 1)
            dve.sem_inc(M["x1"], 1)

            def split(l, slot, n, size):
                dve.wait_ge(hi_done[slot], n + 1)
                dve.tensor_sub(wl[:, slot, 0:size], raw[:, slot, 0:size], wh[:, slot, 0:size].bitcast(F32)).then_inc(split_done[slot], 1)

            def stream(l, name, tile=None, after=None):
                def body(ph, i, u):
                    if tile:
                        order.fresh()
                        tile(ph, i, u)
                    size, _ = two_on(name, ph, i, u)
                    if size:
                        split(l, u % 2, use(l, ph, i, u) + 1, size)
                each_group(dve, l, name, body, after)
                order.fresh()

            def parts(high, low, src):
                order(cp(high, src))
                order(tt(low, src, high.bitcast(F32), ALU.subtract))

            def hidden_tile(l, first):
                def tile(ph, i, u):
                    j = 4 * i + u
                    bank = tile_wait(dve, l, ph, i, u, 1)
                    dve.wait_ge(gate_ready, l * ACT_TILES + GATE0[ph.name] + j + 1)
                    order(tt(tmpf[:], proj[bank][:, 0:T], gate[:, u % 2, :], ALU.mult))
                    dve.sem_inc(bank_free[bank], 1)
                    dve.sem_inc(gate_used[u % 2], 1)
                    parts(hh[:, j, :], hl[:, j, :], tmpf[:])
                    dve.sem_inc(hidden, 1)
                return tile

            def result_tile(l, gain):
                def tile(ph, i, u):
                    if not ph.tiles and u % 2 == 0:
                        return
                    for t in range(2 if ph.tiles else 1):
                        j = 2 * (4 * i + u) + t if ph.tiles else 2 * i + u // 2
                        slot = t if ph.tiles else u // 2
                        bank = tile_wait(dve, l, ph, i, u, t)
                        dve.wait_ge(sq_ready, l * 24 + SQ0[ph.name] + j + 1)
                        order(ts_(y[:, j, :], proj[bank][:, 0:T], gl[:, j, gain:gain + 1], None, ALU.mult))
                        order(tt(acc[:], acc[:], sqt[:, slot, :], ALU.add))
                        dve.sem_inc(bank_free[bank], 1)
                        dve.sem_inc(sq_used[slot], 1)
                return tile

            def copy_tile(l, out):
                def tile(ph, i, u):
                    for t in range(2):
                        bank = tile_wait(dve, l, ph, i, u, t)
                        dst = out(4 * i + u, t)
                        order(cp(dst, proj[bank][:, 0:dst.shape[-1]]))
                        dve.sem_inc(bank_free[bank], 1)
                return tile

            def gated_tile(l, out, gain=None):
                def tile(ph, i, u):
                    for t in range(2):
                        j = 2 * (4 * i + u) + t
                        dve.wait_ge(gate_ready, l * ACT_TILES + GATE0[ph.name] + j + 1)
                        if gain is None:
                            order(tt(tmpf[:], gate[:, t, :], out[:, j, :], ALU.mult))
                        else:
                            order(stt(tmpf[:], gate[:, t, :], gain[:, t:t + 1], out[:, 8 + j, :], ALU.mult, ALU.mult))
                        dve.sem_inc(gate_used[t], 1)
                        parts(oh[:, j, :], ol[:, j, :], tmpf[:])
                return tile

            def merge_tile(l, first, last=False):
                def tile(ph, i, u):
                    if u % 2 == 0:
                        return
                    for t in range(2):
                        j = 2 * (2 * i + u // 2) + t
                        bank = tile_wait(dve, l, ph, i, u, t)
                        dve.wait_ge(gate_ready, l * ACT_TILES + GATE0[ph.name] + j + 1)
                        order(tt(y[:, j, :] if first else tmpf[:], proj[bank][:, 0:T], gate[:, t, :], ALU.mult))
                        dve.sem_inc(bank_free[bank], 1)
                        dve.sem_inc(gate_used[t], 1)
                        if not first:
                            order(tt(y[:, j, :], y[:, j, :], tmpf[:], ALU.add))
                        if last:
                            parts(mh[:, j, :], ml[:, j, :], y[:, j, :])
                return tile

            with dve.Fori(0, L) as l:
                def ready(name):
                    dve.wait_ge(M[name], l + 1)

                def tell(name):
                    dve.sem_inc(M[name], 1)

                def flat(name):
                    return take(dve, l, name)[:].rearrange("p a b -> p (a b)")

                order.fresh()
                def mask_queries(q):
                    order(dve.memset(qmask[:], 0.0))
                    blocks = qmask[:].rearrange("p (b x) -> p b x", x=4 * NS + 1)[:, :, 0:4 * NS]
                    order(cp(blocks.rearrange("p b (h e) -> p b h e", e=NS)[:, :, :, 0], q.rearrange("p h b -> p b h")))

                def read_rows(banks, dst, last):
                    dve.sem_inc(unit_used[last % SRING], 1)
                    for z in range(2):
                        order(cp(dst[:, z * 512:(z + 1) * 512], banks[z][0:NS, :]))

                def split_memory(high, name):
                    ready(high)
                    order(tt(meml[:], mkt[:], memh[:].bitcast(F32), ALU.subtract))
                    tell(name)

                def sum_x(n):
                    norm_wait(dve, l, "sq_half", n)
                    order(dve.tensor_reduce(acc[:], sqw[:, 0:4, :].rearrange("p k t -> p t k"), AX.X, ALU.add))
                    ready(f"sq{n}")
                    order(dve.tensor_reduce(tmpf[:], sqw[:, 4:8, :].rearrange("p k t -> p t k"), AX.X, ALU.add))
                    order(tt(acc[:], acc[:], tmpf[:], ALU.add))
                    tell(f"ssq{n}")

                def norm_x(n, gain):
                    ready(f"rt{n}")
                    order(dve.reciprocal(rt[:], rt[:]))
                    for k in range(KT):
                        order(stt(y[:, k, :], x[:, k, :], gl[:, k, gain:gain + 1], rt[:], ALU.mult, ALU.mult))
                        if k == 3:
                            tell("y_half")
                    tell("y_all")
                    for c, name in ((slice(0, 4), "xh_half"), (slice(4, 8), "xh_all")):
                        norm_wait(dve, l, name, n)
                        order(tt(xl[:, c, :], y[:, c, :], xh[:, c, :].bitcast(F32), ALU.subtract))
                    tell(f"xn{n}")

                def add_result(n, nxt):
                    ready(f"rtp{n}")
                    order(dve.reciprocal(rt[:], rt[:]))
                    for c in (slice(0, 4), slice(4, 8)):
                        order(tt(y[:, c, :], y[:, c, :], rt[:].unsqueeze(1).broadcast_to([P, 4, T]), ALU.mult))
                        order(tt(x[:, c, :], x[:, c, :], y[:, c, :], ALU.add))
                        tell("x_half" if c.start == 0 else nxt)

                for s in range(2):
                    split(l, s, l * HALF, GW)
                split_memory("memhi", "mem_split")
                g2 = gains[:].rearrange("p k (a l) -> p k a l", l=L)
                order(cp(gl[:], g2[:, :, :, l]))
                for a in (1, 5):
                    order(ts_(gl[:, :, a:a + 1], gl[:, :, a:a + 1], 0.5, None, ALU.mult))
                order(cp(cwl[:], convw[:].rearrange("p j (l k) -> p j l k", l=L)[:, :, l, :]))
                order(cp(gnl[:], gng[:, :, l]))

                sum_x(1)
                stream(l, "mv", copy_tile(l, lambda g, t: mvn[:, t, bass.ds(g * 256, 256)]))
                tell("mvn")
                norm_x(1, 0)
                stream(l, "f1i", hidden_tile(l, True))
                order(dve.memset(acc[:], 0.0))
                stream(l, "f1o", result_tile(l, 1))
                tell("sqp1")
                split_memory("memhi2", "mem_split2")
                add_result(1, "x2")
                sum_x(2)
                stream(l, "mk", copy_tile(l, lambda g, t: mkt[:, 2 * g + t, :]))
                tell("mkt_all")
                for t in range(2):
                    order(cp(mkn[:, t, :], flat(f"mkt{t}")))
                    release(dve, f"mkt{t}")
                tell("mkn1")
                norm_x(2, 2)
                o = take(dve, l, "gab")
                order(cp(gb[:, 0:2, :], o[:, 0, 0:16].rearrange("p (t n) -> p t n", t=2)))
                order(cp(gb[0:NS, 2, :], o[0:NS, 0, 16:24]))
                release(dve, "gab")
                tell("ab_in")
                order(tt(abt[:, 0], gb[:, :, 0:4], dtb[:, l, :].unsqueeze(1).broadcast_to([P, 3, H]), ALU.add))
                order(ts_(abt[:, 1], abt[:, 0], -1.0, None, ALU.mult))
                order(tt(abt[:, 1], abt[:, 0], abt[:, 1], ALU.min))
                tell("ab_neg")
                ready("ab_exp")
                order(stt(abt[:, 0], abt[:, 0], 0.0, abt[:, 2], ALU.max, ALU.add))
                order(stt(gb[:, :, 0:4], abt[:, 0], -1.0, abt[:, 3, 0:1].broadcast_to([P, 3, H]), ALU.mult, ALU.mult))
                tell("gb_done")

                stream(l, "mq", copy_tile(l, lambda g, t: mqt[:, 2 * g + t, :]))
                tell("mqt")
                dve.wait_ge(mk_stored, 16 * (l + 1))
                for s in range(2):
                    o = flat(f"ms{s}").rearrange("p (q m) -> p q m", m=NM)
                    order(dve.tensor_reduce(mx[:, 4 * s:4 * s + 4], o, AX.X, ALU.max))
                    order(ts_(mx[:, 4 * s:4 * s + 4], mx[:, 4 * s:4 * s + 4], -DV ** -0.5, None, ALU.mult))
                    tell(f"mmx{s}")
                for s in range(2):
                    ready(f"mpe{s}")
                    order(dve.reciprocal(msum[:, 4 * s:4 * s + 4], msum[:, 4 * s:4 * s + 4]))
                    order(tt(prob[:, 4 * s:4 * s + 4, :], prob[:, 4 * s:4 * s + 4, :],
                             msum[:, 4 * s:4 * s + 4].unsqueeze(2).broadcast_to([P, 4, NM]), ALU.mult))
                    tell(f"mpr{s}")
                for s in range(2):
                    order(cp(pt[:, 2 * s:2 * s + 2].rearrange("p h m t -> p (h m t)"), flat(f"mpt{s}")))
                    release(dve, f"mpt{s}")
                    tell(f"mpT{s}")
                for s in range(2):
                    o = flat(f"mo{s}").rearrange("p (j t) -> p j t", j=4)
                    parts(oh[:, 4 * s:4 * s + 4, 0:SEQ], ol[:, 4 * s:4 * s + 4, 0:SEQ], o)
                    release(dve, f"mo{s}")
                order(cp(qs[:], flat("mqs")[0:NS, :]))
                release(dve, "mqs")
                tell("mqs")
                def score(b):
                    o = flat(f"qb{b}")
                    for m in range(2):
                        slot = unit_wait(dve, l, 2 * b + m)
                        for h in range(H):
                            order(dve.tensor_tensor_reduce(junk[:], sring[:, slot, h * DV:(h + 1) * DV], o[:, h * DV:(h + 1) * DV],
                                                           1.0, 0.0, ALU.mult, ALU.add, sall[:, m, 4 * b + h:4 * b + h + 1]))
                        dve.sem_inc(unit_used[slot], 1)
                    release(dve, f"qb{b}")
                stream(l, "rqk", copy_tile(l, lambda g, t: rot[:, 2 * g + t, :]), after=score)
                tell("rraw")
                stream(l, "rv", copy_tile(l, lambda g, t: rvt[:, 2 * g + t, :]), after=lambda g: score(4 + g))
                tell("rvt")
                tell("sall")
                o = take(dve, l, "smt")[0:32, 0, 0:NM]
                order(dve.tensor_reduce(smx[:, 0:1], o, AX.X, ALU.max))
                order(ts_(smx[:, 0:1], smx[:, 0:1], -DV ** -0.5, None, ALU.mult))
                tell("smx")
                ready("spe")
                order(dve.reciprocal(smx[:, 1:2], smx[:, 1:2]))
                order(ts_(ps[:], ps[:], smx[:, 1:2], None, ALU.mult))
                tell("spr")
                order(dve.memset(pmask[:], 0.0))
                w = 4 * NS
                for m in range(2):
                    blocks = pmask[:, m * NS * w:m * NS * w + NS * (w + 4)].rearrange("p (b x) -> p b x", x=w + 4)[:, :, 0:4]
                    order(cp(blocks, take(dve, l, "spt")[:, 0, m * w:(m + 1) * w].rearrange("p (b h) -> p b h", h=4)))
                release(dve, "spt")
                tell("sptd")
                order(cp(sov[:], flat("smo")[0:4 * NS, :]))
                release(dve, "smo")
                dve.sem_inc(unit_used[(4 * NS - 1) % SRING], 1)
                tell("sov")
                w = 2 * 4 * NS + 1
                o = flat("smw")[:, 0:H * w].rearrange("p (h x) -> p h x", x=w)[:, :, 0:w - 1]
                order(cp(pts[:].rearrange("p (h d) b -> p h d b", h=H), o.rearrange("p h (d b f) -> p h d b f", d=2, f=4)[:, :, :, :, 0]))
                release(dve, "smw")
                parts(oh[:, :, SEQ:T], ol[:, :, SEQ:T], pts[:])
                tell("o_mem")
                stream(l, "x2", merge_tile(l, True))

                for j in range(4):
                    o = take(dve, l, f"rw{j}")[:, :, 0:T]
                    c = 0 if j < 2 else 2
                    r = rot[:, 2 * j:2 * j + 2, :]
                    order(tt(r, r, rot_tab[:, c:c + 1, :].broadcast_to([P, 2, T]), ALU.mult))
                    sw = rsq[:, 0:2, :]
                    order(tt(sw, o, rot_tab[:, c + 1:c + 2, :].broadcast_to([P, 2, T]), ALU.mult))
                    release(dve, f"rw{j}")
                    order(tt(r, r, sw, ALU.add))
                tell("rot")
                order(tt(kn[:], flat("rkn").rearrange("p (n d) -> p n d", d=P), kdec_tab[:].unsqueeze(2).broadcast_to([P, 8, P]), ALU.mult))
                release(dve, "rkn")
                tell("rkd")
                for t in range(2):
                    order(cp(vn[:, t, :], flat(f"rvn{t}")))
                    release(dve, f"rvn{t}")
                tell("rvn")
                order(cp(vs[:], flat("rvs")[0:NS, :]))
                release(dve, "rvs")
                order(cp(ks[:], flat("rks")[0:NS, 0:512]))
                release(dve, "rks")
                for s in range(2):
                    o = take(dve, l, f"rs{s}")
                    order(tt(pr[:, 2 * s:2 * s + 2, 0:256], o[:, :, 0:256], dec_tab[:, 2 * s:2 * s + 2, :], ALU.mult))
                    order(tt(pr[:, 2 * s:2 * s + 2, 256:384], o[:, :, 256:384], dec_tab[:, 2 * s:2 * s + 2, 0:P], ALU.mult))
                    release(dve, f"rs{s}")
                    tell(f"rp{s}")
                for s in range(2):
                    order(cp(rvt[:, 4 * s:4 * s + 4, 0:SEQ], flat(f"ro{s}").rearrange("p (j t) -> p j t", j=4)))
                    release(dve, f"ro{s}")
                order(cp(stg[:], flat("rst")))
                release(dve, "rst")
                tell("rS_out")

                mask_queries(rot[:, 0:4, SEQ:T])
                tell("rvsd")

                def one_row(b):
                    order(ts_(kdb[:, b % 2, :], ks[:], ident[0:NS, b:b + 1], None, ALU.mult))
                    dve.sem_inc(state_kd, 1)

                def update(name, slot, decay):
                    o = flat(name)
                    for h in range(H):
                        r = sring[:, slot, h * DV:(h + 1) * DV]
                        order(stt(r, r, decay(h), o[:, h * DV:(h + 1) * DV], ALU.mult, ALU.add))
                    release(dve, name)
                    dve.sem_inc(state_new, 1)

                def conv_tile(ph, i, u):
                    for t in range(2):
                        j = 2 * (4 * i + u) + t
                        dve.wait_ge(conv_ready, l * 16 + j + 1)
                        r = qkvt[:, j, 0:SEQ]
                        order(ts_(r, full[:, t, 0:SEQ], cwl[:, j, 0:1], None, ALU.mult))
                        for k in range(1, CW):
                            order(stt(r, full[:, t, k:k + SEQ], cwl[:, j, k:k + 1], r, ALU.mult, ALU.add))
                        order(cp(tail[:, j, 0:3], full[:, t, SEQ:SEQ + 3]))
                        dve.sem_inc(conv_used[t], 1)

                def update_states(g):
                    if g + 1 < NS:
                        one_row(g + 1)
                    unit_wait(dve, l, 4 * NS + g)
                    update(f"rS{g}", (4 * NS + g) % SRING, lambda h: float(np.exp(np.log1p(-2.0 ** (-5 - h)))))

                one_row(0)
                stream(l, "gq", conv_tile, after=update_states)
                tell("conv_p")
                o = take(dve, l, "rqs")
                read_rows([o[:, 0], o[:, 1]], qout_ret, 5 * NS - 1)
                release(dve, "rqs")
                tell("rqv")
                order(cp(rvt[:, :, SEQ:T], flat("rqt")[:, 0:KT * NS].rearrange("p (j b) -> p j b", b=NS)))
                release(dve, "rqt")
                tell("rof")
                ready("rlr")
                v4 = "p (h d) t -> p h d t"
                order(tt(rvt[:].rearrange(v4, d=2), rvt[:].rearrange(v4, d=2), r4[:].unsqueeze(2).broadcast_to([P, H, 2, T]), ALU.mult))
                stream(l, "rg", gated_tile(l, rvt))
                tell("o_ret")
                order(cp(sc[:, :, :, 0:3], flat("gcs")[:, 0:384].rearrange("p (j b k) -> p j b k", b=NS, k=3)))
                release(dve, "gcs")
                for k in range(CW):
                    w = cwl[:, :, k:k + 1].broadcast_to([P, 16, NS])
                    if k == 0:
                        order(tt(qkvt[:, :, SEQ:T], sc[:, :, :, 0], w, ALU.mult))
                    else:
                        order(tt(csum[:], sc[:, :, :, k], w, ALU.mult))
                        order(tt(qkvt[:, :, SEQ:T], qkvt[:, :, SEQ:T], csum[:], ALU.add))
                tell("conv_s")
                order(cp(tail[:, :, 3:].rearrange("p j (b k) -> p j b k", k=3), sc[:, :, :, 1:4]))
                tell("tail")
                stream(l, "x0", merge_tile(l, False))


                for z in range(2):
                    order(cp(cso[:, z * 1024:(z + 1) * 1024], flat(f"gct{z}")[0:27, :]))
                    release(dve, f"gct{z}")
                tell("cso")
                ready("gqr")
                order(stt(qkvt[:, 0:4, :], qkvt[:, 0:4, :], DK ** -0.5, sqg[:, 0:4, :], ALU.mult, ALU.mult))
                order(tt(qkvt[:, 4:8, :], qkvt[:, 4:8, :], sqg[:, 4:8, :], ALU.mult))
                tell("gqk")
                dve.wait_ge(conv_stored, 32 * (l + 1))
                for t in range(2):
                    order(cp(vn[:, t, :], flat(f"gvn{t}")))
                    release(dve, f"gvn{t}")
                order(cp(kn[:].rearrange("p n d -> p (n d)"), flat("gkn")))
                release(dve, "gkn")
                order(cp(bc[:], flat("gcol")[:, 0:16]))
                release(dve, "gcol")
                order(tt(ex[:, 0:8], bc[:, 8:16], bc[:, 0:8], ALU.subtract))
                order(cp(ex[:, 8:24], bc[:]))
                tell("bcd")
                ready("gexp")
                order(ts_(ex[:, 8:16], ex[:, 8:16], -1.0, None, ALU.mult))
                ready("geb")

                def masked(s, k):
                    order(tt(c_t[s][:], a_t[s][:], masks[:, k:k + 1, :].broadcast_to([P, 4, P]), ALU.mult))

                for s in range(2):
                    o = take(dve, l, f"gbr{s}")
                    for q in range(4):
                        col = (q % 2) * 4 + 2 * s + q // 2
                        order(ts_(y_m[s][:, q, :], o[:, 0, q * P:(q + 1) * P], bc[:, col:col + 1], 0.0, ALU.subtract, ALU.min))
                    order(cp(a_t[s][:].rearrange("p q m -> p (q m)"), o[:, 1, :]))
                    tell(f"dm{s}")
                    ready(f"dme{s}")
                    order(tt(y_m[s][:], y_m[s][:], tri[:].unsqueeze(1).broadcast_to([P, 4, P]), ALU.mult))
                    o = take(dve, l, f"gG{s}")[:, 0, :].rearrange("p (q m) -> p q m", q=4)
                    order(tt(a_t[s][:], a_t[s][:], o, ALU.mult))
                    release(dve, f"gG{s}")
                    order(tt(a_t[s][:], a_t[s][:], y_m[s][:], ALU.mult))
                    o = take(dve, l, f"gQ{s}")[:, 0, :].rearrange("p (q m) -> p q m", q=4)
                    order(tt(a_q[s][:], y_m[s][:], o, ALU.mult))
                    release(dve, f"gQ{s}")
                    masked(s, 0)
                    order(stt(t_t[s][:], c_t[s][:], -1.0, ident[:].unsqueeze(1).broadcast_to([P, 4, P]), ALU.mult, ALU.add))
                    tell(f"g_at{s}")
                for s in range(2):
                    order(cp(t_m[s][:].rearrange("p q m -> p (q m)"), take(dve, l, f"gT{s}")[:, 0, :]))
                    release(dve, f"gT{s}")
                    masked(s, 1)
                    dve.sem_inc(inv_t, 1)
                for lv in range(6):
                    for s in range(2):
                        if lv < 5:
                            dve.wait_ge(inv_y, l * 12 + 2 * lv + s + 1)
                            masked(s, lv + 2)
                        o = take(dve, l, f"gt{lv}{s}")
                        if lv < 5:
                            order(tt(t_m[s][:].rearrange("p q m -> p (q m)"), t_m[s][:].rearrange("p q m -> p (q m)"), o[:, 0, :], ALU.subtract))
                        order(tt(t_t[s][:].rearrange("p q m -> p (q m)"), t_t[s][:].rearrange("p q m -> p (q m)"), o[:, 1, :], ALU.subtract))
                        release(dve, f"gt{lv}{s}")
                        if lv < 5:
                            dve.sem_inc(inv_t, 1)
                for h in range(H):
                    order(ts_(vb[:, h * DV:(h + 1) * DV], vn[:, 0, h * DV:(h + 1) * DV], gb[:, 0, 4 + h:5 + h], None, ALU.mult))
                tell("gvb")
                for c in range(2):
                    order(tt(kd[:, c], kn[:].rearrange("p (h c) d -> p h c d", c=2)[:, :, c, :],
                             ex[:, c * 4:c * 4 + 4].unsqueeze(2).broadcast_to([P, H, P]), ALU.mult))
                order(cp(vnew[:], flat("gv0")))
                release(dve, "gv0")
                tell("gvn0d")
                dve.wait_ge(ret_stored, 16 * (l + 1))
                order(cp(stg[:], flat("gS0")))
                release(dve, "gS0")
                tell("gsg")
                order(cp(qkvt[:, 8:16, 0:P], flat("go0").rearrange("p (j t) -> p j t", j=KT)))
                release(dve, "go0")
                order(tt(qkvt[:, 0:4, P:SEQ], qkvt[:, 0:4, P:SEQ], erow[:], ALU.mult))
                tell("gqd")
                o = flat("gks")
                for h in range(H):
                    r = vb[:, h * DV:(h + 1) * DV]
                    order(stt(r, o[:, h * DV:(h + 1) * DV], ex[:, 12 + h:13 + h], vn[:, 1, h * DV:(h + 1) * DV], ALU.mult, ALU.add))
                    order(ts_(r, r, gb[:, 1, 4 + h:5 + h], None, ALU.mult))
                release(dve, "gks")
                tell("gvb1")
                order(cp(vnew[:], flat("gv1")))
                release(dve, "gv1")
                tell("gvn1d")
                order(cp(qkvt[:, 8:16, P:SEQ], flat("go1").rearrange("p (j t) -> p j t", j=KT)))
                release(dve, "go1")
                o = flat("gS1")
                for h in range(H):
                    r = stg[:, h * DV:(h + 1) * DV]
                    order(stt(r, r, ex[:, 20 + h:21 + h], o[:, h * DV:(h + 1) * DV], ALU.mult, ALU.add))
                release(dve, "gS1")
                tell("gS_out")
                o = flat("gkS")
                for h in range(H):
                    order(ts_(ks[:, h * P:(h + 1) * P], o[0:NS, h * P:(h + 1) * P], gb[0:NS, 2, 4 + h:5 + h], None, ALU.mult))
                release(dve, "gkS")
                order(cp(vs[:], flat("gvS")[0:NS, :]))
                release(dve, "gvS")
                mask_queries(qkvt[:, 0:4, SEQ:T])
                order(stt(kneg[:], qkvt[:, 4:8, SEQ:T], -1.0, egb[:].rearrange("p (h b) -> p h b", b=NS), ALU.mult, ALU.mult))
                tell("gsmp")

                def new_values(b):
                    order(tt(vns[:], flat(f"gr{b}")[0:NS, :], vs[:], ALU.add))
                    release(dve, f"gr{b}")
                    one_row(b)

                new_values(0)
                for b in range(NS):
                    slot = unit_wait(dve, l, 5 * NS + b)
                    update(f"gx{b}", slot, lambda h: egb[:, h * NS + b:h * NS + b + 1])
                    if b + 1 < NS:
                        new_values(b + 1)
                ready("gqsum")
                read_rows(proj[2:4], qout, 6 * NS - 1)
                tell("gqv")
                order(cp(qkvt[:, 8:16, SEQ:T], flat("gqt")[:, 0:KT * NS].rearrange("p (j b) -> p j b", b=NS)))
                release(dve, "gqt")
                tell("gof")
                ready("glr")
                ov = qkvt[:, 8:16, :].rearrange(v4, d=2)
                order(tt(ov, ov, r4[:].unsqueeze(2).broadcast_to([P, H, 2, T]), ALU.mult))
                stream(l, "gz", gated_tile(l, qkvt, gnl))
                tell("o_gdn")
                stream(l, "x1", merge_tile(l, False, True))
                tell("merged")
                order(dve.memset(acc[:], 0.0))
                stream(l, "out", result_tile(l, 3))
                tell("sqp2")
                add_result(2, "x3")
                sum_x(3)
                norm_x(3, 4)
                stream(l, "f2i", hidden_tile(l, False))
                order(dve.memset(acc[:], 0.0))
                stream(l, "f2o", result_tile(l, 5))
                tell("sqp3")
                add_result(3, "x1")
                dve.wait_ge(mv_stored, 16 * (l + 1))
                dve.wait_ge(gdn_stored, 16 * (l + 1))
                passed(dve)
            for t in range(3):
                n = P if t < 2 else NS
                dve.wait_ge(pro_pe, 20 + t)
                order(cp(yout[0:n, t, :], aux[t % 2][0:n].rearrange("p a b -> p (a b)")))
                dve.sem_inc(pro_dve, 1)


def launch_arrays(inputs):
    i = np.arange(P)
    ident = np.eye(P, dtype=np.float32)
    swap = ident[(i + 64) % P]
    tri = (i[:, None] <= i[None, :]).astype(np.float32)
    masks = np.zeros((P, 7, P), np.float32)
    for k in range(7):
        size = 2 << k
        same = i[:, None] // size == i[None, :] // size
        masks[:, k] = same & (i[:, None] % size < size // 2) & (i[None, :] % size >= size // 2)
    f32 = np.float32
    inv = (f32(10000.0) ** (-np.arange(64, dtype=f32) / f32(64))).astype(f32)
    pos = np.concatenate([np.arange(SEQ), np.full(NS, PAST)]).astype(f32)
    ang = (inv[:, None] * pos[None, :]).astype(f32).astype(np.float64)
    cos, sin = np.cos(ang), np.sin(ang)
    cc, ss = np.concatenate([cos, cos]), np.concatenate([-sin, sin])
    scale = DK ** -0.5
    rot = np.stack([cc, ss, cc * scale, ss * scale], 1).astype(f32)
    lg = np.log1p(-np.exp2(-5.0 - np.arange(H)))
    d = np.arange(SEQ)[None, :] - i[:, None]
    dec = np.where(d[:, None, :] >= 0, np.exp(np.maximum(d, 0)[:, None, :] * lg[None, :, None]), 0.0).astype(f32)
    tok = i[:, None, None] + P * np.arange(2)[None, None, :]
    kdec = np.exp((SEQ - 1 - tok) * lg[None, :, None]).reshape(P, 8).astype(f32)
    return {"t_ident": ident, "t_swap": swap, "t_tri": tri, "t_masks": masks, "t_rot": rot, "t_dec": dec, "t_kdec": kdec}


NORMS = ["norm_ffn1_pre", "norm_ffn1_post", "norm_mix_pre", "norm_mix_post", "norm_ffn2_pre", "norm_ffn2_post", "norm_mem"]
OUTS = [(1, SEQ, D), (NS, 1, D), (L, 1, H, DK, DV), (L, 1, H, DK, DV), (L, 1, 3, 16 * P),
        (L, 1, NM, H, DV), (L, 1, NM, H, DV), (L, NS, H, DK, DV), (L, NS, H, DK, DV), (L, NS, 3, 16 * P)]


def program(nc, aps):
    a = aps
    outs = [nc.dram_tensor(f"out_{k}", s, F32, kind="ExternalOutput").ap() for k, s in enumerate(OUTS)]
    build(nc, a["x_prompt"], a["x_sample"], a["mem_prompt"], a["state_ret"], a["state_gdn"], a["state_conv"],
          a["cache_mem_k"], a["cache_mem_v"], [a[n] for n in NORMS], a["w_mem_k"], a["w_mem_v"], a["w_in"],
          a["gdn_conv_w"], a["gdn_a_log"], a["gdn_dt_bias"], a["gdn_norm"],
          [a["w_branch_ret"], a["w_branch_gdn"], a["w_branch_mem"]], a["w_out"],
          [a["ffn1_w_in"], a["ffn2_w_in"]], [a["ffn1_w_out"], a["ffn2_w_out"]],
          [a[n] for n in ("t_ident", "t_swap", "t_tri", "t_masks", "t_rot", "t_dec", "t_kdec")], outs)


def kernel(**inputs):
    import concourse.bacc as bacc
    from concourse.bass_utils import run_bass_kernel_spmd

    nc = bacc.Bacc("TRN2", target_bir_lowering=False, num_devices=1)
    arrays, aps = {}, {}
    for name, a in list(inputs.items()) + list(launch_arrays(inputs).items()):
        arrays[name] = np.ascontiguousarray(a)
        aps[name] = nc.dram_tensor(name, arrays[name].shape, F32, kind="ExternalInput").ap()
    program(nc, aps)
    r = run_bass_kernel_spmd(nc, [arrays], core_ids=[0])
    return tuple(r.results[0][f"out_{k}"] for k in range(len(OUTS)))
```

```python
from contextlib import ExitStack

import numpy as np

import concourse.bass as bass
from concourse import mybir

F32 = mybir.dt.float32
F32R = mybir.dt.float32r
ALU = mybir.AluOpType
ACT = mybir.ActivationFunctionType
AX = mybir.AxisListType

P = 128
L = 2
D = 1024
KT = D // P
SEQ, NS = 256, 8
T = SEQ + NS
FF = 2816
FT = FF // P
H = 4
DK, DV = 128, 256
NM = 256
CW = 4
PAST = 2048
EPS = 1e-6
GW = 2048
HKT = FT // 2

C_RQK, C_RV, C_RG, C_GQ, C_GZ, C_AB, C_MQ, C_GATE = 0, 1024, 2048, 3072, 5120, 6144, 6152, 7176

PHASES = [("mv", 4, 2), ("f1i", 22, 2), ("f1o", 16, 0), ("mk", 4, 2), ("mq", 4, 2),
          ("rqk", 4, 2), ("rv", 4, 2), ("x2", 8, 2), ("gq", 8, 2), ("rg", 4, 2), ("x0", 8, 2), ("gz", 4, 2),
          ("g1", 4, 2), ("b1", 4, 2), ("out", 4, 2), ("f2i", 22, 2), ("f2o", 16, 0)]
GROUPS = sum(p[1] for p in PHASES)
FIRSTS = sum(p[1] for p in PHASES if p[2])


class Phase:
    def __init__(self, name, groups, tiles, c0, m0, base, last):
        self.name, self.groups, self.tiles, self.c0, self.m0, self.base = name, groups, tiles, c0, m0, base
        self.peel = last


def plan():
    found, c, m, uses = {}, 0, 0, [0] * 4
    for k, (name, groups, tiles) in enumerate(PHASES):
        after = PHASES[k + 1][2] if k + 1 < len(PHASES) else None
        found[name] = Phase(name, groups, tiles, c, m, list(uses), 0 if after == tiles else 2)
        c += groups
        if tiles:
            m += groups
            for b in range(4):
                uses[b] += groups // 2 + (1 if groups % 2 and b < 2 else 0)
        else:
            for b in range(2):
                uses[b] += groups // 4
    return found, uses


PLAN, BANK_USES = plan()
STEPS = (["n1", "p1", "n2", "mkt0", "mkt1", "gab"]
         + ["ms0", "ms1", "mpt0", "mpt1", "mo0", "mo1", "mqs"] + [f"qb{b}" for b in range(NS)] + ["smt", "spt", "smo", "smw"]
         + [f"rw{j}" for j in range(4)] + ["rkn", "rvn0", "rvn1", "rs0", "rs1", "rks", "ro0", "ro1", "rst", "rvs"]
         + ["rqs"] + [f"rS{b}" for b in range(NS)] + ["rqt", "rn0", "rn1"]
         + ["gcs", "gcol", "gev", "gct0", "gct1"] + [f"gn{j}" for j in range(4)] + ["gvn0", "gvn1", "gkn"]
         + [x for s in range(2) for x in (f"gbr{s}", f"gG{s}", f"gQ{s}")] + ["gT0", "gT1"]
         + [f"{x}{lv}{s}" for lv in range(6) for x in ("gy", "gt") for s in range(2)]
         + ["gv0", "gS0", "go0", "gks", "gv1", "go1", "gS1", "gkS", "gvS"]
         + ["gqs", "gr0"] + [x for b in range(NS - 1) for x in (f"gx{b}", f"gr{b + 1}") + ((f"gm{b - 1}",) if b in (1, 2) else ())]
         + [f"gx{NS - 1}", "gqt", "gmt"]
         + ["p2", "n3", "p3"])
PAIR, AUX_USES = {}, [0, 0]
pair = 1
for step in STEPS:
    pair = 0 if step in ("rqs", "gqs") else 1 if step[:2] in ("rS", "gr", "gx") or step in ("gm0", "gm1") else 1 - pair
    PAIR[step] = pair, AUX_USES[pair]
    AUX_USES[pair] += 1

NUNIT = 6 * NS
SRING = 3
MILESTONES = ("mem_split x1 sq1 ssq1 rt1 xn1 sqp1 rtp1 x2 sq2 ssq2 rt2 xn2 sqp2 rtp2 x3 sq3 ssq3 rt3 xn3 sqp3 rtp3 "
              "mvn mkt_all mkn1 ab_in ab_neg ab_exp gb_done mqt mmx0 mmx1 mpe0 mpe1 mpr0 mpr1 mpT0 mpT1 mqs sall smx "
              "spe spr sptd sov rqv gqv glr_prompt gates_in gsqt gsmp conv_p "
              "x_half sq_half y_half y_all xh_half xh_all memhi o_mem merged rraw rot rvt rkd rvn rvsd rp0 rp1 rS_out rof rsq rlr o_ret "
              "conv_s gsq gqr gqk tail cso bcd gexp geb dm0 dm1 dme0 dme1 g_at0 g_at1 "
              "gvb gvn0d gsg gvb1 gvn1d gqd gS_out gof g2sq glr o_gdn ").split()


def build(nc, x_prompt, x_sample, mem_prompt, state_ret, state_gdn, state_conv, cache_mem_k, cache_mem_v,
          norms, w_mem_k, w_mem_v, w_in, gdn_conv_w, gdn_a_log, gdn_dt_bias, gdn_norm, branches, w_out,
          ffn_in, ffn_out, tables, outs):
    (y_prompt, y_sample, ret_p, gdn_p, conv_p, mk_p, mv_p, ret_s, gdn_s, conv_s) = outs
    (t_ident, t_swap, t_tri, t_masks, t_rot, t_dec, t_kdec) = tables
    ctx = ExitStack()
    with ctx:
        def sb(name, shape, dt=F32):
            return ctx.enter_context(nc.sbuf_tensor(name, shape, dt))

        def sem(name):
            return ctx.enter_context(nc.semaphore(name))

        x = sb("x", [P, KT, T])
        xh, xl = sb("xh", [P, KT, T], F32R), sb("xl", [P, KT, T], F32R)
        y = sb("y", [P, KT, T])
        raw = sb("raw", [P, 2, GW])
        wh, wl = sb("wh", [P, 2, GW], F32R), sb("wl", [P, 2, GW], F32R)
        mvn = sb("mvn", [P, 2, D])
        memr = sb("memr", [P, KT, NM])
        sring = sb("sring", [P, SRING, D])
        stg = sb("stg", [P, D])
        rot_tab = sb("rot_tab", [P, 4, T])
        dec_tab = sb("dec_tab", [P, H, SEQ])
        kdec_tab = sb("kdec_tab", [P, 2 * H])
        ident, swap, tri, ones = (sb(n, [P, P]) for n in ("ident", "swap", "tri", "ones"))
        masks = sb("masks", [P, 7, P])
        sc = sb("sc", [P, 16, NS, CW])
        tail = sb("tail", [P, 16, 3 + 3 * NS])
        erow = sb("erow", [P, H, P])
        gate = sb("gate", [P, 2, T])
        sqt = sb("sqt", [P, 2, T])
        tmpf = sb("tmpf", [P, T])
        acc, rt = sb("acc", [P, T]), sb("rt", [P, T])
        full = sb("full", [P, 2, SEQ + 3])
        csum = sb("csum", [P, 16, NS])
        gains, gl = sb("gains", [P, KT, 14]), sb("gl", [P, KT, 7])
        convw, cwl = sb("convw", [P, 16, 2 * CW]), sb("cwl", [P, 16, CW])
        gng, gnl = sb("gng", [P, 2, L]), sb("gnl", [P, 2])
        alog, dtb, epst = sb("alog", [P, L, H]), sb("dtb", [P, L, H]), sb("epst", [P, 1])
        wab = sb("wab", [P, KT, 8])
        gb, abt = sb("gb", [P, 3, 8]), sb("abt", [P, 4, 3, H])
        mx, msum = sb("mx", [P, 8]), sb("msum", [P, 8])
        sall, pts = sb("sall", [P, 2, 4 * NS]), sb("pts", [P, KT, NS])
        ps = sb("ps", [32, NM])
        smx = sb("smx", [32, 2])
        bc, ex = sb("bc", [P, 16]), sb("ex", [P, 24])
        egb = sb("egb", [P, H * NS])
        kneg = sb("kneg", [P, H, NS])
        srs = sb("srs", [P, 2])

        ZONE = 62976

        def at(name, offset, shape, dt=F32):
            with ExitStack() as own:
                if offset:
                    own.enter_context(nc.sbuf_tensor(name + "_below", [P, offset // 4], F32))
                return own.enter_context(nc.sbuf_tensor(name, shape, dt))

        hh = at("hh", 0, [P, FT, T], F32R)
        hl = at("hl", FT * T * 4, [P, FT, T], F32R)
        meml = at("meml", 2 * FT * T * 4, [P, KT, NM], F32R)
        memh = at("memh", 54656, [P, KT, NM], F32R)
        r4 = at("r4", 54656, [P, H, T])
        mkt = at("mkt", 25088, [P, KT, NM])
        sqw = at("sqw", 29184, [P, KT, T])
        xnat = at("xnat", 0, [P, 3, D])
        yout = at("yout", 0, [P, 3, D])
        mnat = at("mnat", 12288, [P, 2, D])
        grow = at("grow", 20480, [16, D])
        crow = at("crow", 24576, [8, 16 * P])
        nrow = at("nrow", 32768, [L, DV])
        qkvt = at("qkvt", 0, [P, 16, T])
        mqt = at("mqt", 0, [P, KT, T])
        pt = at("pt", 8448, [P, H, 2, SEQ])
        prob = at("prob", 16896, [P, 8, NM])
        mkn = at("mkn", 16896, [P, 2, D])
        qs = at("qs", 16896, [NS, D])
        junk = at("junk", 20992, [P, 2 * H, 256])
        pmask = at("pmask", 16896, [P, 2 * NS * 4 * NS + 4 * NS])
        sov = at("sov", 20480, [4 * NS, D])
        qmask = at("qmask", 60928, [P, NS * (4 * NS + 1)])
        qout_ret = at("qout_ret", 16896, [NS, D])
        pr = at("pr", 0, [P, H, 384])
        rsq = at("rsq", 29184, [P, KT, T])
        rot = at("rot", 46080, [P, KT, T])
        vn = at("vn", 16896, [P, 2, D])
        kn = at("kn", 25088, [P, 8, P])
        sqg = at("sqg", 46080, [P, KT, T])
        oh = at("oh", 29184, [P, KT, T], F32R)
        ol = at("ol", 37632, [P, KT, T], F32R)
        rvt = at("rvt", 8448, [P, KT, T])
        rout = at("rout", 46080, [P, KT, T])
        ks_ret = at("ks_ret", 58880, [NS, 512])
        mh = at("mh", 0, [P, KT, T], F32R)
        ml = at("ml", KT * T * 4, [P, KT, T], F32R)
        ks = at("ks", 25344, [NS, 512])
        kdb = at("kdb", 58880, [NS, 2, 512])
        qmask_gdn = at("qmask_gdn", 27392, [P, NS * (4 * NS + 1)])
        gzs = at("gzs", 46080, [P, KT, T])
        g1s = at("g1s", 16896, [P, KT, T])
        scr = at("scr", 16896, [3 * NS, 16 * P])
        cso = at("cso", 16896, [3 + 3 * NS, 16 * P])
        MS = 2048
        a_t = [at(f"a_t{s}", 29184 + s * MS, [P, 4, P]) for s in range(2)]
        t_m = [at(f"t_m{s}", 29184 + (2 + s) * MS, [P, 4, P]) for s in range(2)]
        c_t = [at(f"c_t{s}", 29184 + (4 + s) * MS, [P, 4, P]) for s in range(2)]
        y_m = [at(f"y_m{s}", 29184 + (6 + s) * MS, [P, 4, P]) for s in range(2)]
        t_t = [at(f"t_t{s}", 29184 + (8 + s) * MS, [P, 4, P]) for s in range(2)]
        a_q = [at(f"a_q{s}", 29184 + (10 + s) * MS, [P, 4, P]) for s in range(2)]
        vb = at("vb", 29184, [P, D])
        vnew = at("vnew", 29184 + 2 * MS, [P, D])
        kd = at("kd", 29184 + 4 * MS, [P, 2, H, P])
        sb("zone", [P, ZONE // 4])

        vs, vns, qout = mvn[0:NS, 0, :], mvn[0:NS, 1, :], mvn[0:NS, 1, :]
        kdb_ret = mvn[0:NS, 1, :].rearrange("p (a c) -> p a c", a=2)

        proj = [ctx.enter_context(nc.psum_tensor(f"proj{b}", [P, 512], F32)) for b in range(4)]
        aux = [ctx.enter_context(nc.psum_tensor(f"aux{b}", [P, 2, 512], F32)) for b in range(2)]

        raw_loaded = [sem(f"raw_loaded{s}") for s in range(2)]
        up_loaded = [sem(f"up_loaded{s}") for s in range(2)]
        hi_done = [sem(f"hi_done{s}") for s in range(2)]
        split_done = [sem(f"split_done{s}") for s in range(2)]
        group_done = [sem(f"group_done{s}") for s in range(2)]
        first_done = sem("first_done")
        bank_free = [sem(f"bank_free{b}") for b in range(4)]
        gate_ready, gate_used = sem("gate_ready"), [sem(f"gate_used{s}") for s in range(2)]
        sq_ready, sq_used = sem("sq_ready"), [sem(f"sq_used{s}") for s in range(2)]
        conv_ready, conv_used = sem("conv_ready"), [sem(f"conv_used{s}") for s in range(2)]
        aux_full = [sem(f"aux_full{b}") for b in range(2)]
        aux_free = [sem(f"aux_free{b}") for b in range(2)]
        unit_loaded = [sem(f"unit_loaded{s}") for s in range(SRING)]
        unit_used = [sem(f"unit_used{s}") for s in range(SRING)]
        state_new = sem("state_new")
        state_kd = sem("state_kd")
        state_stored, out_stored = sem("state_stored"), sem("out_stored")
        mk_stored, mv_stored, ret_stored, conv_stored = sem("mk_stored"), sem("mv_stored"), sem("ret_stored"), sem("conv_stored")
        gdn_stored = sem("gdn_stored")
        inv_t, inv_y = sem("inv_t"), sem("inv_y")
        wab_loaded, scr_loaded = sem("wab_loaded"), sem("scr_loaded")
        const_loaded = sem("const_loaded")
        pro_mem, pro_pe, pro_dve, pro_act = sem("pro_mem"), sem("pro_pe"), sem("pro_dve"), sem("pro_act")
        hidden = sem("hidden")
        order_act, order_dve, waits_passed = sem("order_act"), sem("order_dve"), sem("waits_passed")
        M = {n: sem(n) for n in MILESTONES}
        block = ctx.enter_context(nc.Block())
        NBANK = BANK_USES
        HALF = GROUPS // 2

        class Order:

            def __init__(self, e, own):
                self.e, self.own, self.n = e, own, 0

            def fresh(self):
                self.e.sem_clear(self.own)
                self.n = 0

            def __call__(self, ins):
                self.n += 1
                ins.then_inc(self.own, 1)
                self.e.wait_ge(self.own, self.n)

            def apart(self, ins):
                self.n += 1
                ins.then_inc(self.own, 1)

            def wait(self):
                self.e.wait_ge(self.own, self.n)

        def each_group(e, l, name, body, after=None, groups=None):
            ph = PLAN[name]
            if after or groups:
                for g in groups or range(ph.groups):
                    body(ph, g // 4, g % 4)
                    if after:
                        after(g)
                return
            whole = (ph.groups - ph.peel) // 4
            if whole > 1:
                with e.Fori(0, whole) as i:
                    for u in range(4):
                        body(ph, i, u)
            else:
                whole = 0
            for g in range(4 * whole, ph.groups):
                body(ph, g // 4, g % 4)

        def passed(e):
            e.sem_inc(waits_passed, 1)

        def norm_wait(e, l, name, n):
            e.wait_ge(M[name], l * 3 + n)

        def start_at_one(e, sems):
            for s in sems:
                e.sem_inc(s, 1)

        def use(l, ph, i, u):
            return l * HALF + ph.c0 // 2 + 2 * i + u // 2

        def bank_use(l, ph, i, u, b):
            k = 2 * i + u // 2 if ph.tiles else i
            return l * NBANK[b] + ph.base[b] + k

        def step_of(name):
            return PAIR[name]

        def take(e, l, name):
            b, k = step_of(name)
            e.wait_ge(aux_full[b], l * AUX_USES[b] + k + 1)
            return aux[b]

        def release(e, name):
            e.sem_inc(aux_free[step_of(name)[0]], 1)

        def unit_wait(e, l, n):
            e.wait_ge(unit_loaded[n % SRING], 16 * (l * (NUNIT // SRING) + n // SRING + 1))
            return n % SRING

        @block.sync
        def _(sp):
            start_at_one(sp, split_done)
            for dst, src in [
                    (xnat[:, 0:2, :], x_prompt[0].rearrange("(t p) d -> p t d", p=P)),
                    (xnat[0:NS, 2, :], x_sample.rearrange("b s d -> (b s) d")),
                    (mnat[:], mem_prompt[0].rearrange("(t p) d -> p t d", p=P)),
                    (crow[:], gdn_conv_w.rearrange("l j c -> (l j) c")), (nrow[:], gdn_norm),
                    (ident[:], t_ident), (swap[:], t_swap), (tri[:], t_tri), (masks[:], t_masks),
                    (rot_tab[:], t_rot), (dec_tab[:], t_dec), (kdec_tab[:], t_kdec),
                    (alog[:], gdn_a_log.rearrange("l h -> (l h)").partition_broadcast(P).rearrange("p (l h) -> p l h", l=L)),
                    (dtb[:], gdn_dt_bias.rearrange("l h -> (l h)").partition_broadcast(P).rearrange("p (l h) -> p l h", l=L)),
            ] + [(grow[2 * k:2 * k + 2, :], n) for k, n in enumerate(norms)]:
                sp.dma_start(dst, src).then_inc(const_loaded, 16)

            def weight(l, name, i, u):
                def cols(w, off, width=256):
                    return w[l].rearrange("(k p) n -> p k n", p=P)[:, :, bass.ds(off, width)]
                g = 4 * i + u
                if name == "mv":
                    return [cols(w_mem_v, g * 256)]
                if name == "mk":
                    return [cols(w_mem_k, g * 256)]
                if name in ("f1i", "f2i"):
                    w = ffn_in[int(name[1]) - 1]
                    return [cols(w, g * P, P), cols(w, g * P + FF, P)]
                if name in ("f1o", "f2o"):
                    w = ffn_out[int(name[1]) - 1]
                    half = u % 2
                    return [w[l, half * HKT * P:(half + 1) * HKT * P].rearrange("(k p) n -> p k n", p=P)[
                        :, :, bass.ds((2 * i + u // 2) * P, P)]]
                if name in ("x0", "x2"):
                    b, off = int(name[1]), (2 * i + u // 2) * 256
                    return [cols(branches[b], off) if u % 2 else cols(w_in, off + C_GATE + b * D)]
                if name == "g1":
                    return [cols(w_in, g * 256 + C_GATE + D)]
                if name == "b1":
                    return [cols(branches[1], g * 256)]
                if name == "out":
                    return [cols(w_out, g * 256)]
                start = {"mq": C_MQ, "rqk": C_RQK, "rv": C_RV, "rg": C_RG, "gq": C_GQ, "gz": C_GZ}[name]
                return [cols(w_in, g * 256 + start)]

            def load(l, layer, name, ph, i, u, before=0):
                s = u % 2
                parts = weight(layer, name, i, u)
                sp.wait_ge(split_done[s], use(l, ph, i, u) + before + 1)
                passed(sp)
                k, n = parts[0].shape[1], parts[0].shape[2]
                if len(parts) == 2:
                    dst = raw[:, s, :].rearrange("p (k two n) -> p k two n", k=k, two=2)
                    sp.dma_start(dst[:, :, 0, :], parts[0]).then_inc(raw_loaded[s], 16)
                    sp.dma_start(dst[:, :, 1, :], parts[1]).then_inc(up_loaded[s], 16)
                else:
                    dst = raw[:, s, 0:k * n].rearrange("p (k n) -> p k n", k=k)
                    sp.dma_start(dst, parts[0]).then_inc(raw_loaded[s], 16)

            first = PLAN["mv"]
            for g in range(2):
                load(0, 0, "mv", first, 0, g)
            with sp.Fori(0, L) as l:
                for g in range(2, first.groups):
                    load(l, l, "mv", first, 0, g)
                for name, _, _ in PHASES[1:]:
                    each_group(sp, l, name, lambda ph, i, u, name=name: load(l, l, name, ph, i, u))
                for g in range(2):
                    load(l, (l + 1) % L, "mv", first, 0, g, HALF)

            for t in range(2):
                sp.wait_ge(pro_dve, 20 + t)
                sp.dma_start(y_prompt[0, t * P:(t + 1) * P], yout[:, t, :]).then_inc(out_stored, 16)
            sp.wait_ge(pro_dve, 22)
            sp.dma_start(y_sample.rearrange("b s d -> (b s) d"), yout[0:NS, 2, :]).then_inc(out_stored, 16)
            sp.wait_ge(out_stored, 16 * 3)

        @block.gpsimd
        def _(pool):
            start_at_one(pool, unit_used)
            def unit(l, n):
                s, k = n % SRING, n // SRING
                pool.wait_ge(unit_used[s], l * (NUNIT // SRING) + k + 1)
                if n - SRING >= 4 * NS:
                    pool.wait_ge(state_stored, (l * 2 * NS + (n - SRING - 4 * NS + 1)) * 16)
                if n < 4 * NS:
                    cache = cache_mem_k if n < 2 * NS else cache_mem_v
                    b, half = n % (2 * NS) // 2, n % 2
                    src = cache[l, b, half * P:(half + 1) * P].rearrange("m h d -> m (h d)")
                    dst = sring[:, s, :]
                else:
                    st = state_ret if n < 5 * NS else state_gdn
                    src = st[l, n % NS].rearrange("h k v -> k h v")
                    dst = sring[:, s, :].rearrange("p (h v) -> p h v", h=H)
                passed(pool)
                pool.dma_start(dst, src).then_inc(unit_loaded[s], 16)

            def store_state(l, n, to):
                pool.wait_ge(state_new, l * 2 * NS + (n - 4 * NS + 1))
                passed(pool)
                pool.dma_start(to[l, n % NS].rearrange("h k v -> k h v"),
                               sring[:, n % SRING, :].rearrange("p (h v) -> p h v", h=H)).then_inc(state_stored, 16)

            with pool.Fori(0, L) as l:
                passed(pool)
                pool.dma_start(wab[:], w_in[l].rearrange("(k p) n -> p k n", p=P)[:, :, C_AB:C_AB + 8]).then_inc(wab_loaded, 16)
                for n in range(SRING):
                    unit(l, n)
                pool.wait_ge(M["mvn"], l + 1)
                passed(pool)
                pool.dma_start(mv_p[l, 0].rearrange("(t p) h d -> p t (h d)", p=P), mvn[:]).then_inc(mv_stored, 16)
                pool.wait_ge(M["mkn1"], l + 1)
                passed(pool)
                pool.dma_start(mk_p[l, 0].rearrange("(t p) h d -> p t (h d)", p=P), mkn[:]).then_inc(mk_stored, 16)
                for n in range(SRING, 4 * NS + SRING):
                    unit(l, n)
                pool.wait_ge(M["rS_out"], l + 1)
                passed(pool)
                pool.dma_start(ret_p[l, 0].rearrange("h k v -> k h v"), stg[:].rearrange("p (h v) -> p h v", h=H)).then_inc(ret_stored, 16)
                for b in range(NS):
                    store_state(l, 4 * NS + b, ret_s)
                    unit(l, 4 * NS + b + SRING)
                pool.wait_ge(M["rof"], l + 1)
                passed(pool)
                pool.dma_start(scr[:], state_conv[l].rearrange("b j c -> (b j) c")).then_inc(scr_loaded, 16)
                pool.wait_ge(M["cso"], l + 1)
                passed(pool)
                pool.dma_start(conv_p[l, 0], cso[0:3, :]).then_inc(conv_stored, 16)
                passed(pool)
                pool.dma_start(conv_s[l].rearrange("b j c -> (b j) c"), cso[3:3 + 3 * NS, :]).then_inc(conv_stored, 16)
                pool.wait_ge(M["gS_out"], l + 1)
                passed(pool)
                pool.dma_start(gdn_p[l, 0].rearrange("h k v -> k h v"), stg[:].rearrange("p (h v) -> p h v", h=H)).then_inc(gdn_stored, 16)
                for b in range(NS):
                    store_state(l, 5 * NS + b, gdn_s)
                    if 5 * NS + b + SRING < NUNIT:
                        unit(l, 5 * NS + b + SRING)
                for s, n in ((mk_stored, 1), (mv_stored, 1), (ret_stored, 1), (gdn_stored, 1), (conv_stored, 2), (state_stored, 2 * NS)):
                    pool.wait_ge(s, (l + 1) * (16 * n))
                pool.wait_ge(M["ab_in"], l + 1)

        @block.tensor
        def _(pe):
            start_at_one(pe, aux_free + bank_free + group_done)
            pe.wait_ge(const_loaded, 16 * 21)
            for k in range(KT):
                if k >= 4:
                    pe.wait_ge(pro_dve, k - 3)
                for t in range(2):
                    pe.transpose(proj[k % 4][:, t * P:(t + 1) * P], xnat[:, t, k * P:(k + 1) * P], ident[:])
                pe.transpose(proj[k % 4][:, SEQ:T], xnat[0:NS, 2, k * P:(k + 1) * P], ident[0:NS, 0:NS]).then_inc(pro_pe, 1)
            pe.wait_ge(pro_mem, 1)
            for k in range(KT):
                pe.wait_ge(pro_dve, k + 5)
                for t in range(2):
                    mm = pe.transpose(proj[k % 4][:, t * P:(t + 1) * P], mnat[:, t, k * P:(k + 1) * P], ident[:])
                mm.then_inc(pro_pe, 1)
            pe.wait_ge(pro_dve, 13)
            for k in range(KT):
                mm = pe.transpose(proj[0][:, k * 16:k * 16 + 14], grow[0:14, k * P:(k + 1) * P], ident[0:14, 0:14])
            mm.then_inc(pro_pe, 1)
            pe.wait_ge(pro_dve, 14)
            for j in range(16):
                mm = pe.transpose(proj[1][:, j * 8:(j + 1) * 8], crow[:, j * P:(j + 1) * P], ident[0:8, 0:8])
            mm.then_inc(pro_pe, 1)
            pe.wait_ge(pro_dve, 15)
            for j in range(2):
                mm = pe.transpose(proj[2][:, j * 2:(j + 1) * 2], nrow[:, j * P:(j + 1) * P], ident[0:L, 0:L])
            mm.then_inc(pro_pe, 1)
            pe.wait_ge(pro_dve, 19)

            def begin(l, name):
                b, k = step_of(name)
                pe.wait_ge(aux_free[b], l * AUX_USES[b] + k + 1)
                return aux[b]

            def end(mm, name):
                mm.then_inc(aux_full[step_of(name)[0]], 1)

            def products(l, name, high, low, kind="", after=None, branch=None, groups=None):
                def group(ph, i, u):
                    s = u % 2
                    n = use(l, ph, i, u)
                    if branch and u % 2:
                        pe.wait_ge(M[branch], l + 1)
                    pe.wait_ge(split_done[s], n + 2)
                    if ph.tiles:
                        for t in range(2):
                            bank = 2 * s + t
                            pe.wait_ge(bank_free[bank], bank_use(l, ph, i, u, bank) + 1)
                            for k in range(KT):
                                if kind == "natural":
                                    o = proj[bank][:, 0:256]
                                    a, b_ = (m[:, k, t * P:(t + 1) * P] for m in (high, low))
                                    c, d = (m[:, s, k * 256:(k + 1) * 256] for m in (wh, wl))
                                else:
                                    hi_, lo_ = (low if isinstance(low, tuple) and u % 2 else high) if kind == "mix" else (high, low)
                                    a, b_ = (m[:, s, k * 256 + t * P:k * 256 + (t + 1) * P] for m in (wh, wl))
                                    c, d = hi_[:, k, :], lo_[:, k, :]
                                    o = proj[bank][:, 0:hi_.shape[2]]
                                pe.matmul(o, a, c, start=(k == 0), stop=False)
                                pe.matmul(o, a, d, start=False, stop=False)
                                mm = pe.matmul(o, b_, c, start=False, stop=(k == KT - 1))
                            mm.then_inc(group_done[s] if t else first_done, 1)
                    else:
                        bank = u // 2
                        o = proj[bank][:, 0:T]
                        if u % 2 == 0:
                            pe.wait_ge(bank_free[bank], bank_use(l, ph, i, u, bank) + 1)
                        for k in range(HKT):
                            kk = k + HKT * (u % 2)
                            a, b_ = (m[:, s, k * P:(k + 1) * P] for m in (wh, wl))
                            pe.matmul(o, a, high[:, kk, :], start=(kk == 0), stop=False)
                            pe.matmul(o, a, low[:, kk, :], start=False, stop=False)
                            mm = pe.matmul(o, b_, high[:, kk, :], start=False, stop=(kk == FT - 1))
                        mm.then_inc(group_done[s], 1)
                passed(pe)
                each_group(pe, l, name, group, after, groups)

            def total(l, name, ready):
                pe.wait_ge(M[ready], l + 1)
                o = begin(l, name)
                end(pe.matmul(o[:, 0, 0:T], ones[:], acc[:], start=True, stop=True), name)

            def turn(l, name, tiles):
                o = begin(l, name)
                if tiles[0][1].shape[0] <= 32:
                    passed(pe)
                for col, src in tiles:
                    n = src.shape[0]
                    mm = pe.transpose(o[0:src.shape[1], col // 512, col % 512:col % 512 + n], src, ident[0:n, 0:n])
                end(mm, name)

            with pe.Fori(0, L) as l:
                def ready(name):
                    pe.wait_ge(M[name], l + 1)

                ready("mem_split")
                products(l, "mv", memh, meml, "natural", groups=(0, 1, 2))
                total(l, "n1", "ssq1")
                products(l, "mv", memh, meml, "natural", groups=(3,))
                ready("xn1")
                products(l, "f1i", xh, xl)
                pe.wait_ge(hidden, l * 2 * FT + FT)
                products(l, "f1o", hh, hl)
                total(l, "p1", "sqp1")
                products(l, "mk", memh, meml, groups=(0, 1, 2))
                total(l, "n2", "ssq2")
                products(l, "mk", memh, meml, groups=(3,))
                ready("xn2")

                def keys_and_decays(g):
                    if g < 2:
                        if g == 0:
                            ready("mkt_all")
                        turn(l, f"mkt{g}", [(j * P, mkt[:, j, g * P:(g + 1) * P]) for j in range(KT)])
                    elif g == 2:
                        pe.wait_ge(wab_loaded, 16 * (l + 1))
                        o = begin(l, "gab")
                        for t in range(3):
                            n = P if t < 2 else NS
                            for k in range(KT):
                                mm = pe.matmul(o[0:n, 0, t * 8:t * 8 + 8], y[:, k, t * P:t * P + n], wab[:, k, :],
                                               start=(k == 0), stop=(k == KT - 1))
                        end(mm, "gab")

                products(l, "mq", xh, xl, after=keys_and_decays)
                ready("mqt")
                for s in range(2):
                    o = begin(l, f"ms{s}")
                    for hd in range(2):
                        for t in range(2):
                            for d in range(2):
                                j = 2 * (2 * s + hd) + d
                                mm = pe.matmul(o[:, hd, t * 256:(t + 1) * 256], mqt[:, j, t * P:(t + 1) * P], mkt[:, j, :],
                                               start=(d == 0), stop=(d == 1))
                    end(mm, f"ms{s}")

                def attend(g):
                    if g == 1:
                        for s in range(2):
                            ready(f"mpr{s}")
                            turn(l, f"mpt{s}", [(hd * 512 + m * 256 + t * P, prob[:, 4 * s + 2 * hd + t, m * P:(m + 1) * P])
                                                for hd in range(2) for m in range(2) for t in range(2)])
                    elif g == 2:
                        for s in range(2):
                            ready(f"mpT{s}")
                            o = begin(l, f"mo{s}")
                            for hd in range(2):
                                h = 2 * s + hd
                                for dt in range(2):
                                    for m in range(2):
                                        mm = pe.matmul(o[:, hd, dt * 256:(dt + 1) * 256], mvn[:, m, h * 256 + dt * P:h * 256 + (dt + 1) * P],
                                                       pt[:, h, m, :], start=(m == 0), stop=(m == 1))
                            end(mm, f"mo{s}")
                    elif g == 3:
                        turn(l, "mqs", [(j * P, mqt[:, j, SEQ:T]) for j in range(KT)])
                products(l, "rqk", xh, xl, after=attend)

                def spread(b):
                    o = begin(l, f"qb{b}")
                    for z in range(2):
                        mm = pe.matmul(o[:, z, :], ident[0:NS, b:b + 1].broadcast_to([NS, P]), qs[:, z * 512:(z + 1) * 512],
                                       start=True, stop=True)
                    end(mm, f"qb{b}")

                def spread_two(g):
                    if g == 0:
                        ready("mqs")
                    spread(2 * g)
                    spread(2 * g + 1)
                products(l, "rv", xh, xl, after=spread_two)
                ready("sall")
                turn(l, "smt", [(m * P, sall[:, m, :]) for m in range(2)])
                ready("spr")
                turn(l, "spt", [(m * 32, ps[:, m * P:(m + 1) * P]) for m in range(2)])
                ready("sptd")
                o = begin(l, "smo")
                for b in range(NS):
                    for m in range(2):
                        slot = unit_wait(pe, l, 2 * NS + 2 * b + m)
                        lhs = pmask[:, (m * NS + b) * 4 * NS:(m * NS + b + 1) * 4 * NS]
                        for z in range(2):
                            mm = pe.matmul(o[0:4 * NS, z, :], lhs, sring[:, slot, z * 512:(z + 1) * 512],
                                           start=((b, m) == (0, 0)), stop=((b, m) == (NS - 1, 1)))
                        if (b, m) != (NS - 1, 1):
                            mm.then_inc(unit_used[slot], 1)
                end(mm, "smo")
                ready("sov")
                turn(l, "smw", [(j * 4 * NS, sov[:, j * P:(j + 1) * P]) for j in range(KT)])

                def retention(g):
                    if g < 4:
                        if g == 0:
                            ready("rraw")
                        o = begin(l, f"rw{g}")
                        for t in range(2):
                            mm = pe.matmul(o[:, t, 0:T], swap[:], rot[:, 2 * g + t, :], start=True, stop=True)
                        end(mm, f"rw{g}")
                    elif g == 4:
                        ready("rot")
                        turn(l, "rkn", [((2 * h + t) * P, rot[:, 4 + h, t * P:(t + 1) * P]) for h in range(H) for t in range(2)])
                        ready("rvt")
                        turn(l, "rvn0", [(j * P, rvt[:, j, 0:P]) for j in range(KT)])
                    elif g == 5:
                        turn(l, "rvn1", [(j * P, rvt[:, j, P:SEQ]) for j in range(KT)])
                        scores(0)
                    elif g == 6:
                        scores(1)
                        turn(l, "rks", [(h * P, rot[:, 4 + h, SEQ:T]) for h in range(H)])
                    else:
                        ready("rvn")
                        for s in range(2):
                            ready(f"rp{s}")
                            o = begin(l, f"ro{s}")
                            for hd in range(2):
                                h = 2 * s + hd
                                for dt in range(2):
                                    c = h * DV + dt * P
                                    pe.matmul(o[:, hd, dt * 256:(dt + 1) * 256], vn[:, 0, c:c + P], pr[:, h, 0:256],
                                              start=True, stop=False)
                                    mm = pe.matmul(o[:, hd, dt * 256 + P:(dt + 1) * 256], vn[:, 1, c:c + P], pr[:, h, 256:384],
                                                   start=False, stop=True)
                            end(mm, f"ro{s}")
                        ready("rkd")
                        o = begin(l, "rst")
                        for h in range(H):
                            for t in range(2):
                                mm = pe.matmul(o[:, h // 2, (h % 2) * DV:(h % 2 + 1) * DV], kn[:, 2 * h + t, :],
                                               vn[:, t, h * DV:(h + 1) * DV], start=(t == 0), stop=(t == 1))
                        end(mm, "rst")
                        turn(l, "rvs", [(j * P, rvt[:, j, SEQ:T]) for j in range(KT)])

                def scores(s):
                    o = begin(l, f"rs{s}")
                    for hd in range(2):
                        h = 2 * s + hd
                        pe.matmul(o[:, hd, 0:256], rot[:, 4 + h, 0:P], rot[:, h, 0:SEQ], start=True, stop=True)
                        mm = pe.matmul(o[:, hd, 256:384], rot[:, 4 + h, P:SEQ], rot[:, h, P:SEQ], start=True, stop=True)
                    end(mm, f"rs{s}")
                products(l, "x2", (xh, xl), (oh, ol), "mix", branch="o_mem", after=retention)

                def outer(name, b, n, keys, values):
                    pe.wait_ge(state_kd, l * 2 * NS + n)
                    o = begin(l, name)
                    for h in range(H):
                        mm = pe.matmul(o[:, h // 2, (h % 2) * DV:(h % 2 + 1) * DV], keys[:, b % 2, h * P:(h + 1) * P],
                                       values[:, h * DV:(h + 1) * DV], start=True, stop=True)
                    end(mm, name)

                def read_state(b, n, slot, queries, banks, done):
                    pe.wait_ge(state_new, l * 2 * NS + n)
                    for h in range(H):
                        mm = pe.matmul(banks[h // 2][0:NS, (h % 2) * DV:(h % 2 + 1) * DV], queries[:, (b * H + h) * NS:(b * H + h + 1) * NS],
                                       sring[:, slot, h * DV:(h + 1) * DV], start=(b == 0 and h % 2 == 0), stop=(b == NS - 1 and h % 2 == 1))
                    mm.then_inc(unit_used[slot] if b + 1 < NS else done, 1)

                sums = aux[PAIR["rqs"][0]]

                def retain(b):
                    read_state(b, b + 1, (4 * NS + b) % SRING, qmask, [sums[:, 0], sums[:, 1]], aux_full[PAIR["rqs"][0]])

                def update_states(g):
                    if g:
                        retain(g - 1)
                    else:
                        ready("rvsd")
                        begin(l, "rqs")
                    outer(f"rS{g}", g, g + 1, kdb_ret, vs)
                products(l, "gq", xh, xl, after=update_states)
                retain(NS - 1)
                def finish_retention(g):
                    if g == 0:
                        ready("rqv")
                        turn(l, "rqt", [(j * NS, qout_ret[:, j * P:(j + 1) * P]) for j in range(KT)])
                    elif g == 1:
                        ready("rsq")
                        for s in range(2):
                            o = begin(l, f"rn{s}")
                            for hd in range(2):
                                for dt in range(2):
                                    mm = pe.matmul(o[:, hd, 0:T], ones[:], rsq[:, 4 * s + 2 * hd + dt, :], start=(dt == 0), stop=(dt == 1))
                            end(mm, f"rn{s}")
                products(l, "rg", xh, xl, after=finish_retention)
                pe.wait_ge(scr_loaded, 16 * (l + 1))
                turn(l, "gcs", [(j * 24, scr[:, j * P:(j + 1) * P]) for j in range(16)])

                def prepare_delta(g):
                    if g == 0:
                        ready("gb_done")
                        o = begin(l, "gcol")
                        for c in range(2):
                            pe.matmul(o[:, 0, c * 4:c * 4 + 4], tri[:], gb[:, c, 0:4], start=True, stop=True)
                            mm = pe.matmul(o[:, 0, 8 + c * 4:12 + c * 4], ones[:], gb[:, c, 0:4], start=True, stop=True)
                        end(mm, "gcol")
                        o = begin(l, "gev")
                        for h in range(H):
                            mm = pe.matmul(o[:, 0, h * NS:(h + 1) * NS], gb[0:NS, 2, h:h + 1].broadcast_to([NS, P]), ident[0:NS, 0:NS],
                                           start=True, stop=True)
                        end(mm, "gev")
                    elif g == 1:
                        ready("tail")
                        for z in range(2):
                            turn(l, f"gct{z}", [(j * P, tail[:, 8 * z + j, :]) for j in range(8)])
                    elif g in (2, 3):
                        ready("gsq")
                        for j in (2 * g - 4, 2 * g - 3):
                            o = begin(l, f"gn{j}")
                            for t in range(2):
                                mm = pe.matmul(o[:, t, 0:T], ones[:], sqg[:, 2 * j + t, :], start=True, stop=True)
                            end(mm, f"gn{j}")
                    elif g in (4, 5):
                        turn(l, f"gvn{g - 4}", [(j * P, qkvt[:, 8 + j, (g - 4) * P:(g - 3) * P]) for j in range(KT)])
                    elif g == 6:
                        ready("gqk")
                        turn(l, "gkn", [((2 * h + t) * P, qkvt[:, 4 + h, t * P:(t + 1) * P]) for h in range(H) for t in range(2)])
                products(l, "x0", (xh, xl), (oh, ol), "mix", branch="o_ret", after=prepare_delta)

                for s in range(2):
                    mats = [(q, 2 * s + q // 2, q % 2) for q in range(4)]
                    o = begin(l, f"gbr{s}")
                    for q, h, c in mats:
                        pe.matmul(o[:, 0, q * P:(q + 1) * P], gb[:, c, h:h + 1].broadcast_to([P, P]), tri[:], start=True, stop=True)
                    for q, h, c in mats:
                        mm = pe.matmul(o[:, 1, q * P:(q + 1) * P], gb[:, c, 4 + h:5 + h].broadcast_to([P, P]), ident[:],
                                       start=True, stop=True)
                    end(mm, f"gbr{s}")
                    for step, other in (("gG", 4), ("gQ", 0)):
                        o = begin(l, f"{step}{s}")
                        for q, h, c in mats:
                            mm = pe.matmul(o[:, 0, q * P:(q + 1) * P], qkvt[:, 4 + h, c * P:(c + 1) * P],
                                           qkvt[:, other + h, c * P:(c + 1) * P], start=True, stop=True)
                        end(mm, f"{step}{s}")
                for s in range(2):
                    ready(f"g_at{s}")
                    turn(l, f"gT{s}", [(q * P, t_t[s][:, q, :]) for q in range(4)])
                for lv in range(6):
                    for s in range(2):
                        pe.wait_ge(inv_t, l * 12 + 2 * lv + s + 1)
                        o = begin(l, f"gy{lv}{s}")
                        for q in range(4):
                            mm = pe.matmul(o[:, 0, q * P:(q + 1) * P], c_t[s][:, q, :], t_m[s][:, q, :], start=True, stop=True)
                        end(mm, f"gy{lv}{s}")
                    for s in range(2):
                        pe.wait_ge(inv_y, l * 12 + 2 * lv + s + 1)
                        o = begin(l, f"gt{lv}{s}")
                        for q in range(4):
                            pe.matmul(o[:, 0, q * P:(q + 1) * P], t_t[s][:, q, :], y_m[s][:, q, :], start=True, stop=True)
                        for q in range(4):
                            mm = pe.matmul(o[:, 1, q * P:(q + 1) * P], y_m[s][:, q, :], t_t[s][:, q, :], start=True, stop=True)
                        end(mm, f"gt{lv}{s}")

                def per_head(name, lhs, rhs):
                    o = begin(l, name)
                    for h in range(H):
                        mm = pe.matmul(o[:, h // 2, (h % 2) * DV:(h % 2 + 1) * DV], lhs(h), rhs(h), start=True, stop=True)
                    end(mm, name)

                ready("gvb")
                per_head("gv0", lambda h: t_t[h // 2][:, 2 * (h % 2), :], lambda h: vb[:, h * DV:(h + 1) * DV])
                ready("gvn0d")
                per_head("gS0", lambda h: kd[:, 0, h, :], lambda h: vnew[:, h * DV:(h + 1) * DV])
                o = begin(l, "go0")
                for j in range(KT):
                    h = j // 2
                    mm = pe.matmul(o[:, j // 4, (j % 4) * P:(j % 4 + 1) * P], vnew[:, j * P:(j + 1) * P],
                                   a_q[h // 2][:, 2 * (h % 2), :], start=True, stop=True)
                end(mm, "go0")
                ready("gsg")
                per_head("gks", lambda h: qkvt[:, 4 + h, P:SEQ], lambda h: stg[:, h * DV:(h + 1) * DV])
                ready("gvb1")
                per_head("gv1", lambda h: t_t[h // 2][:, 2 * (h % 2) + 1, :], lambda h: vb[:, h * DV:(h + 1) * DV])
                ready("gvn1d")
                ready("gqd")
                o = begin(l, "go1")
                for j in range(KT):
                    h = j // 2
                    r = o[:, j // 4, (j % 4) * P:(j % 4 + 1) * P]
                    pe.matmul(r, vnew[:, j * P:(j + 1) * P], a_q[h // 2][:, 2 * (h % 2) + 1, :], start=True, stop=False)
                    mm = pe.matmul(r, stg[:, j * P:(j + 1) * P], qkvt[:, h, P:SEQ], start=False, stop=True)
                end(mm, "go1")
                per_head("gS1", lambda h: kd[:, 1, h, :], lambda h: vnew[:, h * DV:(h + 1) * DV])
                turn(l, "gkS", [(h * P, qkvt[:, 4 + h, SEQ:T]) for h in range(H)])
                turn(l, "gvS", [(j * P, qkvt[:, 8 + j, SEQ:T]) for j in range(KT)])
                def read_key(b):
                    slot = unit_wait(pe, l, 5 * NS + b)
                    o = begin(l, f"gr{b}")
                    for h in range(H):
                        mm = pe.matmul(o[0:NS, h // 2, (h % 2) * DV:(h % 2 + 1) * DV], kneg[:, h, :],
                                       sring[:, slot, h * DV:(h + 1) * DV], start=True, stop=True)
                    end(mm, f"gr{b}")

                ready("gsmp")
                read_key(0)
                delta_sums = aux[PAIR["gqs"][0]]

                def update_delta(b):
                    if b == 0:
                        begin(l, "gqs")
                    outer(f"gx{b}", b, NS + b + 1, kdb, vns)
                    if b:
                        query_delta(b - 1)
                    if b + 1 < NS:
                        read_key(b + 1)
                    if b in (1, 2):
                        ready("g2sq")
                        o = begin(l, f"gm{b - 1}")
                        for hd in range(2):
                            for dt in range(2):
                                mm = pe.matmul(o[:, hd, 0:SEQ], ones[:], sqw[:, 4 * (b - 1) + 2 * hd + dt, 0:SEQ],
                                               start=(dt == 0), stop=(dt == 1))
                        end(mm, f"gm{b - 1}")

                def query_delta(b):
                    read_state(b, NS + b + 1, (5 * NS + b) % SRING, qmask_gdn, [delta_sums[:, 0], delta_sums[:, 1]],
                               aux_full[PAIR["gqs"][0]])
                products(l, "gz", xh, xl, after=update_delta)
                products(l, "g1", xh, xl, after=lambda g: update_delta(4 + g))
                query_delta(NS - 1)
                ready("gqv")
                turn(l, "gqt", [(j * NS, qout[:, j * P:(j + 1) * P]) for j in range(KT)])
                ready("gsqt")
                o = begin(l, "gmt")
                for h in range(H):
                    for dt in range(2):
                        mm = pe.matmul(o[:, 0, h * NS:(h + 1) * NS], ones[:], csum[:, 2 * h + dt, :], start=(dt == 0), stop=(dt == 1))
                end(mm, "gmt")
                ready("o_gdn")
                products(l, "b1", oh, ol)

                ready("merged")
                products(l, "out", mh, ml)
                total(l, "p2", "sqp2")
                total(l, "n3", "ssq3")
                ready("xn3")
                products(l, "f2i", xh, xl)
                pe.wait_ge(hidden, l * 2 * FT + 2 * FT)
                products(l, "f2o", hh, hl)
                total(l, "p3", "sqp3")

            for t in range(3):
                n = P if t < 2 else NS
                pe.wait_ge(M["x1"], L + 1)
                if t == 2:
                    pe.wait_ge(pro_dve, 20)
                for k in range(KT):
                    mm = pe.transpose(aux[t % 2][0:n, k // 4, (k % 4) * P:(k % 4 + 1) * P], x[:, k, t * P:t * P + n], ident[:])
                mm.then_inc(pro_pe, 1)

        ACT_TILES = 22 * 2 + 24
        GATE0 = {"f1i": 0, "x2": 22, "rg": 30, "x0": 38, "f2i": 46}
        SQ0 = {"f1o": 0, "out": 8, "f2o": 16}

        def tile_wait(e, l, ph, i, u, t):
            if ph.tiles and t == 0:
                e.wait_ge(first_done, l * FIRSTS + ph.m0 + 4 * i + u + 1)
            else:
                e.wait_ge(group_done[u % 2], use(l, ph, i, u) + 2)
            return 2 * (u % 2) + t if ph.tiles else u // 2

        def two_on(name, ph, i, u):
            k = [p[0] for p in PHASES].index(name)
            n = 2 * i + u // 2 + 1
            if isinstance(i, int) and 4 * i + u >= ph.groups - 2:
                k, n = (k + 1) % len(PHASES), 0
            name = PHASES[k][0]
            up = {"f1i": n, "f2i": 11 + n}.get(name)
            return GW if PHASES[k][2] else HKT * P, up

        @block.scalar
        def _(act):
            order = Order(act, order_act)
            start_at_one(act, gate_used + sq_used + conv_used)
            act.wait_ge(const_loaded, 16 * 21)
            act.wait_ge(pro_act, 1)
            order.fresh()
            for t in range(2):
                order(act.activation(stg[:], mnat[:, t, :], ACT.Square, accum_out=srs[:, t:t + 1]))
            order(act.activation(srs[:], srs[:], ACT.Sqrt, bias=epst[:], scale=1.0 / D))
            act.sem_inc(pro_act, 1)

            def split(l, slot, n, size, up=None):
                act.wait_ge(raw_loaded[slot], 16 * (n + 1))
                if up is not None:
                    act.wait_ge(up_loaded[slot], 16 * (l * 22 + up + 1))
                act.wait_ge(group_done[slot], n + 1)
                act.copy(wh[:, slot, 0:size], raw[:, slot, 0:size]).then_inc(hi_done[slot], 1)

            def stream(l, name, tile=None, after=None, groups=None):
                def body(ph, i, u):
                    if tile:
                        order.fresh()
                        tile(ph, i, u)
                    size, up = two_on(name, ph, i, u)
                    split(l, u % 2, use(l, ph, i, u) + 1, size, up)
                each_group(act, l, name, body, after, groups)

            def through(l, func, every=None):
                def tile(ph, i, u):
                    if every == "gate" and u % 2:
                        return
                    for t in range(1 if every == "first" else 2):
                        if every == "first":
                            n, slot = 2 * i + u // 2, u % 2
                            a = GATE0[ph.name] + 4 * i + u
                        else:
                            g = 4 * i + u if every is None else 2 * i + u // 2
                            n, slot = g, t
                            a = GATE0[ph.name] + 2 * g + t
                        bank = tile_wait(act, l, ph, i, u, t)
                        act.wait_ge(gate_used[slot], l * (ACT_TILES // 2) + GATE0[ph.name] // 2 + n + 1)
                        order(act.activation(gate[:, slot, :], proj[bank][:, 0:T], func))
                        act.sem_inc(bank_free[bank], 1)
                        act.sem_inc(gate_ready, 1)
                return tile

            def copied(l, out, func=ACT.Copy):
                def tile(ph, i, u):
                    for t in range(2):
                        bank = tile_wait(act, l, ph, i, u, t)
                        dst = out(4 * i + u, t)
                        order(act.activation(dst, proj[bank][:, 0:dst.shape[-1]], func))
                        act.sem_inc(bank_free[bank], 1)
                return tile

            def squares(l):
                def tile(ph, i, u):
                    if not ph.tiles and u % 2 == 0:
                        return
                    for t in range(2 if ph.tiles else 1):
                        slot = t if ph.tiles else u // 2
                        n = 4 * i + u if ph.tiles else i
                        bank = tile_wait(act, l, ph, i, u, t)
                        act.wait_ge(sq_used[slot], l * 12 + SQ0[ph.name] // 2 + n + 1)
                        order(act.activation(sqt[:, slot, :], proj[bank][:, 0:T], ACT.Square))
                        act.sem_inc(sq_ready, 1)
                return tile

            def scale_memory(layer):
                for k in range(KT):
                    order.apart(act.activation(y[:, k, 0:NM], memr[:, k, :], ACT.Copy, scale=gains[:, k, bass.ds(layer + 12, 1)]))
                order.wait()
                order(act.copy(memh[:], y[:, :, 0:NM]))
                act.sem_inc(M["memhi"], 1)

            act.wait_ge(pro_dve, 19)
            for s in range(2):
                split(0, s, 0, GW)
            scale_memory(0)
            with act.Fori(0, L) as l:
                def ready(name):
                    act.wait_ge(M[name], l + 1)

                def tell(name):
                    act.sem_inc(M[name], 1)

                def root(name, out):
                    o = take(act, l, name)
                    order(act.activation(rt[:], o[:, 0, 0:T], ACT.Sqrt, bias=epst[:], scale=1.0 / D))
                    release(act, name)
                    tell(out)

                def square_x(n):
                    norm_wait(act, l, "x_half", n)
                    order(act.activation(sqw[:, 0:4, :], x[:, 0:4, :], ACT.Square))
                    tell("sq_half")
                    ready(f"x{n}")
                    order(act.activation(sqw[:, 4:8, :], x[:, 4:8, :], ACT.Square))
                    tell(f"sq{n}")

                def high_parts(n):
                    for c, y_in, out in ((slice(0, 4), "y_half", "xh_half"), (slice(4, 8), "y_all", "xh_all")):
                        norm_wait(act, l, y_in, n)
                        order(act.copy(xh[:, c, :], y[:, c, :]))
                        tell(out)

                order.fresh()
                values = copied(l, lambda g, t: mvn[:, t, g * 256:(g + 1) * 256])
                stream(l, "mv", values, groups=(0,))
                square_x(1)
                stream(l, "mv", values, groups=(1,))
                root("n1", "rt1")
                stream(l, "mv", values, groups=(2,))
                high_parts(1)
                stream(l, "mv", values, groups=(3,))
                tell("mvn")
                stream(l, "f1i", through(l, ACT.Silu, "first"))
                stream(l, "f1o", squares(l))
                order.fresh()
                root("p1", "rtp1")
                keys = copied(l, lambda g, t: mkt[:, 2 * g + t, :])
                stream(l, "mk", keys, groups=(0,))
                square_x(2)
                stream(l, "mk", keys, groups=(1,))
                root("n2", "rt2")
                stream(l, "mk", keys, groups=(2,))
                high_parts(2)
                stream(l, "mk", keys, groups=(3,))
                tell("mkt_all")
                stream(l, "mq")
                for s in range(2):
                    ready(f"mmx{s}")
                    o = take(act, l, f"ms{s}")
                    for q in range(4):
                        order.apart(act.activation(prob[:, 4 * s + q, :], o[:, q // 2, (q % 2) * 256:(q % 2 + 1) * 256], ACT.Exp,
                                             bias=mx[:, 4 * s + q:4 * s + q + 1], scale=DV ** -0.5,
                                             accum_out=msum[:, 4 * s + q:4 * s + q + 1]))
                    order.wait()
                    release(act, f"ms{s}")
                    tell(f"mpe{s}")
                ready("ab_neg")
                order(act.activation(abt[:, 2], abt[:, 1], ACT.Exp))
                order(act.activation(abt[:, 3, 0], alog[:, l], ACT.Exp))
                order(act.activation(abt[:, 2], abt[:, 2], ACT.Ln, bias=ones[:, 0:1]))
                order(act.activation(gb[:, :, 4:8], gb[:, :, 4:8], ACT.Sigmoid))
                tell("ab_exp")
                stream(l, "rqk")
                stream(l, "rv")
                order.fresh()
                ready("smx")
                o = take(act, l, "smt")
                order(act.activation(ps[:], o[0:32, 0, 0:NM], ACT.Exp, bias=smx[:, 0:1], scale=DV ** -0.5, accum_out=smx[:, 1:2]))
                release(act, "smt")
                tell("spe")
                stream(l, "x2", through(l, ACT.Sigmoid, "gate"))

                def conv_input(ph, i, u):
                    for t in range(2):
                        bank = tile_wait(act, l, ph, i, u, t)
                        act.wait_ge(conv_used[t], l * 8 + 4 * i + u + 1)
                        order.apart(act.copy(full[:, t, 3:SEQ + 3], proj[bank][:, 0:SEQ]))
                        order(act.copy(sc[:, 2 * (4 * i + u) + t, :, 3], proj[bank][:, SEQ:T]))
                        act.sem_inc(bank_free[bank], 1)
                        act.sem_inc(conv_ready, 1)
                stream(l, "gq", conv_input)
                order.fresh()

                def inverse_root(src, steps, out, name):
                    for s, st in enumerate(steps):
                        o = take(act, l, st)
                        order(act.activation(out[:, 2 * s:2 * s + 2, :], o[:, :, 0:T], ACT.Ln, bias=epst[:], scale=src))
                        release(act, st)
                    order(act.activation(out[:, 0:2 * len(steps), :], out[:, 0:2 * len(steps), :], ACT.Exp, scale=-0.5))
                    tell(name)

                ready("rof")
                order(act.activation(rsq[:], rout[:], ACT.Square))
                tell("rsq")
                inverse_root(1.0 / DV, ["rn0", "rn1"], r4, "rlr")
                stream(l, "rg", through(l, ACT.Silu))
                ready("conv_p")
                order(act.activation(qkvt[:, :, 0:SEQ], qkvt[:, :, 0:SEQ], ACT.Silu))
                ready("conv_s")
                order(act.activation(qkvt[:, :, SEQ:T], qkvt[:, :, SEQ:T], ACT.Silu))
                ready("o_ret")
                order(act.activation(sqg[:], qkvt[:, 0:8, :], ACT.Square))
                tell("gsq")

                def prepare_delta(g):
                    if g == 0:
                        o = take(act, l, "gev")
                        order(act.activation(egb[:], o[:, 0, 0:H * NS], ACT.Exp))
                        release(act, "gev")
                        tell("geb")
                    elif g == 1:
                        ready("bcd")
                        order(act.activation(ex[:], ex[:], ACT.Exp))
                        tell("gexp")
                    elif g in (2, 3):
                        for j in (2 * g - 4, 2 * g - 3):
                            o = take(act, l, f"gn{j}")
                            order(act.activation(sqg[:, 2 * j:2 * j + 2, :], o[:, :, 0:T], ACT.Ln, bias=epst[:]))
                            release(act, f"gn{j}")
                        if g == 3:
                            order(act.activation(sqg[:], sqg[:], ACT.Exp, scale=-0.5))
                            tell("gqr")
                stream(l, "x0", through(l, ACT.Sigmoid, "gate"), after=prepare_delta)
                order.fresh()
                for s in range(2):
                    o = take(act, l, f"gbr{s}")
                    ready(f"dm{s}")
                    for hd in range(2):
                        q = 2 * hd + 1
                        order.apart(act.activation(erow[:, 2 * s + hd, :], o[:, 0, q * P:(q + 1) * P], ACT.Exp))
                    order(act.activation(y_m[s][:], y_m[s][:], ACT.Exp))
                    release(act, f"gbr{s}")
                    tell(f"dme{s}")
                for lv in range(6):
                    for s in range(2):
                        order(act.copy(y_m[s][:].rearrange("p q m -> p (q m)"), take(act, l, f"gy{lv}{s}")[:, 0, :]))
                        release(act, f"gy{lv}{s}")
                        act.sem_inc(inv_y, 1)
                ready("gS_out")
                order(act.activation(sqw[:, :, 0:SEQ], qkvt[:, 8:16, 0:SEQ], ACT.Square))
                tell("g2sq")

                def prompt_roots(g):
                    if g in (1, 2):
                        s = g - 1
                        o = take(act, l, f"gm{s}")
                        order(act.activation(r4[:, 2 * s:2 * s + 2, 0:SEQ], o[:, :, 0:SEQ], ACT.Ln, bias=epst[:], scale=1.0 / DV))
                        release(act, f"gm{s}")
                    if g == 2:
                        order(act.activation(r4[:, :, 0:SEQ], r4[:, :, 0:SEQ], ACT.Exp, scale=-0.5))
                        tell("glr_prompt")
                stream(l, "gz", copied(l, lambda g, t: gzs[:, 2 * g + t, :], ACT.Silu), after=prompt_roots)
                tell("gates_in")
                stream(l, "g1", copied(l, lambda g, t: g1s[:, 2 * g + t, :], ACT.Sigmoid))
                tell("gates_in")
                ready("gof")
                order(act.activation(csum[:, 0:KT, :], qkvt[:, 8:16, SEQ:T], ACT.Square))
                tell("gsqt")
                o = take(act, l, "gmt")[:, 0, 0:H * NS].rearrange("p (h b) -> p h b", b=NS)
                order(act.activation(r4[:, :, SEQ:T], o, ACT.Ln, bias=epst[:], scale=1.0 / DV))
                release(act, "gmt")
                order(act.activation(r4[:, :, SEQ:T], r4[:, :, SEQ:T], ACT.Exp, scale=-0.5))
                tell("glr")
                stream(l, "b1")
                stream(l, "out", squares(l))
                order.fresh()
                root("p2", "rtp2")
                square_x(3)
                root("n3", "rt3")
                high_parts(3)
                ready("xn3")
                scale_memory((l + 1) % L)
                stream(l, "f2i", through(l, ACT.Silu, "first"))
                stream(l, "f2o", squares(l))
                order.fresh()
                root("p3", "rtp3")

        @block.vector
        def _(dve):
            order = Order(dve, order_dve)
            tt, ts_, stt = dve.tensor_tensor, dve.tensor_scalar, dve.scalar_tensor_tensor
            cp = dve.tensor_copy
            order.fresh()
            order(dve.memset(epst[:], EPS))
            order(dve.memset(ones[:], 1.0))
            order(dve.memset(full[:], 0.0))
            order(dve.memset(gb[:], 0.0))
            dve.sem_inc(pro_act, 1)
            dve.wait_ge(const_loaded, 16 * 21)
            for k in range(KT):
                dve.wait_ge(pro_pe, k + 1)
                order(cp(x[:, k, :], proj[k % 4][:, 0:T]))
                dve.sem_inc(pro_dve, 1)
            dve.wait_ge(pro_act, 2)
            order(dve.reciprocal(srs[:], srs[:]))
            for t in range(2):
                order(ts_(mnat[:, t, :], mnat[:, t, :], srs[:, t:t + 1], None, ALU.mult))
            dve.sem_inc(pro_mem, 1)
            for k in range(KT):
                dve.wait_ge(pro_pe, k + 9)
                order(cp(memr[:, k, :], proj[k % 4][:, 0:NM]))
                dve.sem_inc(pro_dve, 1)
            dve.wait_ge(pro_pe, 17)
            order(cp(gains[:], proj[0][:, 0:KT * 16].rearrange("p (k n) -> p k n", n=16)[:, :, 0:14]))
            dve.sem_inc(pro_dve, 1)
            dve.wait_ge(pro_pe, 18)
            order(cp(convw[:], proj[1][:, 0:P].rearrange("p (j n) -> p j n", n=8)))
            dve.sem_inc(pro_dve, 1)
            dve.wait_ge(pro_pe, 19)
            order(cp(gng[:], proj[2][:, 0:4].rearrange("p (j n) -> p j n", n=2)))
            dve.sem_inc(pro_dve, 1)
            dve.sem_inc(M["x_half"], 1)
            dve.sem_inc(M["x1"], 1)

            def split(l, slot, n, size):
                dve.wait_ge(hi_done[slot], n + 1)
                dve.tensor_sub(wl[:, slot, 0:size], raw[:, slot, 0:size], wh[:, slot, 0:size].bitcast(F32)).then_inc(split_done[slot], 1)

            def stream(l, name, tile=None, after=None, groups=None, first=None):
                def body(ph, i, u):
                    if tile:
                        order.fresh()
                        tile(ph, i, u)
                    if first:
                        first(4 * i + u)
                    size, _ = two_on(name, ph, i, u)
                    split(l, u % 2, use(l, ph, i, u) + 1, size)
                each_group(dve, l, name, body, after, groups)
                order.fresh()

            def parts(high, low, src):
                order(cp(high, src))
                order(tt(low, src, high.bitcast(F32), ALU.subtract))

            def hidden_tile(l, first):
                def tile(ph, i, u):
                    j = 4 * i + u
                    bank = tile_wait(dve, l, ph, i, u, 1)
                    dve.wait_ge(gate_ready, l * ACT_TILES + GATE0[ph.name] + j + 1)
                    order(tt(tmpf[:], proj[bank][:, 0:T], gate[:, u % 2, :], ALU.mult))
                    dve.sem_inc(bank_free[bank], 1)
                    dve.sem_inc(gate_used[u % 2], 1)
                    parts(hh[:, j, :], hl[:, j, :], tmpf[:])
                    dve.sem_inc(hidden, 1)
                return tile

            def result_tile(l, gain, done):
                def tile(ph, i, u):
                    if not ph.tiles and u % 2 == 0:
                        return
                    for t in range(2 if ph.tiles else 1):
                        j = 2 * (4 * i + u) + t if ph.tiles else 2 * i + u // 2
                        slot = t if ph.tiles else u // 2
                        bank = tile_wait(dve, l, ph, i, u, t)
                        dve.wait_ge(sq_ready, l * 24 + SQ0[ph.name] + j + 1)
                        order(ts_(y[:, j, :], proj[bank][:, 0:T], gl[:, j, gain:gain + 1], None, ALU.mult))
                        order(tt(acc[:], acc[:], sqt[:, slot, :], ALU.add))
                        dve.sem_inc(bank_free[bank], 1)
                        dve.sem_inc(sq_used[slot], 1)
                        if isinstance(i, int) and j == KT - 1:
                            dve.sem_inc(M[done], 1)
                return tile

            def copy_tile(l, out):
                def tile(ph, i, u):
                    for t in range(2):
                        bank = tile_wait(dve, l, ph, i, u, t)
                        dst = out(4 * i + u, t)
                        order(cp(dst, proj[bank][:, 0:dst.shape[-1]]))
                        dve.sem_inc(bank_free[bank], 1)
                return tile

            def gated_tile(l, out):
                def tile(ph, i, u):
                    for t in range(2):
                        j = 2 * (4 * i + u) + t
                        dve.wait_ge(gate_ready, l * ACT_TILES + GATE0[ph.name] + j + 1)
                        order(tt(tmpf[:], gate[:, t, :], out[:, j, :], ALU.mult))
                        dve.sem_inc(gate_used[t], 1)
                        parts(oh[:, j, :], ol[:, j, :], tmpf[:])
                return tile

            def merge_tile(l, first):
                def tile(ph, i, u):
                    if u % 2 == 0:
                        return
                    for t in range(2):
                        j = 2 * (2 * i + u // 2) + t
                        bank = tile_wait(dve, l, ph, i, u, t)
                        dve.wait_ge(gate_ready, l * ACT_TILES + GATE0[ph.name] + j + 1)
                        order(tt(y[:, j, :] if first else tmpf[:], proj[bank][:, 0:T], gate[:, t, :], ALU.mult))
                        dve.sem_inc(bank_free[bank], 1)
                        dve.sem_inc(gate_used[t], 1)
                        if not first:
                            order(tt(y[:, j, :], y[:, j, :], tmpf[:], ALU.add))
                return tile

            def split_memory(n):
                dve.wait_ge(M["memhi"], n)
                order(tt(meml[:], y[:, :, 0:NM], memh[:].bitcast(F32), ALU.subtract))
                dve.sem_inc(M["mem_split"], 1)

            order.fresh()
            for s in range(2):
                split(0, s, 0, GW)
            split_memory(1)
            with dve.Fori(0, L) as l:
                def ready(name):
                    dve.wait_ge(M[name], l + 1)

                def tell(name):
                    dve.sem_inc(M[name], 1)

                def flat(name):
                    return take(dve, l, name)[:].rearrange("p a b -> p (a b)")

                order.fresh()
                def mask_queries(qmask, q):
                    order(dve.memset(qmask[:], 0.0))
                    blocks = qmask[:].rearrange("p (b x) -> p b x", x=4 * NS + 1)[:, :, 0:4 * NS]
                    order(cp(blocks.rearrange("p b (h e) -> p b h e", e=NS)[:, :, :, 0], q.rearrange("p h b -> p b h")))

                def read_rows(banks, dst, last):
                    dve.sem_inc(unit_used[last % SRING], 1)
                    for z in range(2):
                        order(cp(dst[:, z * 512:(z + 1) * 512], banks[z][0:NS, :]))

                def sum_x(n):
                    norm_wait(dve, l, "sq_half", n)
                    order(dve.tensor_reduce(acc[:], sqw[:, 0:4, :].rearrange("p k t -> p t k"), AX.X, ALU.add))
                    ready(f"sq{n}")
                    order(dve.tensor_reduce(tmpf[:], sqw[:, 4:8, :].rearrange("p k t -> p t k"), AX.X, ALU.add))
                    order(tt(acc[:], acc[:], tmpf[:], ALU.add))
                    tell(f"ssq{n}")

                def norm_x(n, gain, between=None):
                    ready(f"rt{n}")
                    order(dve.reciprocal(rt[:], rt[:]))
                    for k in range(KT):
                        order.apart(stt(y[:, k, :], x[:, k, :], gl[:, k, gain:gain + 1], rt[:], ALU.mult, ALU.mult))
                        if k == 3:
                            order.wait()
                            tell("y_half")
                    order.wait()
                    tell("y_all")
                    if between:
                        between()
                    for c, name in ((slice(0, 4), "xh_half"), (slice(4, 8), "xh_all")):
                        norm_wait(dve, l, name, n)
                        order(tt(xl[:, c, :], y[:, c, :], xh[:, c, :].bitcast(F32), ALU.subtract))
                    tell(f"xn{n}")

                def add_result(n, nxt):
                    ready(f"rtp{n}")
                    order(dve.reciprocal(rt[:], rt[:]))
                    for c in (slice(0, 4), slice(4, 8)):
                        order(tt(y[:, c, :], y[:, c, :], rt[:].unsqueeze(1).broadcast_to([P, 4, T]), ALU.mult))
                        order(tt(x[:, c, :], x[:, c, :], y[:, c, :], ALU.add))
                        tell("x_half" if c.start == 0 else nxt)

                stream(l, "mv", groups=(0,))
                sum_x(1)
                g2 = gains[:].rearrange("p k (a l) -> p k a l", l=L)
                order(cp(gl[:], g2[:, :, :, l]))
                for a in (1, 5):
                    order(ts_(gl[:, :, a:a + 1], gl[:, :, a:a + 1], 0.5, None, ALU.mult))
                order(cp(cwl[:], convw[:].rearrange("p j (l k) -> p j l k", l=L)[:, :, l, :]))
                order(cp(gnl[:], gng[:, :, l]))

                stream(l, "mv", groups=(1,))
                norm_x(1, 0, lambda: stream(l, "mv", groups=(2,)))
                stream(l, "mv", groups=(3,))
                stream(l, "f1i", hidden_tile(l, True))
                order(dve.memset(acc[:], 0.0))
                stream(l, "f1o", result_tile(l, 1, "sqp1"))
                add_result(1, "x2")
                stream(l, "mk", groups=(0,))
                sum_x(2)
                stream(l, "mk", groups=(1,))
                norm_x(2, 2, lambda: stream(l, "mk", groups=(2,)))
                stream(l, "mk", groups=(3,))
                def keys_and_decays(g):
                    if g < 2:
                        order(cp(mkn[:, g, :], flat(f"mkt{g}")))
                        release(dve, f"mkt{g}")
                        if g == 1:
                            tell("mkn1")
                    elif g == 2:
                        o = take(dve, l, "gab")
                        order(cp(gb[:, 0:2, :], o[:, 0, 0:16].rearrange("p (t n) -> p t n", t=2)))
                        order(cp(gb[0:NS, 2, :], o[0:NS, 0, 16:24]))
                        release(dve, "gab")
                        tell("ab_in")
                        order(tt(abt[:, 0], gb[:, :, 0:4], dtb[:, l, :].unsqueeze(1).broadcast_to([P, 3, H]), ALU.add))
                        order(ts_(abt[:, 1], abt[:, 0], -1.0, None, ALU.mult))
                        order(tt(abt[:, 1], abt[:, 0], abt[:, 1], ALU.min))
                        tell("ab_neg")

                stream(l, "mq", copy_tile(l, lambda g, t: mqt[:, 2 * g + t, :]), after=keys_and_decays)
                tell("mqt")
                dve.wait_ge(mk_stored, 16 * (l + 1))
                for s in range(2):
                    o = flat(f"ms{s}").rearrange("p (q m) -> p q m", m=NM)
                    order(dve.tensor_reduce(mx[:, 4 * s:4 * s + 4], o, AX.X, ALU.max))
                    order(ts_(mx[:, 4 * s:4 * s + 4], mx[:, 4 * s:4 * s + 4], -DV ** -0.5, None, ALU.mult))
                    tell(f"mmx{s}")

                def attend(g):
                    if g == 0:
                        for s in range(2):
                            ready(f"mpe{s}")
                            order(dve.reciprocal(msum[:, 4 * s:4 * s + 4], msum[:, 4 * s:4 * s + 4]))
                            order(tt(prob[:, 4 * s:4 * s + 4, :], prob[:, 4 * s:4 * s + 4, :],
                                     msum[:, 4 * s:4 * s + 4].unsqueeze(2).broadcast_to([P, 4, NM]), ALU.mult))
                            tell(f"mpr{s}")
                    elif g == 1:
                        for s in range(2):
                            order(cp(pt[:, 2 * s:2 * s + 2].rearrange("p h m t -> p (h m t)"), flat(f"mpt{s}")))
                            release(dve, f"mpt{s}")
                            tell(f"mpT{s}")
                    elif g == 2:
                        for s in range(2):
                            o = flat(f"mo{s}").rearrange("p (j t) -> p j t", j=4)
                            parts(oh[:, 4 * s:4 * s + 4, 0:SEQ], ol[:, 4 * s:4 * s + 4, 0:SEQ], o)
                            release(dve, f"mo{s}")
                    else:
                        ready("ab_exp")
                        order(stt(abt[:, 0], abt[:, 0], 0.0, abt[:, 2], ALU.max, ALU.add))
                        order(stt(gb[:, :, 0:4], abt[:, 0], -1.0, abt[:, 3, 0:1].broadcast_to([P, 3, H]), ALU.mult, ALU.mult))
                        tell("gb_done")
                        order(cp(qs[:], flat("mqs")[0:NS, :]))
                        release(dve, "mqs")
                        tell("mqs")
                stream(l, "rqk", copy_tile(l, lambda g, t: rot[:, 2 * g + t, :]), after=attend)
                tell("rraw")

                def score(b):
                    o = flat(f"qb{b}")
                    for m in range(2):
                        slot = unit_wait(dve, l, 2 * b + m)
                        for h in range(H):
                            order.apart(dve.tensor_tensor_reduce(junk[:, 4 * m + h, :], sring[:, slot, h * DV:(h + 1) * DV], o[:, h * DV:(h + 1) * DV],
                                                           1.0, 0.0, ALU.mult, ALU.add, sall[:, m, 4 * b + h:4 * b + h + 1]))
                        order.wait()
                        dve.sem_inc(unit_used[slot], 1)
                    release(dve, f"qb{b}")

                def score_two(g):
                    score(2 * g)
                    score(2 * g + 1)
                stream(l, "rv", copy_tile(l, lambda g, t: rvt[:, 2 * g + t, :]), after=score_two)
                tell("rvt")
                tell("sall")
                o = take(dve, l, "smt")[0:32, 0, 0:NM]
                order(dve.tensor_reduce(smx[:, 0:1], o, AX.X, ALU.max))
                order(ts_(smx[:, 0:1], smx[:, 0:1], -DV ** -0.5, None, ALU.mult))
                tell("smx")
                ready("spe")
                order(dve.reciprocal(smx[:, 1:2], smx[:, 1:2]))
                order(ts_(ps[:], ps[:], smx[:, 1:2], None, ALU.mult))
                tell("spr")
                order(dve.memset(pmask[:], 0.0))
                w = 4 * NS
                for m in range(2):
                    blocks = pmask[:, m * NS * w:m * NS * w + NS * (w + 4)].rearrange("p (b x) -> p b x", x=w + 4)[:, :, 0:4]
                    order(cp(blocks, take(dve, l, "spt")[:, 0, m * w:(m + 1) * w].rearrange("p (b h) -> p b h", h=4)))
                release(dve, "spt")
                tell("sptd")
                order(cp(sov[:], flat("smo")[0:4 * NS, :]))
                release(dve, "smo")
                dve.sem_inc(unit_used[(4 * NS - 1) % SRING], 1)
                tell("sov")
                w = 2 * 4 * NS + 1
                o = flat("smw")[:, 0:H * w].rearrange("p (h x) -> p h x", x=w)[:, :, 0:w - 1]
                order(cp(pts[:].rearrange("p (h d) b -> p h d b", h=H), o.rearrange("p h (d b f) -> p h d b f", d=2, f=4)[:, :, :, :, 0]))
                release(dve, "smw")
                parts(oh[:, :, SEQ:T], ol[:, :, SEQ:T], pts[:])
                tell("o_mem")

                def decayed(s):
                    o = take(dve, l, f"rs{s}")
                    order(tt(pr[:, 2 * s:2 * s + 2, 0:256], o[:, :, 0:256], dec_tab[:, 2 * s:2 * s + 2, :], ALU.mult))
                    order(tt(pr[:, 2 * s:2 * s + 2, 256:384], o[:, :, 256:384], dec_tab[:, 2 * s:2 * s + 2, 0:P], ALU.mult))
                    release(dve, f"rs{s}")
                    tell(f"rp{s}")

                def retention(g):
                    if g < 4:
                        o = take(dve, l, f"rw{g}")[:, :, 0:T]
                        c = 0 if g < 2 else 2
                        r = rot[:, 2 * g:2 * g + 2, :]
                        order(tt(r, r, rot_tab[:, c:c + 1, :].broadcast_to([P, 2, T]), ALU.mult))
                        order(tt(sqt[:], o, rot_tab[:, c + 1:c + 2, :].broadcast_to([P, 2, T]), ALU.mult))
                        release(dve, f"rw{g}")
                        order(tt(r, r, sqt[:], ALU.add))
                        if g == 3:
                            tell("rot")
                    elif g == 4:
                        order(tt(kn[:], flat("rkn").rearrange("p (n d) -> p n d", d=P),
                                 kdec_tab[:].unsqueeze(2).broadcast_to([P, 8, P]), ALU.mult))
                        release(dve, "rkn")
                        tell("rkd")
                        order(cp(vn[:, 0, :], flat("rvn0")))
                        release(dve, "rvn0")
                    elif g == 5:
                        order(cp(vn[:, 1, :], flat("rvn1")))
                        release(dve, "rvn1")
                        tell("rvn")
                        decayed(0)
                    elif g == 6:
                        decayed(1)
                        order(cp(ks_ret[:], flat("rks")[0:NS, 0:512]))
                        release(dve, "rks")
                        mask_queries(qmask, rot[:, 0:4, SEQ:T])
                    else:
                        for s in range(2):
                            order(cp(rout[:, 4 * s:4 * s + 4, 0:SEQ], flat(f"ro{s}").rearrange("p (j t) -> p j t", j=4)))
                            release(dve, f"ro{s}")
                        order(cp(stg[:], flat("rst")))
                        release(dve, "rst")
                        tell("rS_out")
                        dve.wait_ge(mv_stored, 16 * (l + 1))
                        order(cp(vs, flat("rvs")[0:NS, :]))
                        release(dve, "rvs")
                        tell("rvsd")
                stream(l, "x2", merge_tile(l, True), after=retention)

                def one_row(b, masked, keys):
                    order(ts_(masked[:, b % 2, :], keys[:], ident[0:NS, b:b + 1], None, ALU.mult))
                    dve.sem_inc(state_kd, 1)

                def update(name, slot, decay):
                    o = flat(name)
                    for h in range(H):
                        r = sring[:, slot, h * DV:(h + 1) * DV]
                        order.apart(stt(r, r, decay(h), o[:, h * DV:(h + 1) * DV], ALU.mult, ALU.add))
                    order.wait()
                    release(dve, name)
                    dve.sem_inc(state_new, 1)

                def conv_tile(ph, i, u):
                    for t in range(2):
                        j = 2 * (4 * i + u) + t
                        dve.wait_ge(conv_ready, l * 16 + j + 1)
                        r = qkvt[:, j, 0:SEQ]
                        order(ts_(r, full[:, t, 0:SEQ], cwl[:, j, 0:1], None, ALU.mult))
                        for k in range(1, CW):
                            order(stt(r, full[:, t, k:k + SEQ], cwl[:, j, k:k + 1], r, ALU.mult, ALU.add))
                        order(cp(tail[:, j, 0:3], full[:, t, SEQ:SEQ + 3]))
                        dve.sem_inc(conv_used[t], 1)

                def update_states(g):
                    if g + 1 < NS:
                        one_row(g + 1, kdb_ret, ks_ret)
                    unit_wait(dve, l, 4 * NS + g)
                    update(f"rS{g}", (4 * NS + g) % SRING, lambda h: float(np.exp(np.log1p(-2.0 ** (-5 - h)))))

                one_row(0, kdb_ret, ks_ret)
                stream(l, "gq", conv_tile, after=update_states)
                tell("conv_p")
                o = take(dve, l, "rqs")
                read_rows([o[:, 0], o[:, 1]], qout_ret, 5 * NS - 1)
                release(dve, "rqs")
                tell("rqv")
                order(cp(rout[:, :, SEQ:T], flat("rqt")[:, 0:KT * NS].rearrange("p (j b) -> p j b", b=NS)))
                release(dve, "rqt")
                tell("rof")
                ready("rlr")
                v4 = "p (h d) t -> p h d t"
                order(tt(rout[:].rearrange(v4, d=2), rout[:].rearrange(v4, d=2), r4[:].unsqueeze(2).broadcast_to([P, H, 2, T]), ALU.mult))
                stream(l, "rg", gated_tile(l, rout))
                tell("o_ret")
                order(cp(sc[:, :, :, 0:3], flat("gcs")[:, 0:384].rearrange("p (j b k) -> p j b k", b=NS, k=3)))
                release(dve, "gcs")
                for k in range(CW):
                    w = cwl[:, :, k:k + 1].broadcast_to([P, 16, NS])
                    if k == 0:
                        order(tt(qkvt[:, :, SEQ:T], sc[:, :, :, 0], w, ALU.mult))
                    else:
                        order(tt(csum[:], sc[:, :, :, k], w, ALU.mult))
                        order(tt(qkvt[:, :, SEQ:T], qkvt[:, :, SEQ:T], csum[:], ALU.add))
                tell("conv_s")
                order(cp(tail[:, :, 3:].rearrange("p j (b k) -> p j b k", k=3), sc[:, :, :, 1:4]))
                tell("tail")

                def prepare_delta(g):
                    if g == 0:
                        order(cp(bc[:], flat("gcol")[:, 0:16]))
                        release(dve, "gcol")
                        order(tt(ex[:, 0:8], bc[:, 8:16], bc[:, 0:8], ALU.subtract))
                        order(cp(ex[:, 8:24], bc[:]))
                        tell("bcd")
                    elif g == 1:
                        for z in range(2):
                            order(cp(cso[:, z * 1024:(z + 1) * 1024], flat(f"gct{z}")[0:27, :]))
                            release(dve, f"gct{z}")
                        tell("cso")
                    elif g == 2:
                        ready("gexp")
                        order(ts_(ex[:, 8:16], ex[:, 8:16], -1.0, None, ALU.mult))
                        ready("geb")
                    elif g == 4:
                        ready("gqr")
                        order(stt(qkvt[:, 0:4, :], qkvt[:, 0:4, :], DK ** -0.5, sqg[:, 0:4, :], ALU.mult, ALU.mult))
                        order(tt(qkvt[:, 4:8, :], qkvt[:, 4:8, :], sqg[:, 4:8, :], ALU.mult))
                        tell("gqk")
                    elif g in (5, 6):
                        if g == 5:
                            dve.wait_ge(conv_stored, 32 * (l + 1))
                        order(cp(vn[:, g - 5, :], flat(f"gvn{g - 5}")))
                        release(dve, f"gvn{g - 5}")
                    elif g == 7:
                        order(cp(kn[:].rearrange("p n d -> p (n d)"), flat("gkn")))
                        release(dve, "gkn")
                stream(l, "x0", merge_tile(l, False), after=prepare_delta)

                def masked(s, k):
                    order(tt(c_t[s][:], a_t[s][:], masks[:, k:k + 1, :].broadcast_to([P, 4, P]), ALU.mult))

                for s in range(2):
                    o = take(dve, l, f"gbr{s}")
                    for q in range(4):
                        col = (q % 2) * 4 + 2 * s + q // 2
                        order.apart(ts_(y_m[s][:, q, :], o[:, 0, q * P:(q + 1) * P], bc[:, col:col + 1], 0.0, ALU.subtract, ALU.min))
                    order(cp(a_t[s][:].rearrange("p q m -> p (q m)"), o[:, 1, :]))
                    tell(f"dm{s}")
                    ready(f"dme{s}")
                    order(tt(y_m[s][:], y_m[s][:], tri[:].unsqueeze(1).broadcast_to([P, 4, P]), ALU.mult))
                    o = take(dve, l, f"gG{s}")[:, 0, :].rearrange("p (q m) -> p q m", q=4)
                    order(tt(a_t[s][:], a_t[s][:], o, ALU.mult))
                    release(dve, f"gG{s}")
                    order(tt(a_t[s][:], a_t[s][:], y_m[s][:], ALU.mult))
                    o = take(dve, l, f"gQ{s}")[:, 0, :].rearrange("p (q m) -> p q m", q=4)
                    order(tt(a_q[s][:], y_m[s][:], o, ALU.mult))
                    release(dve, f"gQ{s}")
                    masked(s, 0)
                    order(stt(t_t[s][:], c_t[s][:], -1.0, ident[:].unsqueeze(1).broadcast_to([P, 4, P]), ALU.mult, ALU.add))
                    tell(f"g_at{s}")
                for s in range(2):
                    order(cp(t_m[s][:].rearrange("p q m -> p (q m)"), take(dve, l, f"gT{s}")[:, 0, :]))
                    release(dve, f"gT{s}")
                    masked(s, 1)
                    dve.sem_inc(inv_t, 1)
                for lv in range(6):
                    for s in range(2):
                        if lv < 5:
                            dve.wait_ge(inv_y, l * 12 + 2 * lv + s + 1)
                            masked(s, lv + 2)
                        o = take(dve, l, f"gt{lv}{s}")
                        if lv < 5:
                            order(tt(t_m[s][:].rearrange("p q m -> p (q m)"), t_m[s][:].rearrange("p q m -> p (q m)"), o[:, 0, :], ALU.subtract))
                        order(tt(t_t[s][:].rearrange("p q m -> p (q m)"), t_t[s][:].rearrange("p q m -> p (q m)"), o[:, 1, :], ALU.subtract))
                        release(dve, f"gt{lv}{s}")
                        if lv < 5:
                            dve.sem_inc(inv_t, 1)
                for h in range(H):
                    order.apart(ts_(vb[:, h * DV:(h + 1) * DV], vn[:, 0, h * DV:(h + 1) * DV], gb[:, 0, 4 + h:5 + h], None, ALU.mult))
                order.wait()
                tell("gvb")
                for c in range(2):
                    order(tt(kd[:, c], kn[:].rearrange("p (h c) d -> p h c d", c=2)[:, :, c, :],
                             ex[:, c * 4:c * 4 + 4].unsqueeze(2).broadcast_to([P, H, P]), ALU.mult))
                order(cp(vnew[:], flat("gv0")))
                release(dve, "gv0")
                tell("gvn0d")
                dve.wait_ge(ret_stored, 16 * (l + 1))
                order(cp(stg[:], flat("gS0")))
                release(dve, "gS0")
                tell("gsg")
                order(cp(qkvt[:, 8:16, 0:P], flat("go0").rearrange("p (j t) -> p j t", j=KT)))
                release(dve, "go0")
                order(tt(qkvt[:, 0:4, P:SEQ], qkvt[:, 0:4, P:SEQ], erow[:], ALU.mult))
                tell("gqd")
                o = flat("gks")
                for h in range(H):
                    r = vb[:, h * DV:(h + 1) * DV]
                    order.apart(stt(r, o[:, h * DV:(h + 1) * DV], ex[:, 12 + h:13 + h], vn[:, 1, h * DV:(h + 1) * DV], ALU.mult, ALU.add))
                order.wait()
                for h in range(H):
                    r = vb[:, h * DV:(h + 1) * DV]
                    order.apart(ts_(r, r, gb[:, 1, 4 + h:5 + h], None, ALU.mult))
                order.wait()
                release(dve, "gks")
                tell("gvb1")
                order(cp(vnew[:], flat("gv1")))
                release(dve, "gv1")
                tell("gvn1d")
                order(cp(qkvt[:, 8:16, P:SEQ], flat("go1").rearrange("p (j t) -> p j t", j=KT)))
                release(dve, "go1")
                o = flat("gS1")
                for h in range(H):
                    r = stg[:, h * DV:(h + 1) * DV]
                    order.apart(stt(r, r, ex[:, 20 + h:21 + h], o[:, h * DV:(h + 1) * DV], ALU.mult, ALU.add))
                order.wait()
                release(dve, "gS1")
                tell("gS_out")
                o = flat("gkS")
                for h in range(H):
                    order.apart(ts_(ks[:, h * P:(h + 1) * P], o[0:NS, h * P:(h + 1) * P], gb[0:NS, 2, 4 + h:5 + h], None, ALU.mult))
                order.wait()
                release(dve, "gkS")
                order(cp(vs, flat("gvS")[0:NS, :]))
                release(dve, "gvS")
                mask_queries(qmask_gdn, qkvt[:, 0:4, SEQ:T])
                order(stt(kneg[:], qkvt[:, 4:8, SEQ:T], -1.0, egb[:].rearrange("p (h b) -> p h b", b=NS), ALU.mult, ALU.mult))
                tell("gsmp")

                def new_values(b):
                    order(tt(vns, flat(f"gr{b}")[0:NS, :], vs, ALU.add))
                    release(dve, f"gr{b}")
                    one_row(b, kdb, ks)

                ov = qkvt[:, 8:16, :]

                def update_delta(b):
                    unit_wait(dve, l, 5 * NS + b)
                    update(f"gx{b}", (5 * NS + b) % SRING, lambda h: egb[:, h * NS + b:h * NS + b + 1])

                def finish_prompt(g):
                    if g < 3:
                        new_values(5 + g)
                    if g == 0:
                        ready("glr_prompt")
                        op = ov[:, :, 0:SEQ].rearrange(v4, d=2)
                        order(tt(op, op, r4[:, :, 0:SEQ].unsqueeze(2).broadcast_to([P, H, 2, SEQ]), ALU.mult))
                        dve.wait_ge(M["gates_in"], 2 * l + 1)
                    for t in range(2):
                        j = 2 * g + t
                        order(stt(tmpf[:, 0:SEQ], gzs[:, j, 0:SEQ], gnl[:, t:t + 1], ov[:, j, 0:SEQ], ALU.mult, ALU.mult))
                        parts(oh[:, j, 0:SEQ], ol[:, j, 0:SEQ], tmpf[:, 0:SEQ])

                new_values(0)
                stream(l, "gz", first=update_delta, after=lambda g: new_values(g + 1))
                stream(l, "g1", first=lambda g: update_delta(4 + g), after=finish_prompt)
                o = take(dve, l, "gqs")
                read_rows([o[:, 0], o[:, 1]], qout, 6 * NS - 1)
                release(dve, "gqs")
                tell("gqv")
                order(cp(ov[:, :, SEQ:T], flat("gqt")[:, 0:KT * NS].rearrange("p (j b) -> p j b", b=NS)))
                release(dve, "gqt")
                tell("gof")
                ready("glr")
                os = ov[:, :, SEQ:T].rearrange(v4, d=2)
                order(tt(os, os, r4[:, :, SEQ:T].unsqueeze(2).broadcast_to([P, H, 2, NS]), ALU.mult))
                four = "p (h d) b -> p h d b"
                for d in range(2):
                    order(stt(pts[:].rearrange(four, d=2)[:, :, d, :], gzs[:, :, SEQ:T].rearrange(four, d=2)[:, :, d, :],
                              gnl[:, d:d + 1], ov[:, :, SEQ:T].rearrange(four, d=2)[:, :, d, :], ALU.mult, ALU.mult))
                parts(oh[:, :, SEQ:T], ol[:, :, SEQ:T], pts[:])
                tell("o_gdn")
                dve.wait_ge(M["gates_in"], 2 * l + 2)
                passed(dve)

                def merge_delta(ph, i, u):
                    for t in range(2):
                        j = 2 * (4 * i + u) + t
                        bank = tile_wait(dve, l, ph, i, u, t)
                        order(tt(tmpf[:], proj[bank][:, 0:T], g1s[:, j, :], ALU.mult))
                        dve.sem_inc(bank_free[bank], 1)
                        order(tt(y[:, j, :], y[:, j, :], tmpf[:], ALU.add))
                        parts(mh[:, j, :], ml[:, j, :], y[:, j, :])
                stream(l, "b1", merge_delta)
                tell("merged")
                order(dve.memset(acc[:], 0.0))
                stream(l, "out", result_tile(l, 3, "sqp2"))
                add_result(2, "x3")
                sum_x(3)
                norm_x(3, 4)
                split_memory(l + 2)
                stream(l, "f2i", hidden_tile(l, False))
                order(dve.memset(acc[:], 0.0))
                stream(l, "f2o", result_tile(l, 5, "sqp3"))
                add_result(3, "x1")
                dve.wait_ge(mv_stored, 16 * (l + 1))
                dve.wait_ge(gdn_stored, 16 * (l + 1))
                passed(dve)
            for t in range(3):
                n = P if t < 2 else NS
                dve.wait_ge(pro_pe, 20 + t)
                order(cp(yout[0:n, t, :], aux[t % 2][0:n].rearrange("p a b -> p (a b)")))
                dve.sem_inc(pro_dve, 1)


def launch_arrays(inputs):
    i = np.arange(P)
    ident = np.eye(P, dtype=np.float32)
    swap = ident[(i + 64) % P]
    tri = (i[:, None] <= i[None, :]).astype(np.float32)
    masks = np.zeros((P, 7, P), np.float32)
    for k in range(7):
        size = 2 << k
        same = i[:, None] // size == i[None, :] // size
        masks[:, k] = same & (i[:, None] % size < size // 2) & (i[None, :] % size >= size // 2)
    f32 = np.float32
    inv = (f32(10000.0) ** (-np.arange(64, dtype=f32) / f32(64))).astype(f32)
    pos = np.concatenate([np.arange(SEQ), np.full(NS, PAST)]).astype(f32)
    ang = (inv[:, None] * pos[None, :]).astype(f32).astype(np.float64)
    cos, sin = np.cos(ang), np.sin(ang)
    cc, ss = np.concatenate([cos, cos]), np.concatenate([-sin, sin])
    scale = DK ** -0.5
    rot = np.stack([cc, ss, cc * scale, ss * scale], 1).astype(f32)
    lg = np.log1p(-np.exp2(-5.0 - np.arange(H)))
    d = np.arange(SEQ)[None, :] - i[:, None]
    dec = np.where(d[:, None, :] >= 0, np.exp(np.maximum(d, 0)[:, None, :] * lg[None, :, None]), 0.0).astype(f32)
    tok = i[:, None, None] + P * np.arange(2)[None, None, :]
    kdec = np.exp((SEQ - 1 - tok) * lg[None, :, None]).reshape(P, 8).astype(f32)
    return {"t_ident": ident, "t_swap": swap, "t_tri": tri, "t_masks": masks, "t_rot": rot, "t_dec": dec, "t_kdec": kdec}


NORMS = ["norm_ffn1_pre", "norm_ffn1_post", "norm_mix_pre", "norm_mix_post", "norm_ffn2_pre", "norm_ffn2_post", "norm_mem"]
OUTS = [(1, SEQ, D), (NS, 1, D), (L, 1, H, DK, DV), (L, 1, H, DK, DV), (L, 1, 3, 16 * P),
        (L, 1, NM, H, DV), (L, 1, NM, H, DV), (L, NS, H, DK, DV), (L, NS, H, DK, DV), (L, NS, 3, 16 * P)]


def program(nc, aps):
    a = aps
    outs = [nc.dram_tensor(f"out_{k}", s, F32, kind="ExternalOutput").ap() for k, s in enumerate(OUTS)]
    build(nc, a["x_prompt"], a["x_sample"], a["mem_prompt"], a["state_ret"], a["state_gdn"], a["state_conv"],
          a["cache_mem_k"], a["cache_mem_v"], [a[n] for n in NORMS], a["w_mem_k"], a["w_mem_v"], a["w_in"],
          a["gdn_conv_w"], a["gdn_a_log"], a["gdn_dt_bias"], a["gdn_norm"],
          [a["w_branch_ret"], a["w_branch_gdn"], a["w_branch_mem"]], a["w_out"],
          [a["ffn1_w_in"], a["ffn2_w_in"]], [a["ffn1_w_out"], a["ffn2_w_out"]],
          [a[n] for n in ("t_ident", "t_swap", "t_tri", "t_masks", "t_rot", "t_dec", "t_kdec")], outs)


def kernel(**inputs):
    import concourse.bacc as bacc
    from concourse.bass_utils import run_bass_kernel_spmd

    nc = bacc.Bacc("TRN2", target_bir_lowering=False, num_devices=1)
    arrays, aps = {}, {}
    for name, a in list(inputs.items()) + list(launch_arrays(inputs).items()):
        arrays[name] = np.ascontiguousarray(a)
        aps[name] = nc.dram_tensor(name, arrays[name].shape, F32, kind="ExternalInput").ap()
    program(nc, aps)
    r = run_bass_kernel_spmd(nc, [arrays], core_ids=[0])
    return tuple(r.results[0][f"out_{k}"] for k in range(len(OUTS)))
```
